# Optimizing a Trainium2 kernel written in Bass

```python
import jax, jax.numpy as jnp
from jax import lax
import numpy as np

D_MODEL = 1024
BATCH = 1
SEQ = 512
DEPTH = 2

HEAD_DIM = 64
PLE_DIM = 256
GRID_W = 64
ROPE_THETA = 10000.0
RMS_EPS = 1e-6
D_FF = 2816
A_HEADS = 12
A_KV_HEADS = 4
A_GROUP = A_HEADS // A_KV_HEADS
A_RADIUS = 128
B_PAIRS = ((128, 1), (512, 4), (2048, 16))
B_SLOTS = 4
B_HEADS = B_SLOTS * len(B_PAIRS)
C_HEADS = D_MODEL // HEAD_DIM
NA_KH = 8
NA_KW = 16

A_Q = A_HEADS * HEAD_DIM
A_KV = A_KV_HEADS * HEAD_DIM
B_W = B_HEADS * HEAD_DIM
AB_IN = A_Q + 2 * A_KV + 3 * B_W
AB_OUT = A_Q + B_SLOTS * HEAD_DIM
C_IN = 3 * C_HEADS * HEAD_DIM
C_OUT = C_HEADS * HEAD_DIM
N_EVEN = (DEPTH + 1) // 2
N_ODD = DEPTH // 2
NEG_INF = -1e30


def rmsnorm(x, g):
    xf = x.astype(jnp.float32)
    y = xf * lax.rsqrt(jnp.mean(xf * xf, axis=-1, keepdims=True) + RMS_EPS)
    return (y * g.astype(jnp.float32)).astype(x.dtype)

def swiglu(x, w_gate, w_up, w_down):
    return (jax.nn.silu(x @ w_gate) * (x @ w_up)) @ w_down

def rope(x, pos):
    half = x.shape[-1] // 2
    inv = ROPE_THETA ** (-jnp.arange(half, dtype=jnp.float32) / half)
    ang = pos.astype(jnp.float32)[:, None] * inv[None, :]
    cos = jnp.cos(ang)[None, :, None, :]
    sin = jnp.sin(ang)[None, :, None, :]
    xf = x.astype(jnp.float32)
    x1, x2 = xf[..., :half], xf[..., half:]
    return jnp.concatenate([x1 * cos - x2 * sin, x2 * cos + x1 * sin], axis=-1).astype(x.dtype)

def banded_attention(q, k, v, radius, sink=None):
    n, L, hk, g, dh = q.shape
    bs = radius
    nb = -(-L // bs)
    lp = nb * bs
    q = jnp.pad(q, ((0, 0), (0, lp - L), (0, 0), (0, 0), (0, 0)))
    kv_pad = ((0, 0), (bs, lp - L + bs), (0, 0), (0, 0))
    k = jnp.pad(k, kv_pad).reshape(n, nb + 2, bs, hk, dh)
    v = jnp.pad(v, kv_pad).reshape(n, nb + 2, bs, hk, dh)
    kw = jnp.concatenate([k[:, :-2], k[:, 1:-1], k[:, 2:]], axis=2)
    vw = jnp.concatenate([v[:, :-2], v[:, 1:-1], v[:, 2:]], axis=2)
    qb = q.reshape(n, nb, bs, hk, g, dh)
    qpos = jnp.arange(lp).reshape(nb, bs)
    kpos = (jnp.arange(nb)[:, None] - 1) * bs + jnp.arange(3 * bs)[None, :]
    mask = (jnp.abs(qpos[:, :, None] - kpos[:, None, :]) <= radius) & ((kpos >= 0) & (kpos < L))[:, None, :]
    s = jnp.einsum('nbqhgd,nbkhd->nbhgqk', qb, kw).astype(jnp.float32) * (dh ** -0.5)
    s = jnp.where(mask[None, :, None, None], s, NEG_INF)
    m = jnp.max(s, axis=-1)
    if sink is not None:
        m = jnp.maximum(m, sink[:, :, None])
    e = jnp.exp(s - m[..., None])
    den = jnp.sum(e, axis=-1)
    if sink is not None:
        den = den + jnp.exp(sink[:, :, None] - m)
    pr = (e / den[..., None]).astype(v.dtype)
    o = jnp.einsum('nbhgqk,nbkhd->nbqhgd', pr, vw).reshape(n, lp, hk, g, dh)[:, :L]
    lse = (m + jnp.log(den)).transpose(0, 1, 4, 2, 3).reshape(n, lp, hk, g)[:, :L]
    return o, lse

def dilated_attention(q, k, v):
    bsz, s, _, dh = q.shape
    outs, lses = [], []
    for gi, (window, dil) in enumerate(B_PAIRS):
        lo = gi * B_SLOTS
        sub = s // dil

        def to_res(t):
            t = t[:, :, lo:lo + B_SLOTS]
            return t.reshape(bsz, sub, dil, B_SLOTS, dh).transpose(0, 2, 1, 3, 4).reshape(bsz * dil, sub, B_SLOTS, dh)

        o, lse = banded_attention(to_res(q)[:, :, :, None], to_res(k), to_res(v), window // (2 * dil))
        outs.append(o[:, :, :, 0].reshape(bsz, dil, sub, B_SLOTS, dh).transpose(0, 2, 1, 3, 4).reshape(bsz, s, B_SLOTS, dh))
        lses.append(lse[..., 0].reshape(bsz, dil, sub, B_SLOTS).transpose(0, 2, 1, 3).reshape(bsz, s, B_SLOTS))
    wts = jax.nn.softmax(jnp.stack(lses, axis=0), axis=0)
    out = jnp.einsum('gbsh,gbshd->bshd', wts, jnp.stack(outs, axis=0).astype(jnp.float32))
    return out.astype(q.dtype)

def neighbourhood_attention(q, k, v, rpb):
    bsz, s, nh, dh = q.shape
    rows = s // GRID_W
    kh = min(NA_KH, rows)
    kw = NA_KW
    qg = q.reshape(bsz, rows, GRID_W, nh, dh)
    kg = k.reshape(bsz, rows, GRID_W, nh, dh)
    vg = v.reshape(bsz, rows, GRID_W, nh, dh)
    cols = jnp.arange(GRID_W)
    col_start = jnp.clip(cols - kw // 2, 0, GRID_W - kw)
    col_idx = col_start[:, None] + jnp.arange(kw)[None, :]
    dc = col_idx - cols[:, None] + (NA_KW - 1)
    scale = dh ** -0.5

    def row_fn(i):
        rs = jnp.clip(i - kh // 2, 0, rows - kh)
        k_win = lax.dynamic_slice_in_dim(kg, rs, kh, axis=1)[:, :, col_idx]
        v_win = lax.dynamic_slice_in_dim(vg, rs, kh, axis=1)[:, :, col_idx]
        q_row = lax.dynamic_index_in_dim(qg, i, axis=1, keepdims=False)
        sc = jnp.einsum('bjhd,bajkhd->bhjak', q_row, k_win).astype(jnp.float32) * scale
        dr = rs + jnp.arange(kh) - i + (NA_KH - 1)
        bias = rpb[:, dr][:, :, dc].transpose(0, 2, 1, 3).astype(jnp.float32)
        sc = (sc + bias[None]).reshape(bsz, nh, GRID_W, kh * kw)
        pr = jax.nn.softmax(sc, axis=-1).reshape(bsz, nh, GRID_W, kh, kw).astype(v.dtype)
        return jnp.einsum('bhjak,bajkhd->bjhd', pr, v_win)

    o = lax.map(row_fn, jnp.arange(rows))
    return o.transpose(1, 0, 2, 3, 4).reshape(bsz, s, nh, dh)

def ab_mixer(xn, w_in, sink, w_out, pos):
    bsz, s, _ = xn.shape
    splits = [A_Q, A_Q + A_KV, A_Q + 2 * A_KV, A_Q + 2 * A_KV + B_W, A_Q + 2 * A_KV + 2 * B_W]
    qa, ka, va, qb, kb, vb = jnp.split(xn @ w_in, splits, axis=-1)
    qa = rope(qa.reshape(bsz, s, A_HEADS, HEAD_DIM), pos).reshape(bsz, s, A_KV_HEADS, A_GROUP, HEAD_DIM)
    ka = rope(ka.reshape(bsz, s, A_KV_HEADS, HEAD_DIM), pos)
    va = va.reshape(bsz, s, A_KV_HEADS, HEAD_DIM)
    oa, _ = banded_attention(qa, ka, va, A_RADIUS, sink.astype(jnp.float32).reshape(A_KV_HEADS, A_GROUP))
    shp = (bsz, s, B_HEADS, HEAD_DIM)
    ob = dilated_attention(rope(qb.reshape(shp), pos), rope(kb.reshape(shp), pos), vb.reshape(shp))
    mixed = jnp.concatenate([oa.reshape(bsz, s, A_Q).astype(xn.dtype),
                             ob.reshape(bsz, s, B_SLOTS * HEAD_DIM).astype(xn.dtype)], axis=-1)
    return mixed @ w_out

def c_mixer(xn, w_in, rpb, w_out):
    bsz, s, _ = xn.shape
    q, k, v = jnp.split(xn @ w_in, 3, axis=-1)
    shp = (bsz, s, C_HEADS, HEAD_DIM)
    o = neighbourhood_attention(q.reshape(shp), k.reshape(shp), v.reshape(shp), rpb)
    return o.reshape(bsz, s, C_OUT) @ w_out

def first_inputs(seed: int = 0) -> dict:
    key = jax.random.key(seed)
    ks = jax.random.split(key, 21)
    d = D_MODEL

    def nrm(k, shape, scale):
        return scale * jax.random.normal(k, shape, jnp.float32)

    def gain(k, shape):
        return 1.0 + 0.05 * jax.random.normal(k, shape, jnp.float32)

    return {
        'x': nrm(ks[0], (BATCH, SEQ, d), 1.0),
        'p': nrm(ks[1], (DEPTH, BATCH, SEQ, PLE_DIM), 1.0),
        'norm_ffn1': gain(ks[2], (DEPTH, d)),
        'ffn1_w_gate': nrm(ks[3], (DEPTH, d, D_FF), d ** -0.5),
        'ffn1_w_up': nrm(ks[4], (DEPTH, d, D_FF), d ** -0.5),
        'ffn1_w_down': nrm(ks[5], (DEPTH, D_FF, d), D_FF ** -0.5),
        'norm_mix': gain(ks[6], (DEPTH, d)),
        'w_in_ab': nrm(ks[7], (N_EVEN, d, AB_IN), d ** -0.5),
        'sink_a': nrm(ks[8], (N_EVEN, A_HEADS), 0.5),
        'w_out_ab': nrm(ks[9], (N_EVEN, AB_OUT, d), AB_OUT ** -0.5),
        'w_in_c': nrm(ks[10], (N_ODD, d, C_IN), d ** -0.5),
        'rpb_c': nrm(ks[11], (N_ODD, C_HEADS, 2 * NA_KH - 1, 2 * NA_KW - 1), 0.5),
        'w_out_c': nrm(ks[12], (N_ODD, C_OUT, d), C_OUT ** -0.5),
        'norm_ffn2': gain(ks[13], (DEPTH, d)),
        'ffn2_w_gate': nrm(ks[14], (DEPTH, d, D_FF), d ** -0.5),
        'ffn2_w_up': nrm(ks[15], (DEPTH, d, D_FF), d ** -0.5),
        'ffn2_w_down': nrm(ks[16], (DEPTH, D_FF, d), D_FF ** -0.5),
        'norm_ple': gain(ks[17], (DEPTH, d)),
        'w_ple_gate': nrm(ks[18], (DEPTH, d, d), d ** -0.5),
        'w_ple_proj': nrm(ks[19], (DEPTH, PLE_DIM, d), PLE_DIM ** -0.5),
        'norm_final': gain(ks[20], (d,)),
    }

def first_block(x, p, norm_ffn1, ffn1_w_gate, ffn1_w_up, ffn1_w_down, norm_mix, w_in_ab, sink_a,
              w_out_ab, w_in_c, rpb_c, w_out_c, norm_ffn2, ffn2_w_gate, ffn2_w_up, ffn2_w_down,
              norm_ple, w_ple_gate, w_ple_proj, norm_final):
    s = x.shape[1]
    pos = jnp.arange(s, dtype=jnp.int32)
    h = x
    for i in range(DEPTH):
        h = h + 0.5 * swiglu(rmsnorm(h, norm_ffn1[i]), ffn1_w_gate[i], ffn1_w_up[i], ffn1_w_down[i])
        hn = rmsnorm(h, norm_mix[i])
        j = i // 2
        if i % 2 == 0:
            h = h + ab_mixer(hn, w_in_ab[j], sink_a[j], w_out_ab[j], pos)
        else:
            h = h + c_mixer(hn, w_in_c[j], rpb_c[j], w_out_c[j])
        h = h + 0.5 * swiglu(rmsnorm(h, norm_ffn2[i]), ffn2_w_gate[i], ffn2_w_up[i], ffn2_w_down[i])
        gate = jax.nn.sigmoid(rmsnorm(h, norm_ple[i]) @ w_ple_gate[i])
        h = h + gate * (p[i] @ w_ple_proj[i])
    return rmsnorm(h, norm_final)


DEPTH_2 = 1

NORM_EPS = 1e-6
RWKV_HEADS = 8
RWKV_HEAD = 64
RWKV_W = RWKV_HEADS * RWKV_HEAD
DECAY_LORA = 64
ICLR_LORA = 64
GATE_LORA = 128
VRES_LORA = 32
RWKV_LN_EPS = 64e-5
N_DIR = 2
RWKV_COLS = 3 * RWKV_W + N_DIR * DECAY_LORA + N_DIR * ICLR_LORA + GATE_LORA
POOL_WINDOWS = (2, 4, 8, 16)
POOL_GROUPS = len(POOL_WINDOWS)
POOL_GROUP_W = 128
POOL_W = POOL_GROUPS * POOL_GROUP_W
ATT_HEADS = 8
ATT_KV_HEADS = 2
ATT_GROUP = ATT_HEADS // ATT_KV_HEADS
ATT_HEAD = 64
ATT_W = ATT_HEADS * ATT_HEAD
ATT_COLS = (ATT_HEADS + 2 * ATT_KV_HEADS) * ATT_HEAD
ROPE_AXIS_DIM = ATT_HEAD // 2
Q_BLOCK = 128
N_BRANCH = 3
GATE_COLS = N_BRANCH * D_MODEL
N_PROJ = RWKV_COLS + POOL_W + ATT_COLS + GATE_COLS
N_EXPERTS = 16
EXPERT_FF = 1024
CAPACITY_FACTOR = 2


def rms_norm(x, g, eps=NORM_EPS):
    xf = x.astype(jnp.float32)
    y = xf * lax.rsqrt(jnp.mean(xf * xf, axis=-1, keepdims=True) + eps)
    return (y * g.astype(jnp.float32)).astype(x.dtype)

def centred_token_shift(p, mu_prev, mu_next):
    zero = jnp.zeros_like(p[:, :1])
    p_prev = jnp.concatenate([zero, p[:, :-1]], axis=1)
    p_next = jnp.concatenate([p[:, 1:], zero], axis=1)
    return p + mu_prev * (p_prev - p) + mu_next * (p_next - p)

def _heads(z):
    return z.reshape(z.shape[:-1] + (RWKV_HEADS, RWKV_HEAD))

def rwkv7_bidir(p, hn, vres, v_first, w0, w2, a0, a2, g2, k_k, k_a, r_k, ln_w, ln_b):
    B, S, _ = p.shape
    f32 = jnp.float32
    dt = p.dtype
    pf = p.astype(f32)
    offs = np.cumsum([RWKV_W, RWKV_W, RWKV_W, N_DIR * DECAY_LORA, N_DIR * ICLR_LORA]).tolist()
    r, k, v, wd, ad, gd = jnp.split(pf, offs, axis=-1)
    wd = wd.reshape(B, S, N_DIR, DECAY_LORA)
    ad = ad.reshape(B, S, N_DIR, ICLR_LORA)
    w_raw = w0.astype(f32) + jnp.einsum('bsel,elc->bsec', jnp.tanh(wd), w2.astype(f32))
    decay = jnp.exp(-jnp.exp(-jax.nn.softplus(-w_raw) - 0.5))
    a = jax.nn.sigmoid(a0.astype(f32) + jnp.einsum('bsel,elc->bsec', ad, a2.astype(f32)))
    g = jnp.einsum('bsl,lc->bsc', jax.nn.sigmoid(gd), g2.astype(f32))
    if v_first is None:
        v_first = v
    else:
        v0, v1, v2 = vres
        mix = jax.nn.sigmoid(v0.astype(f32) + jnp.einsum('bsd,dl,lc->bsc', hn.astype(f32), v1.astype(f32), v2.astype(f32)))
        v = v + (v_first - v) * mix
    kk = _heads(k * k_k.astype(f32))
    kk = kk / jnp.maximum(jnp.linalg.norm(kk, axis=-1, keepdims=True), 1e-12)
    k_dir = k[:, :, None, :] * (1.0 + (a - 1.0) * k_a.astype(f32))

    def both(z):
        return jnp.stack([z, jnp.flip(z, 1)], axis=2)

    def per_dir(z):
        return jnp.stack([z[:, :, 0], jnp.flip(z[:, :, 1], 1)], axis=2)

    def time_major(z):
        return _heads(z).transpose(1, 2, 0, 3, 4)

    inputs = (time_major(both(r)), time_major(per_dir(decay)), time_major(per_dir(k_dir)),
              time_major(both(v)), both(kk).transpose(1, 2, 0, 3, 4), time_major(per_dir(a)))

    def step(state, inp):
        r_t, w_t, k_t, v_t, kk_t, a_t = inp
        sa = jnp.einsum('dbhij,dbhj->dbhi', state, -kk_t)
        state = (state * w_t[..., None, :] + sa[..., :, None] * (kk_t * a_t)[..., None, :]
                 + v_t[..., :, None] * k_t[..., None, :])
        return state, jnp.einsum('dbhij,dbhj->dbhi', state, r_t)

    state0 = jnp.zeros((N_DIR, B, RWKV_HEADS, RWKV_HEAD, RWKV_HEAD), f32)
    _, ys = lax.scan(step, state0, inputs)
    y = (ys[:, 0] + jnp.flip(ys[:, 1], 0)).transpose(1, 0, 2, 3)
    mu = jnp.mean(y, axis=-1, keepdims=True)
    var = jnp.mean(jnp.square(y - mu), axis=-1, keepdims=True)
    yn = (y - mu) * lax.rsqrt(var + RWKV_LN_EPS) * _heads(ln_w.astype(f32)) + _heads(ln_b.astype(f32))
    bonus = jnp.sum(_heads(r) * _heads(k_dir.sum(axis=2)) * _heads(r_k.astype(f32)), axis=-1, keepdims=True) * _heads(v)
    out = (yn + bonus).reshape(B, S, RWKV_W) * g
    return out.astype(dt), v_first

def multiscale_pool(z, pool_w, pool_scale):
    B, S, _ = z.shape
    zg = z.astype(jnp.float32).reshape(B, S, POOL_GROUPS, POOL_GROUP_W)
    csum = jnp.concatenate([jnp.zeros((B, 1, POOL_GROUPS, POOL_GROUP_W), jnp.float32), jnp.cumsum(zg, axis=1)], axis=1)
    t = jnp.arange(S)
    outs = []
    for gi, w in enumerate(POOL_WINDOWS):
        lo = w // 2
        hi = w - lo - 1
        start = jnp.clip(t - lo, 0, S)
        end = jnp.clip(t + hi + 1, 0, S)
        cnt = (end - start).astype(jnp.float32)
        outs.append((csum[:, end, gi] - csum[:, start, gi]) / cnt[None, :, None] - zg[:, :, gi])
    pooled = jnp.stack(outs, axis=2)
    y = jnp.einsum('bsgc,gcd->bsgd', pooled, pool_w.astype(jnp.float32)).reshape(B, S, POOL_W)
    return (y * pool_scale.astype(jnp.float32)).astype(z.dtype)

def axial_rope(seq):
    rows = seq // GRID_W
    row = jnp.repeat(jnp.arange(rows, dtype=jnp.float32), GRID_W)
    col = jnp.tile(jnp.arange(GRID_W, dtype=jnp.float32), rows)
    freqs = ROPE_THETA ** (-jnp.arange(0, ROPE_AXIS_DIM, 2, dtype=jnp.float32) / ROPE_AXIS_DIM)
    ang = jnp.concatenate([row[:, None] * freqs, col[:, None] * freqs], axis=-1)
    return jnp.cos(ang), jnp.sin(ang)

def apply_rope(x, cos, sin):
    xp = x.reshape(x.shape[:-1] + (ATT_HEAD // 2, 2))
    x0, x1 = xp[..., 0], xp[..., 1]
    c = cos[None, :, None, :]
    s = sin[None, :, None, :]
    return jnp.stack([x0 * c - x1 * s, x0 * s + x1 * c], axis=-1).reshape(x.shape)

def gqa_axial(p_att, q_norm, k_norm):
    B, S, _ = p_att.shape
    dt = p_att.dtype
    q, k, v = jnp.split(p_att, [ATT_W, ATT_W + ATT_KV_HEADS * ATT_HEAD], axis=-1)
    q = rms_norm(q.reshape(B, S, ATT_HEADS, ATT_HEAD), q_norm).astype(jnp.float32)
    k = rms_norm(k.reshape(B, S, ATT_KV_HEADS, ATT_HEAD), k_norm).astype(jnp.float32)
    cos, sin = axial_rope(S)
    q = (apply_rope(q, cos, sin) * (ATT_HEAD ** -0.5)).astype(dt)
    k = apply_rope(k, cos, sin).astype(dt)
    v = v.reshape(B, S, ATT_KV_HEADS, ATT_HEAD)
    n_blocks = S // Q_BLOCK
    q_blocks = q.reshape(B, n_blocks, Q_BLOCK, ATT_KV_HEADS, ATT_GROUP, ATT_HEAD).transpose(1, 0, 3, 4, 2, 5)
    k_t = k.transpose(0, 2, 1, 3)
    v_t = v.transpose(0, 2, 1, 3)

    def block(qb):
        s = jnp.einsum('bkgqd,bksd->bkgqs', qb, k_t).astype(jnp.float32)
        pr = jax.nn.softmax(s, axis=-1).astype(dt)
        return jnp.einsum('bkgqs,bksd->bkgqd', pr, v_t)

    o = lax.map(block, q_blocks)
    return o.transpose(1, 0, 4, 2, 3, 5).reshape(B, S, ATT_W)

def expert_choice_ffn(h, router, w_gate, w_up, w_down):
    B, S, D = h.shape
    cap = CAPACITY_FACTOR * S // N_EXPERTS
    aff = jax.nn.softmax(jnp.einsum('bsd,de->bse', h, router).astype(jnp.float32), axis=-1)
    vals, idx = lax.top_k(aff.transpose(0, 2, 1), cap)
    xg = jax.vmap(lambda hb, ib: hb[ib])(h, idx)
    hid = jax.nn.silu(jnp.einsum('becd,edf->becf', xg, w_gate)) * jnp.einsum('becd,edf->becf', xg, w_up)
    y = jnp.einsum('becf,efd->becd', hid, w_down) * vals[..., None].astype(h.dtype)
    return jax.vmap(lambda ib, yb: jnp.zeros((S, D), yb.dtype).at[ib.reshape(-1)].add(yb.reshape(-1, D)))(idx, y)

def second_inputs(seed: int = 0) -> dict:
    key = jax.random.key(seed)
    ks = iter(jax.random.split(key, 40))

    def nrm(shape, scale):
        return jax.random.normal(next(ks), shape, jnp.float32) * scale

    def uni(shape, lo, hi):
        return jax.random.uniform(next(ks), shape, jnp.float32, lo, hi)

    L = DEPTH_2
    Lv = DEPTH_2 - 1
    return {
        'x': nrm((BATCH, SEQ, D_MODEL), 1.0),
        'norm_mix': 1.0 + nrm((L, D_MODEL), 0.05),
        'w_in': nrm((L, D_MODEL, N_PROJ), D_MODEL ** -0.5),
        'shift_prev': uni((L, RWKV_COLS), 0.0, 0.5),
        'shift_next': uni((L, RWKV_COLS), 0.0, 0.5),
        'rwkv_w0': uni((L, N_DIR, RWKV_W), -5.0, 1.0),
        'rwkv_w2': nrm((L, N_DIR, DECAY_LORA, RWKV_W), 0.5 * DECAY_LORA ** -0.5),
        'rwkv_a0': nrm((L, N_DIR, RWKV_W), 0.5),
        'rwkv_a2': nrm((L, N_DIR, ICLR_LORA, RWKV_W), ICLR_LORA ** -0.5),
        'rwkv_g2': nrm((L, GATE_LORA, RWKV_W), GATE_LORA ** -0.5),
        'rwkv_k_k': 0.85 + nrm((L, RWKV_W), 0.05),
        'rwkv_k_a': 1.0 + nrm((L, RWKV_W), 0.05),
        'rwkv_r_k': nrm((L, RWKV_W), 0.1),
        'rwkv_ln_w': 1.0 + nrm((L, RWKV_W), 0.05),
        'rwkv_ln_b': nrm((L, RWKV_W), 0.02),
        'vres_v0': 0.5 + nrm((Lv, RWKV_W), 0.3),
        'vres_w1': nrm((Lv, D_MODEL, VRES_LORA), D_MODEL ** -0.5),
        'vres_w2': nrm((Lv, VRES_LORA, RWKV_W), VRES_LORA ** -0.5),
        'pool_w': nrm((L, POOL_GROUPS, POOL_GROUP_W, POOL_GROUP_W), POOL_GROUP_W ** -0.5),
        'pool_scale': 1.0 + nrm((L, POOL_W), 0.1),
        'q_norm': 1.0 + nrm((L, ATT_HEAD), 0.05),
        'k_norm': 1.0 + nrm((L, ATT_HEAD), 0.05),
        'w_branch_rwkv': nrm((L, RWKV_W, D_MODEL), RWKV_W ** -0.5),
        'w_branch_pool': nrm((L, POOL_W, D_MODEL), POOL_W ** -0.5),
        'w_branch_attn': nrm((L, ATT_W, D_MODEL), ATT_W ** -0.5),
        'w_out': nrm((L, D_MODEL, D_MODEL), D_MODEL ** -0.5),
        'norm_ffn': 1.0 + nrm((L, D_MODEL), 0.05),
        'router': nrm((L, D_MODEL, N_EXPERTS), D_MODEL ** -0.5),
        'exp_gate': nrm((L, N_EXPERTS, D_MODEL, EXPERT_FF), D_MODEL ** -0.5),
        'exp_up': nrm((L, N_EXPERTS, D_MODEL, EXPERT_FF), D_MODEL ** -0.5),
        'exp_down': nrm((L, N_EXPERTS, EXPERT_FF, D_MODEL), EXPERT_FF ** -0.5),
        'norm_final': 1.0 + nrm((D_MODEL,), 0.05),
    }

def second_block(x, norm_mix, w_in, shift_prev, shift_next, rwkv_w0, rwkv_w2, rwkv_a0, rwkv_a2, rwkv_g2,
              rwkv_k_k, rwkv_k_a, rwkv_r_k, rwkv_ln_w, rwkv_ln_b, vres_v0, vres_w1, vres_w2,
              pool_w, pool_scale, q_norm, k_norm, w_branch_rwkv, w_branch_pool, w_branch_attn, w_out,
              norm_ffn, router, exp_gate, exp_up, exp_down, norm_final):
    B, S, D = x.shape
    split_at = [RWKV_COLS, RWKV_COLS + POOL_W, RWKV_COLS + POOL_W + ATT_COLS]
    v_first = None
    for l in range(DEPTH_2):
        hn = rms_norm(x, norm_mix[l])
        proj = jnp.einsum('bsd,dn->bsn', hn, w_in[l])
        p_rwkv, p_pool, p_att, p_gate = jnp.split(proj, split_at, axis=-1)
        p_rwkv = centred_token_shift(p_rwkv, shift_prev[l], shift_next[l])
        vres = None if l == 0 else (vres_v0[l - 1], vres_w1[l - 1], vres_w2[l - 1])
        y_a, v_first = rwkv7_bidir(p_rwkv, hn, vres, v_first, rwkv_w0[l], rwkv_w2[l], rwkv_a0[l], rwkv_a2[l],
                                   rwkv_g2[l], rwkv_k_k[l], rwkv_k_a[l], rwkv_r_k[l], rwkv_ln_w[l], rwkv_ln_b[l])
        y_b = multiscale_pool(p_pool, pool_w[l], pool_scale[l])
        y_c = gqa_axial(p_att, q_norm[l], k_norm[l])
        gates = jax.nn.sigmoid(p_gate).reshape(B, S, N_BRANCH, D)
        merged = (gates[:, :, 0] * (y_a @ w_branch_rwkv[l]) + gates[:, :, 1] * (y_b @ w_branch_pool[l])
                  + gates[:, :, 2] * (y_c @ w_branch_attn[l]))
        x = x + merged @ w_out[l]
        x = x + expert_choice_ffn(rms_norm(x, norm_ffn[l]), router[l], exp_gate[l], exp_up[l], exp_down[l])
    return rms_norm(x, norm_final)


def setup_inputs(seed=0):
    out = dict(first_inputs(seed))
    for name, value in second_inputs(seed + 1).items():
        if name != "x":
            out[name + "_2"] = value
    return out


def reference(
    x, p, norm_ffn1, ffn1_w_gate, ffn1_w_up, ffn1_w_down, norm_mix, w_in_ab, sink_a, w_out_ab,
    w_in_c, rpb_c, w_out_c, norm_ffn2, ffn2_w_gate, ffn2_w_up, ffn2_w_down, norm_ple,
    w_ple_gate, w_ple_proj, norm_final, norm_mix_2, w_in_2, shift_prev_2, shift_next_2,
    rwkv_w0_2, rwkv_w2_2, rwkv_a0_2, rwkv_a2_2, rwkv_g2_2, rwkv_k_k_2, rwkv_k_a_2, rwkv_r_k_2,
    rwkv_ln_w_2, rwkv_ln_b_2, vres_v0_2, vres_w1_2, vres_w2_2, pool_w_2, pool_scale_2, q_norm_2,
    k_norm_2, w_branch_rwkv_2, w_branch_pool_2, w_branch_attn_2, w_out_2, norm_ffn_2, router_2,
    exp_gate_2, exp_up_2, exp_down_2, norm_final_2,
):
    x = first_block(
        x, p, norm_ffn1, ffn1_w_gate, ffn1_w_up, ffn1_w_down, norm_mix, w_in_ab, sink_a,
        w_out_ab, w_in_c, rpb_c, w_out_c, norm_ffn2, ffn2_w_gate, ffn2_w_up, ffn2_w_down,
        norm_ple, w_ple_gate, w_ple_proj, norm_final,
    )
    return second_block(
        x, norm_mix_2, w_in_2, shift_prev_2, shift_next_2, rwkv_w0_2, rwkv_w2_2, rwkv_a0_2,
        rwkv_a2_2, rwkv_g2_2, rwkv_k_k_2, rwkv_k_a_2, rwkv_r_k_2, rwkv_ln_w_2, rwkv_ln_b_2,
        vres_v0_2, vres_w1_2, vres_w2_2, pool_w_2, pool_scale_2, q_norm_2, k_norm_2,
        w_branch_rwkv_2, w_branch_pool_2, w_branch_attn_2, w_out_2, norm_ffn_2, router_2,
        exp_gate_2, exp_up_2, exp_down_2, norm_final_2,
    )


_drawn_inputs = setup_inputs


def setup_inputs(seed=0):
    import zlib

    import numpy as np

    out = dict(_drawn_inputs(seed))
    spreads = {}
    factors = {'norm_mix': 2.787,
     'sink_a': 64.0,
     'norm_ple': 3.532,
     'rwkv_w2_2': 4.778,
     'rwkv_k_k_2': 14.415,
     'rwkv_k_a_2': 2.777,
     'rwkv_ln_w_2': 3.422,
     'rwkv_ln_b_2': 7.748,
     'q_norm_2': 8.0,
     'k_norm_2': 8.0,
     'norm_ffn_2': 3.205}
    for name, (base, spread) in spreads.items():
        noise = np.random.default_rng([zlib.crc32(name.encode()), seed]).standard_normal(out[name].shape)
        drawn = base * np.exp(spread * noise) if base else spread * noise
        out[name] = __import__('jax').numpy.asarray(drawn.astype(out[name].dtype))
    for name, factor in factors.items():
        out[name] = (out[name] * factor).astype(out[name].dtype)
    return out
```

```python
from contextlib import ExitStack

import numpy as np

import concourse.bass as bass
from concourse import mybir

F32 = mybir.dt.float32
ALU = mybir.AluOpType
ACT = mybir.ActivationFunctionType
AX_X = mybir.AxisListType.X

P = 128
S = 512
D = 1024
KT = 8
FF = 22
EPS = 1e-6
NEG = -1e30
NSLOT = 4
SLOT = 2048

A_TILES = [(0, 3), (1, 4), (2, 5), (6, 9), (7, 10), (8, 11)]
ATT_TILES = [(0, 4), (1, 5), (2, 6), (3, 7)]

VEC = {}
_at = 0
for _name, _n in [("norm_ffn1_0", 8), ("norm_ffn1_1", 8), ("norm_mix_0", 8), ("norm_mix_1", 8),
                  ("norm_ffn2_0", 8), ("norm_ffn2_1", 8), ("norm_ple_0", 8), ("norm_ple_1", 8),
                  ("norm_final", 8), ("norm_mix_2", 8), ("norm_ffn_2", 8), ("norm_final_2", 8),
                  ("shift_prev", 15), ("shift_next", 15), ("w0_0", 4), ("w0_1", 4), ("a0_0", 4), ("a0_1", 4),
                  ("k_k", 4), ("k_a", 4), ("r_k", 4), ("ln_w", 4), ("ln_b", 4), ("pool_scale", 4),
                  ("q_norm", 1), ("k_norm", 1)]:
    VEC[_name] = _at
    _at += _n
NVEC = _at


class Queue:

    def __init__(self, eng, sem, skip_own=False):
        self.eng, self.sem, self.skip_own = eng, sem, skip_own
        self.count, self.seen, self.last = 0, {}, None

    def wait(self, *tokens):
        need = {}
        stack = list(tokens)
        while stack:
            w = stack.pop()
            if isinstance(w, list):
                stack.extend(w)
            elif w is not None and not (self.skip_own and w[0] is self.sem):
                if w[1] > max(self.seen.get(id(w[0]), 0), need.get(id(w[0]), (None, 0))[1]):
                    need[id(w[0])] = w
        for key, (s, v) in need.items():
            self.eng.wait_ge(s, v)
            self.seen[key] = v

    def __call__(self, fn, *waits, mark=True):
        self.wait(*waits)
        self.last = fn(self.eng)
        return self.sealed() if mark else self.now()

    def sealed(self):
        self.last.then_inc(self.sem, 1)
        self.count += 1
        return self.now()

    def now(self):
        return (self.sem, self.count)


class Pool:

    def __init__(self, items):
        self.items = list(items)
        self.ready = [(i, []) for i in range(len(self.items))]

    def take(self):
        i, toks = self.ready.pop(0)
        return i, self.items[i], toks

    def put(self, i, *toks):
        self.ready.append((i, list(toks)))


class Net:
    def __init__(self, nc, ctx, ins):
        self.nc, self.ctx, self.ins = nc, ctx, ins
        sem = lambda n: ctx.enter_context(nc.semaphore(n))
        self.sem = sem
        self.pe = Queue(nc.tensor, sem("s_pe"), skip_own=True)
        self.act = Queue(nc.scalar, sem("s_act"))
        self.dve = Queue(nc.vector, sem("s_dve"))
        self.pool = Queue(nc.gpsimd, sem("s_pool"))
        self.sp = Queue(nc.sync, sem("s_sp"))
        self.nf = 52160
        self.arena = ctx.enter_context(nc.sbuf_tensor("arena", [P, self.nf], F32))
        self.top = 0
        self.banks = Pool([ctx.enter_context(nc.psum_tensor(f"bank{i}", [P, 512], F32)) for i in range(8)])
        self.wsem = [sem(f"s_w{i}") for i in range(NSLOT)]
        self.wcount = [0] * NSLOT
        self.nsem = 0
        ring = [self.buf(SLOT) for _ in range(NSLOT)]
        self.wslots = Pool(ring)

    def buf(self, n):
        a = self.arena[:, self.top:self.top + n]
        self.top += n
        assert self.top <= self.nf, self.top
        return a

    def load(self, pairs, *waits):
        s = self.sem(f"s_ld{self.nsem}")
        self.nsem += 1
        for dst, src in pairs:
            self.sp(lambda e, dst=dst, src=src: e.dma_start(dst, src).then_inc(s, 16), *waits, mark=False)
        return (s, 16 * len(pairs))

    def weights(self, src, n):
        i, ap, free = self.wslots.take()
        dst = ap[:, 0:n]
        if len(src.shape) == 3:
            dst = dst.rearrange("p (a b) -> p a b", a=src.shape[1])
        s = self.wsem[i]
        self.wcount[i] += 16
        self.sp(lambda e: e.dma_start(dst, src).then_inc(s, 16), free, mark=False)
        return ap[:, 0:n], (s, self.wcount[i]), i

    def barrier(self):
        toks = [q.now() for q in (self.pe, self.act, self.dve, self.pool)]
        for q in (self.pe, self.act, self.dve, self.pool):
            q.wait(toks)
        return toks

    def group(self, out, pairs, *waits):
        n = len(pairs)
        for j, pr in enumerate(pairs):
            lhsT, rhs = pr[0], pr[1]
            own = pr[2] if len(pr) > 2 else None
            tok = self.pe(lambda e, l=lhsT, r=rhs, j=j: e.matmul(out, l, r, start=(j == 0), stop=(j == n - 1)),
                          own, waits and list(waits), mark=(j == n - 1))
        return tok

    def transpose(self, out, src, *waits, mark=True):
        k = src.shape[0]
        return self.pe(lambda e: e.transpose(out, src, self.ident[0:k, 0:k]), *waits, mark=mark)


class Norm:

    def __init__(self, n):
        self.n, self.pend, self.k = n, [], 0
        self.b, self.bank, self.free = n.banks.take()

    def add(self, ap, tok):
        n = self.n
        i, sq, free = n.sq.take()
        t = n.act(lambda e: e.activation(sq, ap, ACT.Square), tok, free)
        self.pend.append((i, sq, t))

    def flush(self):
        n = self.n
        for i, sq, t in self.pend:
            k = self.k
            tok = n.pe(lambda e, k=k, sq=sq: e.matmul(self.bank[:, :], n.ones, sq, start=(k == 0), stop=(k == KT - 1)),
                       t, self.free)
            n.sq.put(i, tok)
            self.k += 1
            self.tok = tok
        self.pend = []

    def finish(self, gain, dst, *waits):
        n = self.n
        self.flush()
        assert self.k == KT
        r = n.rstd
        t = n.dve(lambda e: e.tensor_scalar(r, self.bank[:, :], 1.0 / D, EPS, ALU.mult, ALU.add), self.tok, n.rstd_free)
        n.banks.put(self.b, t)
        t = n.act(lambda e: e.activation(r, r, ACT.Sqrt), t)
        t = n.dve(lambda e: e.reciprocal(r, r), t)
        toks = []
        for k in range(KT):
            g = n.vec(gain, k)
            toks.append(n.dve(lambda e, k=k, g=g: e.scalar_tensor_tensor(out=dst[k], in0=n.h[k], scalar=g, in1=r,
                                                                       op0=ALU.mult, op1=ALU.mult), t, *waits))
        n.rstd_free = toks[-1]
        return toks


def make_net(nc, ctx, ins):
    n = Net(nc, ctx, ins)
    n.ident, n.ones, n.bones, n.rot1, n.rot2 = (n.buf(P) for _ in range(5))
    n.vecs = n.buf(NVEC)
    n.cc = n.buf(15 + 4 + 2)
    n.sq = Pool([n.buf(512) for _ in range(3)])
    n.rstd = n.buf(512)
    n.rstd_free = None
    n.xn = [n.buf(512) for _ in range(KT)]
    n.h_base = n.top
    n.h = [n.buf(512) for _ in range(KT)]
    n.vec = lambda name, k=0: n.vecs[:, VEC[name] + k:VEC[name] + k + 1]
    c = ins["consts"]
    n.t_const = n.load([(n.ident, c[0]), (n.ones, c[1]), (n.bones, c[2]), (n.rot1, c[3]), (n.rot2, c[4]),
                        (n.vecs, ins["vecs"])])
    for q in (n.pe, n.act, n.dve, n.pool):
        q.wait(n.t_const)
    return n


def ffn(n, w_gu, w_dn, norm, gain):
    mark = n.top
    hid = [n.buf(512) for _ in range(FF)]
    sgs = Pool([n.buf(512) for _ in range(2)])
    xt = norm.finish(gain, n.xn)
    ht = []
    for m in range(FF):
        w, wt, ws = n.weights(w_gu[m], 2048)
        w = w.rearrange("p (g k c) -> p g k c", g=2, k=KT)
        gb, g, gf = n.banks.take()
        ub, u, uf = n.banks.take()
        tg = n.group(g[:, :], [(w[:, 0, k, :], n.xn[k], xt[k]) for k in range(KT)], wt, gf)
        tu = n.group(u[:, :], [(w[:, 1, k, :], n.xn[k]) for k in range(KT)], uf)
        n.wslots.put(ws, tu)
        i, sg, sf = sgs.take()
        t = n.act(lambda e, sg=sg, g=g: e.activation(sg, g[:, :], ACT.Silu), tg, sf)
        n.banks.put(gb, t)
        t = n.dve(lambda e, m=m, sg=sg, u=u: e.tensor_tensor(hid[m], sg, u[:, :], ALU.mult), t, tu)
        n.banks.put(ub, t)
        sgs.put(i, t)
        ht.append(t)
    nxt = Norm(n)
    for m in range(KT):
        b, bank, bf = n.banks.take()
        pairs = []
        blocks = []
        for half in range(2):
            w, wt, ws = n.weights(w_dn[m, :, half * 1408:(half + 1) * 1408], 1408)
            w = w.rearrange("p (k c) -> p k c", k=11)
            blocks.append(ws)
            pairs += [(w[:, k, :], hid[half * 11 + k], [ht[half * 11 + k], wt]) for k in range(11)]
        tok = n.group(bank[:, :], pairs, bf)
        for ws in blocks:
            n.wslots.put(ws, tok)
        nxt.flush()
        t = n.dve(lambda e, m=m, bank=bank: e.scalar_tensor_tensor(out=n.h[m], in0=bank[:, :], scalar=0.5, in1=n.h[m],
                                                                 op0=ALU.mult, op1=ALU.add), tok)
        n.banks.put(b, t)
        nxt.add(n.h[m], t)
        n.ht[m] = t
    n.top = mark
    n.barrier()
    return nxt


def out_proj(n, wsrc, rhs, toks):
    nxt = Norm(n)
    for m2 in range(4):
        w, wt, ws = n.weights(wsrc[m2], 2048)
        w = w.rearrange("p (a k c) -> p a k c", a=2, k=KT)
        for a in range(2):
            m = 2 * m2 + a
            b, bank, bf = n.banks.take()
            tok = n.group(bank[:, :], [(w[:, a, k, :], rhs[k], toks[k]) for k in range(KT)], wt, bf)
            nxt.flush()
            t = n.dve(lambda e, m=m, bank=bank: e.tensor_tensor(n.h[m], bank[:, :], n.h[m], ALU.add), tok)
            n.banks.put(b, t)
            nxt.add(n.h[m], t)
            n.ht[m] = t
        n.wslots.put(ws, tok)
    return nxt


def rope(n, raw, rawt, rot, cos, sin, tmps, dst, *waits):
    b, bank, bf = n.banks.take()
    tr = n.group(bank[:, :], [(rot, raw)], rawt, bf)
    i, tmp, tf = tmps.take()
    t1 = n.pool(lambda e: e.tensor_tensor(dst, raw, cos, ALU.mult), rawt, *waits)
    t2 = n.dve(lambda e: e.tensor_tensor(tmp, bank[:, :], sin, ALU.mult), tr, tf, *waits)
    n.banks.put(b, t2)
    t = n.dve(lambda e: e.tensor_tensor(dst, dst, tmp, ALU.add), t1, t2)
    tmps.put(i, t)
    return t, [tr, t1]


def heads_fm(n, blocks, xt, use):
    m = 0
    for src, cnt in blocks:
        w, wt, ws = n.weights(src, cnt * 1024)
        w = w.rearrange("p (a k c) -> p a k c", a=cnt, k=KT)
        for a in range(cnt):
            b, bank, bf = n.banks.take()
            tok = n.group(bank[:, :], [(w[:, a, k, :], n.xn[k], xt[k]) for k in range(KT)], wt, bf)
            n.banks.put(b, use(m, bank, tok))
            m += 1
        n.wslots.put(ws, tok)


def values_tm(n, src, cols, xt, sel, dst):
    w, wt, ws = n.weights(src, KT * cols)
    w = w.rearrange("p (k c) -> p k c", k=KT)
    toks = []
    for i in range(4):
        b, bank, bf = n.banks.take()
        tok = n.group(bank[:, 0:cols], [(sel(k, i), w[:, k, :], xt[k]) for k in range(KT)], wt, bf)
        t = n.act(lambda e, i=i, bank=bank: e.activation(dst(i), bank[:, 0:cols], ACT.Copy), tok)
        n.banks.put(b, t)
        toks.append(t)
    n.wslots.put(ws, tok)
    return toks


class Attention:

    def __init__(self, n, width):
        self.n = n
        self.sc = Pool([n.buf(width) for _ in range(5)])
        self.pt = Pool([n.buf(width) for _ in range(2)])
        self.st = Pool([n.buf(8) for _ in range(6)])
        self.toks = []

    def run(self, units):
        steps = [self.scores, self.biased, self.exps, self.scaled, self.turned, self.copied, self.values, self.stored]
        units = [dict(u) for u in units]
        for t in range(len(units) + len(steps) - 1):
            for s in range(len(steps) - 1, -1, -1):
                if 0 <= t - s < len(units):
                    steps[s](units[t - s])

    def scores(self, u):
        n = self.n
        u["sb"] = []
        if "before" in u:
            u["before"]()
        for part in u["keys"]:
            b, bank, bf = n.banks.take()
            off = 0
            for kap in part:
                w = kap.shape[-1]
                tok = n.pe(lambda e, bank=bank, off=off, w=w, kap=kap: e.matmul(bank[:, off:off + w], u["q"], kap,
                                                                              start=True, stop=True),
                           bf, u["waits"])
                off += w
            u["sb"].append((b, bank, off, tok))

    def biased(self, u):
        n = self.n
        u["sci"], sc, scf = self.sc.take()
        u["sti"], st, stf = self.st.take()
        u["sc"], u["st"] = sc, st
        off = 0
        u["first"] = []
        for j, (b, bank, w, tok) in enumerate(u["sb"]):
            o = sc[:, off:off + w]
            m = st[:, j:j + 1]
            if u["mask"] is None:
                t = n.dve(lambda e: e.tensor_reduce(m, bank[:, 0:w], AX_X, ALU.max), tok, scf, stf)
                u["raw"] = (b, bank, t)
            else:
                init = u["sink"] if j == 0 and u["sink"] is not None else (st[:, j - 1:j] if j else -3e38)
                prev = u["first"][-1] if j else None
                t = n.dve(lambda e, o=o, bank=bank, w=w, m=m, j=j, init=init: e.tensor_tensor_reduce(
                    o, bank[:, 0:w], u["mask"][j], 1.0, init, ALU.add, ALU.max, m), tok, scf, stf, prev, u["waits"])
                n.banks.put(b, t)
            u["first"].append(t)
            off += w
        u["w"] = off
        j = len(u["sb"]) - 1
        u["t"] = n.dve(lambda e: e.tensor_scalar(st[:, 2:3], st[:, j:j + 1], -1.0, None, ALU.mult), u["first"])

    def exps(self, u):
        n = self.n
        sc, st, w = u["sc"], u["st"], u["w"]
        src = sc[:, 0:w] if u["mask"] is not None else u["raw"][1][:, 0:w]
        u["te"] = n.act(lambda e: e.activation(sc[:, 0:w], src, ACT.Exp, bias=st[:, 2:3], accum_out=st[:, 3:4]),
                        u["t"])
        if u["mask"] is None:
            n.banks.put(u["raw"][0], u["te"])
        if u["sink"] is not None:
            u["ts"] = n.act(lambda e: e.activation(st[:, 5:6], u["sink"], ACT.Exp, bias=st[:, 2:3]), u["t"])

    def scaled(self, u):
        n = self.n
        sc, st, w = u["sc"], u["st"], u["w"]
        t = u["te"]
        if u["sink"] is not None:
            t = n.dve(lambda e: e.tensor_tensor(st[:, 3:4], st[:, 3:4], st[:, 5:6], ALU.add), t, u["ts"])
        t = n.dve(lambda e: e.reciprocal(st[:, 4:5], st[:, 3:4]), t)
        u["tp"] = n.dve(lambda e: e.tensor_scalar(sc[:, 0:w], sc[:, 0:w], st[:, 4:5], None, ALU.mult), t)
        self.st.put(u["sti"], u["tp"])

    def turned(self, u):
        n = self.n
        sc = u["sc"]
        nb = u["w"] // P
        u["tb"] = []
        for g in range(0, nb, 4):
            b, bank, bf = n.banks.take()
            c = min(4, nb - g)
            for j in range(c):
                tok = n.transpose(bank[:, j * P:(j + 1) * P], sc[:, (g + j) * P:(g + j + 1) * P], u["tp"], bf,
                                  mark=(j == c - 1))
            u["tb"].append((b, bank, c, tok))
        self.sc.put(u["sci"], tok)

    def copied(self, u):
        n = self.n
        u["pti"], pt, pf = self.pt.take()
        u["pt"] = pt
        off = 0
        u["tc"] = []
        for b, bank, c, tok in u["tb"]:
            w = c * P
            t = n.act(lambda e, off=off, w=w, bank=bank: e.activation(pt[:, off:off + w], bank[:, 0:w], ACT.Copy),
                      tok, pf)
            n.banks.put(b, t)
            u["tc"].append(t)
            off += w

    def values(self, u):
        n = self.n
        b, bank, bf = n.banks.take()
        par = u["par"]
        o = bank[par * 64:par * 64 + 64, 0:P]
        tok = n.group(o, [(v, u["pt"][:, j * P:(j + 1) * P]) for j, v in enumerate(u["v"])], bf, u["tc"], u["waits"])
        self.pt.put(u["pti"], tok)
        u["pv"] = (b, o, tok)
        u["done_reading"] = tok
        if "after" in u:
            u["after"](tok)

    def stored(self, u):
        n = self.n
        b, o, tok = u["pv"]
        t = n.dve(lambda e: e.tensor_copy(u["out"], o), tok)
        n.banks.put(b, t)
        self.toks.append(t)


def ab_mixer(n, norm):
    ins = n.ins
    mark = n.top
    cos, sin = n.buf(512), n.buf(512)
    ma = n.buf(384)
    mb1 = n.buf(2048)
    mb23 = n.buf(256)
    sink = n.buf(12)
    qa = [n.buf(512) for _ in range(6)]
    ka = [n.buf(512) for _ in range(2)]
    va = n.buf(1024).rearrange("p (i c) -> p i c", i=4)
    qb = [n.buf(512) for _ in range(6)]
    kb = [n.buf(512) for _ in range(6)]
    vb = n.buf(3072).rearrange("p (g i c) -> p g i c", g=3, i=4)
    raws = Pool([n.buf(512) for _ in range(2)])
    tmps = Pool([n.buf(512) for _ in range(1)])
    o = [n.buf(512) for _ in range(8)]
    bar = n.barrier()
    tl = n.load([(cos, ins["rope1"][0]), (sin, ins["rope1"][1]), (ma, ins["mask_a"]), (mb1, ins["mask_b1"]),
                 (mb23, ins["mask_b23"]), (sink, ins["sink_a"].to_broadcast([P, 12]))], bar)
    xt = norm.finish("norm_mix_0", n.xn)
    dsts = qa + ka + qb + kb
    rt = {}

    def use(m, bank, tok):
        i, raw, rf = raws.take()
        scale = 0.125 if m < 6 or 8 <= m < 14 else 1.0
        t = n.act(lambda e: e.activation(raw, bank[:, :], ACT.Copy, scale=scale), tok, rf)
        done, reads = rope(n, raw, t, n.rot1, cos, sin, tmps, dsts[m], tl)
        raws.put(i, done, *reads)
        rt[m] = done
        return t

    heads_fm(n, [(ins["w_ab_qk"][j], 2) for j in range(10)], xt, use)
    tv = values_tm(n, ins["w_ab_v"][0], 256, xt, lambda k, i: n.xn[k][:, i * P:(i + 1) * P], lambda i: va[:, i, :])
    tvb = []
    for g in range(3):
        if g == 0:
            sel = lambda k, i: n.xn[k][:, i * P:(i + 1) * P]
        else:
            sel = lambda k, i: n.xn[k].rearrange("p (m r) -> p r m", r=4)[:, i, :]
        tvb += values_tm(n, ins["w_ab_v"][1 + g], 256, xt, sel, lambda i, g=g: vb[:, g, i, :])
    n.att = Attention(n, 768)
    units = []
    for t, pair in enumerate(A_TILES):
        for par, h in enumerate(pair):
            g = h // 3
            ps = slice(par * 64, par * 64 + 64)
            for i in range(4):
                lo, hi = max(0, i - 1), min(4, i + 2)
                ms = P * (lo - i + 1)
                units.append(dict(q=qa[t][ps, i * P:(i + 1) * P], keys=[[ka[g // 2][ps, lo * P:hi * P]]],
                                  mask=[ma[:, ms:ms + (hi - lo) * P]], sink=sink[:, h:h + 1], par=par,
                                  v=[va[:, j, g * 64:g * 64 + 64] for j in range(lo, hi)],
                                  out=o[t][ps, i * P:(i + 1) * P], waits=[rt[t], rt[6 + g // 2], tl] + tv))
    cls = lambda ap: ap.rearrange("p (m r) -> p r m", r=4)
    for s in range(4):
        par = s % 2
        ps = slice(par * 64, par * 64 + 64)
        t = [(g * 4 + s) // 2 for g in range(3)]
        for r in range(4):
            units.append(dict(
                q=[cls(qb[t[g]][ps, :])[:, r, :] for g in range(3)],
                keys=[[kb[t[0]][ps, :]], [cls(kb[t[1]][ps, :])[:, r, :], cls(kb[t[2]][ps, :])[:, r, :]]],
                mask=[mb1[:, r * 512:(r + 1) * 512], mb23], sink=None, par=par,
                v=[vb[:, 0, j, s * 64:s * 64 + 64] for j in range(4)] + [vb[:, g, r, s * 64:s * 64 + 64] for g in (1, 2)],
                out=cls(o[6 + s // 2][ps, :])[:, r, :],
                waits=[rt[8 + x] for x in t] + [rt[14 + x] for x in t] + [tl] + tvb))
    run_units(n.att, units)
    nxt = out_proj(n, ins["w_ab_out"], o, [n.att.toks] * 8)
    n.top = mark
    n.barrier()
    return nxt


def run_units(att, units):
    n = att.n
    plain = att.scores

    def scores(u):
        if not isinstance(u["q"], list):
            return plain(u)
        u["sb"] = []
        qs = list(u["q"])
        for part in u["keys"]:
            b, bank, bf = n.banks.take()
            off = 0
            for kap in part:
                w = kap.shape[-1]
                q = qs.pop(0)
                tok = n.pe(lambda e, bank=bank, off=off, w=w, kap=kap, q=q: e.matmul(bank[:, off:off + w], q, kap,
                                                                                   start=True, stop=True),
                           bf, u["waits"])
                off += w
            u["sb"].append((b, bank, off, tok))

    att.scores = scores
    att.run(units)


def c_mixer(n, norm):
    ins = n.ins
    mark = n.top
    cm = n.buf(1024)
    q = [n.buf(512) for _ in range(8)]
    k = [n.buf(512) for _ in range(8)]
    v = n.buf(4096).rearrange("p (i c) -> p i c", i=4)
    o = [n.buf(512) for _ in range(8)]
    bias = Pool([n.buf(1024) for _ in range(3)])
    bar = n.barrier()
    tl = n.load([(cm, ins["mask_c"])], bar)
    xt = norm.finish("norm_mix_1", n.xn)
    dsts = q + k
    rt = {}

    def use(m, bank, tok):
        rt[m] = n.act(lambda e: e.activation(dsts[m], bank[:, :], ACT.Copy, scale=0.125 if m < 8 else 1.0), tok)
        return rt[m]

    heads_fm(n, [(ins["w_c_qk"][j], 2) for j in range(8)], xt, use)
    tv = []
    for g in range(4):
        tv.append(values_tm(n, ins["w_c_v"][g], 256, xt, lambda kk, i: n.xn[kk][:, i * P:(i + 1) * P],
                            lambda i, g=g: v[:, i, g * 256:(g + 1) * 256]))
    att = Attention(n, 512)
    units = []
    bsem = n.sem("s_bias")
    bcount = [0]
    for h in range(16):
        t, par = h // 2, h % 2
        ps = slice(par * 64, par * 64 + 64)
        bias_of = {}
        for i in range(4):
            u = dict(q=q[t][ps, i * P:(i + 1) * P], keys=[[k[t][ps, :]]], sink=None, par=par,
                     v=[v[:, j, h * 64:h * 64 + 64] for j in range(4)], out=o[t][ps, i * P:(i + 1) * P],
                     mask=[None], waits=[rt[t], rt[8 + t]] + tv[h // 4])
            units.append(u)
    real = att.biased
    real_scores = att.scores
    cur = {}

    def fetch(h):
        i, ap, free = bias.take()
        bcount[0] += 16
        want = bcount[0]
        n.sp(lambda e: e.dma_start(ap, ins["rpb"][h]).then_inc(bsem, 16), free, cur.get("last"), bar, mark=False)
        t = n.pool(lambda e: e.tensor_tensor(ap, ap, cm, ALU.add), (bsem, want), tl)
        cur["last"] = t
        cur[h] = (i, ap, t)

    def scores(u):
        h, i = u["hi"]
        if i == 0:
            if h == 0:
                fetch(0)
            if h + 1 < 16:
                fetch(h + 1)
        real_scores(u)

    def biased(u):
        h, i = u["hi"]
        bi, ap, t = cur[h]
        u["mask"] = [ap[:, (7 - 2 * i) * 64:(15 - 2 * i) * 64]]
        u["waits"] = u["waits"] + [t]
        real(u)
        if i == 3:
            bias.put(bi, u["t"])

    for x, u in enumerate(units):
        u["hi"] = (x // 4, x % 4)
    att.scores, att.biased = scores, biased
    att.run(units)
    nxt = out_proj(n, ins["w_c_out"], o, [att.toks] * 8)
    n.top = mark
    n.barrier()
    return nxt


def ple(n, layer, norm):
    ins = n.ins
    mark = n.top
    p = [n.buf(512) for _ in range(2)]
    sgs = Pool([n.buf(512) for _ in range(2)])
    tl = n.load([(p[j], ins["p"][layer, j]) for j in range(2)], n.barrier())
    xt = norm.finish(f"norm_ple_{layer}", n.xn)
    nxt = Norm(n)
    for m in range(KT):
        w, wt, ws = n.weights(ins["w_ple"][layer, m], 1280)
        w = w.rearrange("p (k c) -> p k c", k=10)
        gb, g, gf = n.banks.take()
        ub, u, uf = n.banks.take()
        tg = n.group(g[:, :], [(w[:, k, :], n.xn[k], xt[k]) for k in range(KT)], wt, gf)
        tu = n.group(u[:, :], [(w[:, KT + k, :], p[k]) for k in range(2)], uf, tl)
        n.wslots.put(ws, tu)
        nxt.flush()
        i, sg, sf = sgs.take()
        t = n.act(lambda e, sg=sg, g=g: e.activation(sg, g[:, :], ACT.Sigmoid), tg, sf)
        n.banks.put(gb, t)
        t = n.dve(lambda e, sg=sg, u=u: e.tensor_tensor(sg, sg, u[:, :], ALU.mult), t, tu)
        n.banks.put(ub, t)
        t = n.dve(lambda e, sg=sg, m=m: e.tensor_tensor(n.h[m], n.h[m], sg, ALU.add), t)
        sgs.put(i, t)
        nxt.add(n.h[m], t)
        n.ht[m] = t
    n.top = mark
    n.barrier()
    return nxt


def first_block(n):
    ins = n.ins
    tx = n.load([(n.h[k], ins["x"][k]) for k in range(KT)])
    norm = Norm(n)
    n.ht = [tx] * KT
    for k in range(KT):
        norm.add(n.h[k], tx)
        norm.flush()
    for layer in range(2):
        norm = ffn(n, ins["w_gu"][2 * layer], ins["w_dn"][2 * layer], norm, f"norm_ffn1_{layer}")
        norm = (ab_mixer if layer == 0 else c_mixer)(n, norm)
        norm = ffn(n, ins["w_gu"][2 * layer + 1], ins["w_dn"][2 * layer + 1], norm, f"norm_ffn2_{layer}")
        norm = ple(n, layer, norm)
    n.ht = norm.finish("norm_final", n.h)
    norm = Norm(n)
    for k in range(KT):
        norm.add(n.h[k], n.ht[k])
        norm.flush()
    return norm


def shift_tokens(n, raw, c0, mp, mn, dst, tok, free):
    x, p, q = raw[:, 1:513], raw[:, 0:512], raw[:, 2:514]
    t = n.dve(lambda e: e.tensor_scalar(dst, x, c0, None, ALU.mult), tok, free)
    t = n.dve(lambda e: e.scalar_tensor_tensor(out=dst, in0=p, scalar=mp, in1=dst, op0=ALU.mult, op1=ALU.add), t)
    t = n.dve(lambda e: e.scalar_tensor_tensor(out=dst, in0=q, scalar=mn, in1=dst, op0=ALU.mult, op1=ALU.add), t)
    return t


def rwkv(n, xt):
    ins = n.ins
    v4 = lambda b: b.rearrange("p (a t) -> p a t", a=4)
    R, K = n.buf(2048), n.buf(2048)
    Y = n.y_rwkv = n.buf(2048)
    V, KK, BON = (n.buf(2048) for _ in range(3))
    lora = [n.buf(512) for _ in range(3)]
    reset = n.buf(512)
    masks = n.buf(448)
    ptc = v4(n.buf(32))
    state = n.buf(512)
    AL, RT, BT, KTL = (n.buf(2048) for _ in range(4))
    work = n.top
    raws = Pool([n.buf(514) for _ in range(2)])
    bar = n.barrier()
    tl = n.load([(reset, ins["reset"])], bar)
    mp, mn, c0 = n.vec("shift_prev"), n.vec("shift_next"), n.cc[:, 0:15]
    omka = n.cc[:, 15:19]
    vv = lambda name, k: n.vecs[:, VEC[name]:VEC[name] + k]
    t = n.dve(lambda e: e.tensor_tensor(c0, vv("shift_prev", 15), vv("shift_next", 15), ALU.add))
    t = n.dve(lambda e: e.tensor_scalar(c0, c0, -1.0, 1.0, ALU.mult, ALU.add), t)
    tc = n.dve(lambda e: e.tensor_scalar(omka, vv("k_a", 4), -1.0, 1.0, ALU.mult, ALU.add), t)
    tz = []
    for r in raws.items:
        n.pool(lambda e, r=r: e.memset(r[:, 0:1], 0.0))
        tz = n.pool(lambda e, r=r: e.memset(r[:, 513:514], 0.0))
    dsts = [b[:, j * 512:(j + 1) * 512] for b in (R, K, V) for j in range(4)] + lora
    done = {}

    def use(m, bank, tok):
        i, raw, rf = raws.take()
        t = n.act(lambda e: e.activation(raw[:, 1:513], bank[:, :], ACT.Copy), tok, rf)
        done[m] = shift_tokens(n, raw, n.cc[:, m:m + 1], n.vec("shift_prev", m), n.vec("shift_next", m), dsts[m],
                               [t, tz, tc], None)
        raws.put(i, done[m])
        return t

    heads_fm(n, [(ins["w2_rwkv"][j], 2) for j in range(7)] + [(ins["w2_rwkv1"], 1)], xt, use)
    t_wd = n.act(lambda e: e.activation(lora[0], lora[0], ACT.Tanh), done[12])
    t_gd = n.act(lambda e: e.activation(lora[2], lora[2], ACT.Sigmoid), done[14])
    bar = n.barrier()
    n.top = work
    scr = [n.buf(512) for _ in range(10)]
    kk_t = []
    for j in range(4):
        kk, sq = KK[:, j * 512:(j + 1) * 512], scr[j]
        t = n.dve(lambda e, j=j, kk=kk: e.tensor_scalar(kk, K[:, j * 512:(j + 1) * 512], n.vec("k_k", j), None, ALU.mult))
        t = n.act(lambda e, kk=kk, sq=sq: e.activation(sq, kk, ACT.Square), t)
        b, bank, bf = n.banks.take()
        tok = n.group(bank[:, :], [(n.bones, sq)], t, bf)
        t = n.act(lambda e, bank=bank, sq=sq: e.activation(sq, bank[:, :], ACT.Sqrt), tok)
        n.banks.put(b, t)
        t = n.dve(lambda e, sq=sq: e.tensor_scalar(sq, sq, 1e-12, None, ALU.max), t)
        t = n.dve(lambda e, sq=sq: e.reciprocal(sq, sq), t)
        kk_t.append(n.dve(lambda e, kk=kk, sq=sq: e.tensor_tensor(kk, kk, sq, ALU.mult), t))
    n.barrier()
    ct = lambda b: b.rearrange("p (c t) -> p c t", t=64)
    for d in range(2):
        n.top = work
        scr = [n.buf(512) for _ in range(14)]
        bar = n.barrier()
        tm = n.load([(masks, ins["mask_r"][d])], bar)
        free = [[], []]
        lw_ap, lwt, lws = n.weights(ins["lora"][d], 1024)
        for j in range(4):
            js = slice(j * 512, (j + 1) * 512)
            sg, lw, C, X, P1, Pe, IP = scr[7 * (j % 2):7 * (j % 2) + 7]
            fr = free[j % 2]
            b, bank, bf = n.banks.take()
            tok = n.group(bank[:, :], [(lw_ap[:, j * 128:(j + 1) * 128], lora[0])], lwt, t_wd, bf)
            t = n.act(lambda e, sg=sg, bank=bank, j=j, d=d: e.activation(sg, bank[:, :], ACT.Sigmoid, bias=n.vec(f"w0_{d}", j)), tok, fr)
            n.banks.put(b, t)
            b, bank, bf = n.banks.take()
            tok = n.group(bank[:, :], [(lw_ap[:, 512 + j * 128:512 + (j + 1) * 128], lora[1])], lwt, bf)
            if j == 3:
                n.wslots.put(lws, tok)
            tlw = n.dve(lambda e, lw=lw, sg=sg: e.tensor_scalar(lw, sg, -float(np.exp(-0.5)), None, ALU.mult), t, fr)
            ta = n.act(lambda e, sg=sg, bank=bank, j=j, d=d: e.activation(sg, bank[:, :], ACT.Sigmoid, bias=n.vec(f"a0_{d}", j)), tok, tlw)
            n.banks.put(b, ta)
            av = sg
            tC = n.dve(lambda e, C=C, lw=lw: e.tensor_tensor_scan(C, reset, lw, 0.0, ALU.mult, ALU.add), tlw, tl)
            if d == 0:
                inc, exc = C, X
                tX = n.dve(lambda e, C=C, lw=lw, X=X: e.tensor_tensor(X, C, lw, ALU.subtract), tC)
                ti = tC
            else:
                inc, exc = C, X
                tot = ct(C)[:, :, 63:64].to_broadcast([P, 8, 64])
                tX = n.dve(lambda e, C=C, X=X, tot=tot: e.tensor_tensor(ct(X), tot, ct(C), ALU.subtract), tC)
                ti = n.dve(lambda e, C=C, lw=lw, X=X: e.tensor_tensor(C, X, lw, ALU.add), tX)
            tP = n.act(lambda e, P1=P1, inc=inc: e.activation(P1, inc, ACT.Exp), ti)
            tPe = n.act(lambda e, Pe=Pe, exc=exc: e.activation(Pe, exc, ACT.Exp), tX)
            tIP = n.act(lambda e, IP=IP, inc=inc: e.activation(IP, inc, ACT.Exp, scale=-1.0), ti)
            end = 63 if d == 0 else 0
            t1 = n.pool(lambda e, j=j, P1=P1, end=end: e.tensor_copy(ptc[:, j, :], ct(P1)[:, :, end]), tP)
            t2 = n.pool(lambda e, js=js, P1=P1: e.tensor_tensor(RT[:, js], R[:, js], P1, ALU.mult), tP)
            t3 = n.dve(lambda e, js=js, Pe=Pe: e.scalar_tensor_tensor(out=AL[:, js], in0=KK[:, js], scalar=-1.0, in1=Pe,
                                                                   op0=ALU.mult, op1=ALU.mult), tPe, kk_t)
            t4 = n.dve(lambda e, js=js, av=av, lw=lw: e.tensor_tensor(lw, KK[:, js], av, ALU.mult), ta, ti, tX)
            t4 = n.pool(lambda e, js=js, IP=IP, lw=lw: e.tensor_tensor(BT[:, js], lw, IP, ALU.mult), t4, tIP)
            t5 = n.dve(lambda e, av=av, j=j: e.tensor_scalar(av, av, n.vec("k_a", j), n.cc[:, 15 + j:16 + j], ALU.mult, ALU.add), t4, tc)
            t5 = n.dve(lambda e, av=av, js=js: e.tensor_tensor(av, av, K[:, js], ALU.mult), t5)
            t6 = n.dve(lambda e, av=av, js=js, IP=IP: e.tensor_tensor(KTL[:, js], av, IP, ALU.mult), t5, tIP)
            if d == 0:
                t7 = n.pool(lambda e, av=av, js=js: e.tensor_copy(BON[:, js], av), t5)
            else:
                t7 = n.pool(lambda e, av=av, js=js: e.tensor_tensor(BON[:, js], BON[:, js], av, ALU.add), t5)
            free[j % 2] = [t1, t2, t3, t4, t6, t7]
        n.top = work
        chunks(n, d, dict(R=R, V=V, AL=AL, RT=RT, BT=BT, KT=KTL, Y=Y, masks=masks, ptc=ptc, state=state, tm=tm))
    n.top = work
    bar = n.barrier()
    scr = [n.buf(512) for _ in range(8)]
    gw, gwt, gs = n.weights(ins["g2"], 512)
    yt = []
    fr = [[], []]
    for j in range(4):
        js = slice(j * 512, (j + 1) * 512)
        y = Y[:, js]
        mu, yc, sq, bo = scr[4 * (j % 2):4 * (j % 2) + 4]
        b, bank, bf = n.banks.take()
        tok = n.group(bank[:, :], [(n.bones, y)], bf)
        t = n.dve(lambda e, yc=yc, bank=bank, y=y: e.scalar_tensor_tensor(out=yc, in0=bank[:, :], scalar=-1.0 / 64, in1=y,
                                                                       op0=ALU.mult, op1=ALU.add), tok, fr[j % 2])
        n.banks.put(b, t)
        ty = t
        t = n.act(lambda e, sq=sq, yc=yc: e.activation(sq, yc, ACT.Square), t, fr[j % 2])
        b, bank, bf = n.banks.take()
        tok = n.group(bank[:, :], [(n.bones, sq)], t, bf)
        t = n.dve(lambda e, mu=mu, bank=bank: e.tensor_scalar(mu, bank[:, :], 1.0 / 64, 64e-5, ALU.mult, ALU.add), tok, fr[j % 2])
        n.banks.put(b, t)
        t = n.act(lambda e, mu=mu: e.activation(mu, mu, ACT.Sqrt), t)
        t = n.dve(lambda e, mu=mu: e.reciprocal(mu, mu), t)
        t = n.dve(lambda e, yc=yc, mu=mu: e.tensor_tensor(yc, yc, mu, ALU.mult), t, ty)
        tn = n.dve(lambda e, yc=yc, j=j: e.tensor_scalar(yc, yc, n.vec("ln_w", j), n.vec("ln_b", j), ALU.mult, ALU.add), t)
        t = n.dve(lambda e, bo=bo, js=js, j=j: e.scalar_tensor_tensor(out=bo, in0=BON[:, js], scalar=n.vec("r_k", j), in1=R[:, js],
                                                                   op0=ALU.mult, op1=ALU.mult), fr[j % 2])
        b, bank, bf = n.banks.take()
        tok = n.group(bank[:, :], [(n.bones, bo)], t, bf)
        t = n.dve(lambda e, bo=bo, bank=bank, js=js: e.tensor_tensor(bo, bank[:, :], V[:, js], ALU.mult), tok)
        n.banks.put(b, t)
        t = n.dve(lambda e, bo=bo, yc=yc: e.tensor_tensor(yc, yc, bo, ALU.add), t, tn)
        b, bank, bf = n.banks.take()
        tok = n.group(bank[:, :], [(gw[:, j * 128:(j + 1) * 128], lora[2])], gwt, t_gd, bf)
        t = n.dve(lambda e, y=y, yc=yc, bank=bank: e.tensor_tensor(y, yc, bank[:, :], ALU.mult), t, tok)
        n.banks.put(b, t)
        fr[j % 2] = [t]
        yt.append(t)
    n.wslots.put(gs, tok)
    return yt


def chunks(n, d, q):
    NT = 12
    assert n.top + 24 * 512 <= n.nf, n.top + 24 * 512 - n.nf
    bufs = [[n.buf(512) for _ in range(NT)] for _ in range(2)]
    f4 = lambda b: b.rearrange("p (a t) -> p a t", a=4)
    bar = n.barrier()
    last = [None] * 2
    for s in range(2):
        for i in range(4):
            n.pool(lambda e, s=s, i=i: e.memset(bufs[s][i], 0.0))
    tz = n.pool(lambda e: e.memset(q["state"], 0.0))
    n.barrier()
    Dm = q["masks"][:, 0:128].unsqueeze(1).to_broadcast([P, 4, 128])
    Om = q["masks"][:, 128:256].unsqueeze(1).to_broadcast([P, 4, 128])
    Sm = q["masks"][:, 256:384].unsqueeze(1).to_broadcast([P, 4, 128])
    Im = q["masks"][:, 384:448].unsqueeze(1).to_broadcast([P, 8, 64])
    Id = n.ident.unsqueeze(1).to_broadcast([P, 4, 128])
    ST = q["state"]
    seq = dict(st=tz, y=None)

    def mul4(lhs, rhs, waits, lhs2=None, rhs2=None):
        b, bank, bf = n.banks.take()
        for p in range(4):
            c = slice(p * 128, (p + 1) * 128)
            n.pe(lambda e, c=c: e.matmul(bank[:, c], lhs[:, c], rhs[:, c], start=True, stop=lhs2 is None), bf, waits,
                 mark=False)
            if lhs2 is not None:
                n.pe(lambda e, c=c: e.matmul(bank[:, c], lhs2[:, c], rhs2[:, c], start=False, stop=True), mark=False)
        return b, bank

    def turn4(src, waits):
        b, bank, bf = n.banks.take()
        for p in range(4):
            c = slice(p * 128, (p + 1) * 128)
            n.transpose(bank[:, c], src[:, c], bf, waits, mark=False)
        return b, bank

    def sealed():
        return n.pe.sealed()

    def out_act(pair, dst, *waits):
        b, bank = pair
        t = n.act(lambda e: e.activation(dst, bank[:, :], ACT.Copy), *waits)
        n.banks.put(b, t)
        return t

    def out_dve(pair, dst, *waits):
        b, bank = pair
        t = n.dve(lambda e: e.tensor_copy(dst, bank[:, :]), *waits)
        n.banks.put(b, t)
        return t

    def add_dve(pair, dst, *waits):
        b, bank = pair
        t = n.dve(lambda e: e.tensor_tensor(dst, bank[:, :], dst, ALU.add), *waits)
        n.banks.put(b, t)
        return t

    def s0(u):
        c = u["c"]
        B = u["B"]
        cs = slice(c * 64, (c + 1) * 64)
        prev = last[u["s"]]
        toks = []
        for i, (name, eng) in enumerate((("AL", "p"), ("BT", "p"), ("KT", "a"), ("V", "a"))):
            src = f4(q[name])[:, :, cs]
            dst = B[i].rearrange("p (a h t) -> p a h t", a=4, h=2)
            for h in range(2):
                hs = slice(h * 64, h * 64 + 64)
                if eng == "p":
                    toks.append(n.pool(lambda e, src=src, dst=dst, hs=hs, h=h: e.tensor_copy(dst[hs, :, h, :], src[hs]), prev))
                else:
                    toks.append(n.act(lambda e, src=src, dst=dst, hs=hs, h=h: e.activation(dst[hs, :, h, :], src[hs], ACT.Copy), prev))
        u["t0"] = toks
        r = f4(q["RT"])[:, :, cs]
        u["r"] = r
        m1 = mul4(B[1], B[0], toks)
        m2 = mul4(B[2], B[0], toks)
        b, bank, bf = n.banks.take()
        for z in range(2):
            for p in range(4):
                n.pe(lambda e, z=z, p=p: e.matmul(bank[:, z * 256 + p * 64:z * 256 + p * 64 + 64],
                                                B[1 + z][:, p * 128:(p + 1) * 128], r[:, p, :], start=True, stop=True),
                     bf, mark=False)
        t = sealed()
        w = [t, q["tm"], prev]
        n.dve(lambda e: e.tensor_tensor(f4(B[4]), f4(m1[1][:, :]), Dm, ALU.mult), w)
        ta = n.dve(lambda e: e.tensor_tensor(f4(B[5]), f4(m1[1][:, :]), Om, ALU.mult), w)
        n.banks.put(m1[0], ta)
        tb = n.dve(lambda e: e.tensor_tensor(f4(B[6]), f4(m2[1][:, :]), Sm, ALU.mult), w)
        n.banks.put(m2[0], tb)
        e8 = lambda x: x.rearrange("p (a t) -> p a t", a=8)
        tc = n.dve(lambda e: e.tensor_tensor(e8(B[7]), e8(bank[:, :]), Im, ALU.mult), w)
        n.banks.put(b, tc)
        u["tN"], u["t6"], u["t7"] = ta, tb, tc

    def s1(u):
        B = u["B"]
        a = turn4(B[4], u["tN"])
        b = turn4(B[1], u["t0"])
        k = turn4(B[2], None)
        v = turn4(B[3], None)
        t = sealed()
        u["tA"] = out_dve(a, B[8], t)
        u["tb"] = out_act(b, B[9], t, last[u["s"]])
        u["tk"] = out_act(k, B[10], t)
        u["tv"] = out_act(v, B[11], t)
        u["tP"] = n.dve(lambda e: e.tensor_tensor(f4(B[1]), f4(B[4]), Id, ALU.add), t)

    def s2(u):
        B = u["B"]
        x = mul4(B[8], B[4], [u["tA"]])
        y = mul4(B[4], B[8], None)
        t = sealed()
        u["tx"] = out_act(x, B[2], t)
        u["ty"] = out_dve(y, B[3], t)

    def s3(u):
        B = u["B"]
        x = mul4(B[3], B[2], [u["tx"], u["ty"]])
        y = mul4(B[2], B[3], None)
        p = mul4(B[3], B[1], [u["tP"]])
        t = sealed()
        u["tx"] = out_act(x, B[4], t)
        u["ty"] = out_act(y, B[8], t)
        u["tP"] = add_dve(p, B[1], t)

    def s4(u):
        B = u["B"]
        y = mul4(B[4], B[8], [u["tx"], u["ty"]])
        p = mul4(B[8], B[1], [u["tP"]])
        t = sealed()
        u["ty"] = out_act(y, B[2], t)
        u["tP"] = add_dve(p, B[1], t)

    def s5(u):
        B = u["B"]
        p = mul4(B[2], B[1], [u["ty"], u["tP"]])
        u["tP"] = add_dve(p, B[1], sealed())

    def s6(u):
        B = u["B"]
        p = turn4(B[1], [u["tP"]])
        u["tPT"] = out_act(p, B[3], sealed())

    def s7(u):
        B = u["B"]
        z = mul4(B[3], B[5], [u["tPT"]])
        y = mul4(B[5], B[3], None)
        t = sealed()
        u["tx"] = out_act(z, B[4], t)
        u["ty"] = out_dve(y, B[8], t)

    def s8(u):
        B = u["B"]
        y = mul4(B[4], B[8], [u["tx"], u["ty"]])
        u["tz"] = out_act(y, B[2], sealed())

    def s9(u):
        B = u["B"]
        p = mul4(B[2], B[1], [u["tz"], u["tP"]])
        u["tP"] = add_dve(p, B[1], sealed())

    def s10(u):
        B = u["B"]
        p = mul4(B[8], B[1], [u["tP"], u["ty"]])
        u["tP"] = add_dve(p, B[1], sealed())

    def s11(u):
        B = u["B"]
        x = mul4(B[0], ST, [seq["st"], u["t6"], u["tv"], u["t0"]], B[6], B[11])
        u["tX"] = out_act(x, B[3], sealed())

    def s12(u):
        B = u["B"]
        x = mul4(B[1], B[3], [u["tX"], u["tP"]])
        u["tU"] = out_dve(x, B[5], sealed())

    def s13(u):
        B, c = u["B"], u["c"]
        waits = [u["tU"], u["tb"], u["tk"], u["tv"], u["t7"], seq["st"]]
        x = mul4(B[9], B[5], waits, B[10], B[11])
        b, bank, bf = n.banks.take()
        for p in range(4):
            c2 = slice(p * 128, (p + 1) * 128)
            o = bank[:, p * 64:(p + 1) * 64]
            prods = [(ST[:, c2], u["r"][:, p, :]), (B[5][:, c2], B[7][:, p * 64:(p + 1) * 64]),
                     (B[11][:, c2], B[7][:, 256 + p * 64:256 + (p + 1) * 64])]
            for j, (l, r) in enumerate(prods):
                n.pe(lambda e, o=o, l=l, r=r, j=j: e.matmul(o, l, r, start=(j == 0), stop=(j == 2)), bf, waits, mark=False)
        t = sealed()
        ta = n.dve(lambda e: e.tensor_tensor(ST, x[1][:, :], ST, ALU.add), t)
        n.banks.put(x[0], ta)
        pt = q["ptc"][:, :, c:c + 1].to_broadcast([P, 4, 128])
        seq["st"] = n.dve(lambda e: e.tensor_tensor(f4(ST), f4(ST), pt, ALU.mult), ta)
        y = f4(q["Y"])[:, :, c * 64:(c + 1) * 64]
        ps = bank[:, 0:256].rearrange("p (a t) -> p a t", a=4)
        if d == 0:
            ty = n.act(lambda e: e.activation(y, ps, ACT.Copy), t)
        else:
            ty = n.dve(lambda e: e.tensor_tensor(y, ps, y, ALU.add), t)
        n.banks.put(b, ty)
        last[u["s"]] = [t]

    steps = [s0, s1, s2, s3, s4, s5, s6, s7, s8, s9, s10, s11, s12, s13]
    order = range(8) if d == 0 else range(7, -1, -1)
    units = [dict(c=c, s=i % 2, B=bufs[i % 2]) for i, c in enumerate(order)]
    L = 7
    for tau in range(L * (len(units) - 1) + len(steps)):
        for i in range(len(units)):
            s = tau - L * i
            if 0 <= s < len(steps):
                steps[s](units[i])


def pool_branch(n, xt):
    ins = n.ins
    a = Pool([n.buf(528) for _ in range(2)])
    bufs = [n.buf(528) for _ in range(2)]
    icnt = n.buf(2048)
    pooled = [n.buf(512) for _ in range(4)]
    bar = n.barrier()
    tl = n.load([(icnt, ins["icnt"])], bar)
    tz = None
    for r in a.items:
        n.pool(lambda e, r=r: e.memset(r[:, 0:8], 0.0))
        tz = n.pool(lambda e, r=r: e.memset(r[:, 520:528], 0.0))
    w, wt, ws = n.weights(ins["pool_w"], 512)
    out = []

    def use(m, bank, tok):
        i, z, zf = a.take()
        tz1 = n.act(lambda e: e.activation(z[:, 8:520], bank[:, :], ACT.Copy), tok, zf)
        wd = (2, 4, 8, 16)[m]
        src, ln, t = z, 528, [tz1, tz]
        for s in range(m + 1):
            st = 1 << s
            ln -= st
            dst = bufs[s % 2]
            t = n.dve(lambda e, src=src, dst=dst, st=st, ln=ln: e.tensor_tensor(dst[:, 0:ln], src[:, 0:ln], src[:, st:st + ln],
                                                                              ALU.add), t)
            src = dst
        x0 = 8 - wd // 2
        t = n.dve(lambda e, src=src: e.tensor_tensor(pooled[m], src[:, x0:x0 + 512], icnt[:, m * 512:(m + 1) * 512], ALU.mult), t, tl)
        t = n.dve(lambda e: e.tensor_tensor(pooled[m], pooled[m], z[:, 8:520], ALU.subtract), t)
        a.put(i, t)
        out.append(t)
        return tz1

    heads_fm(n, [(ins["w2_pool"][j], 2) for j in range(2)], xt, use)
    toks = []
    for m in range(4):
        b, bank, bf = n.banks.take()
        tok = n.group(bank[:, :], [(w[:, m * 128:(m + 1) * 128], pooled[m])], wt, out[m], bf)
        t = n.dve(lambda e, m=m, bank=bank: e.tensor_scalar(n.y_pool[m], bank[:, :], n.vec("pool_scale", m), None, ALU.mult), tok)
        n.banks.put(b, t)
        toks.append(t)
    n.wslots.put(ws, tok)
    return toks


def axial_attention(n, xt):
    ins = n.ins
    cos, sin = n.buf(512), n.buf(512)
    q = [n.buf(512) for _ in range(4)]
    k = n.buf(512)
    v = n.buf(512).rearrange("p (i c) -> p i c", i=4)
    raws = Pool([n.buf(512) for _ in range(2)])
    tmps = Pool([n.buf(512) for _ in range(2)])
    rs = Pool([n.buf(512) for _ in range(2)])
    bar = n.barrier()
    tl = n.load([(cos, ins["rope2"][0]), (sin, ins["rope2"][1])], bar)
    dsts = q + [k]
    rt = {}

    def use(m, bank, tok):
        i, raw, rf = raws.take()
        j, r, rrf = rs.take()
        t0 = n.act(lambda e: e.activation(raw, bank[:, :], ACT.Copy), tok, rf)
        t = n.act(lambda e: e.activation(r, raw, ACT.Square), t0, rrf)
        b, bk, bf = n.banks.take()
        tk = n.group(bk[:, :], [(n.bones, r)], t, bf)
        t = n.dve(lambda e: e.tensor_scalar(r, bk[:, :], 1.0 / 64, EPS, ALU.mult, ALU.add), tk)
        n.banks.put(b, t)
        t = n.act(lambda e: e.activation(r, r, ACT.Sqrt, scale=64.0 if m < 4 else 1.0), t)
        t = n.dve(lambda e: e.reciprocal(r, r), t)
        g = n.vec("q_norm" if m < 4 else "k_norm")
        t = n.dve(lambda e: e.scalar_tensor_tensor(out=raw, in0=raw, scalar=g, in1=r, op0=ALU.mult, op1=ALU.mult), t)
        rs.put(j, t)
        done, reads = rope(n, raw, t, n.rot2, cos, sin, tmps, dsts[m], tl)
        raws.put(i, done, *reads)
        rt[m] = done
        return t0

    heads_fm(n, [(ins["w2_att"][0], 2), (ins["w2_att"][1], 2), (ins["w2_att1"], 1)], xt, use)
    tv = values_tm(n, ins["w2_attv"], 128, xt, lambda kk, i: n.xn[kk][:, i * P:(i + 1) * P], lambda i: v[:, i, :])
    att = Attention(n, 512)
    units = []
    for t, pair in enumerate(ATT_TILES):
        for par, h in enumerate(pair):
            ps = slice(par * 64, par * 64 + 64)
            for i in range(4):
                units.append(dict(q=q[t][ps, i * P:(i + 1) * P], keys=[[k[ps, :]]], mask=None, sink=None, par=par,
                                  v=[v[:, j, par * 64:par * 64 + 64] for j in range(4)],
                                  out=n.y_att[t][ps, i * P:(i + 1) * P], waits=[rt[t], rt[4]] + tv))
    att.run(units)
    return att.toks


def merge(n, xt, yt, pt, at):
    mark = n.top
    sgs = Pool([n.buf(512) for _ in range(3)])
    mg = [n.buf(512) for _ in range(KT)]
    n.barrier()
    ys = [([n.y_rwkv[:, j * 512:(j + 1) * 512] for j in range(4)], yt), (n.y_pool, pt), (n.y_att, [at] * 4)]
    mt = []
    for m in range(KT):
        for z in range(3):
            w, wt, ws = n.weights(n.ins["w2_gate"][m, z], 1536)
            w = w.rearrange("p (k c) -> p k c", k=12)
            gb, g, gf = n.banks.take()
            ub, u, uf = n.banks.take()
            tg = n.group(g[:, :], [(w[:, k, :], n.xn[k], xt[k]) for k in range(KT)], wt, gf)
            tu = n.group(u[:, :], [(w[:, KT + k, :], ys[z][0][k], ys[z][1][k]) for k in range(4)], uf)
            n.wslots.put(ws, tu)
            i, sg, sf = sgs.take()
            t = n.act(lambda e, sg=sg, g=g: e.activation(sg, g[:, :], ACT.Sigmoid), tg, sf)
            n.banks.put(gb, t)
            if z == 0:
                t = n.dve(lambda e, m=m, sg=sg, u=u: e.tensor_tensor(mg[m], sg, u[:, :], ALU.mult), t, tu)
                n.banks.put(ub, t)
                ta = t
            else:
                t = n.dve(lambda e, sg=sg, u=u: e.tensor_tensor(sg, sg, u[:, :], ALU.mult), t, tu)
                n.banks.put(ub, t)
                t = ta = n.dve(lambda e, m=m, sg=sg: e.tensor_tensor(mg[m], mg[m], sg, ALU.add), t, ta)
            sgs.put(i, t)
        mt.append(ta)
    nxt = out_proj(n, n.ins["w2_out"], mg, mt)
    n.top = mark
    n.barrier()
    return nxt


def experts(n, norm):
    ins = n.ins
    mark = n.top
    router = n.buf(128)
    iota = n.buf(64)
    slotcol = n.buf(1)
    sels = n.buf(1024)
    small = n.buf(4 * 16 * 4 + 16)
    affT, work, slotT, eq = (n.buf(512) for _ in range(4))
    mx8 = n.buf(8)
    ones5 = n.buf(512)
    big = n.buf(8192)
    hn_tok = big[:, 0:4096].rearrange("p (i f) -> p i f", i=4)
    G = big[:, 4096:8192].rearrange("p (i s) -> p i s", i=4)
    ys = [big[:, i * 1024:(i + 1) * 1024] for i in range(8)]
    xg = n.buf(8192).rearrange("p (k s) -> p k s", k=KT)
    gv = [n.buf(512) for _ in range(8)]
    va = Pool([n.buf(512) for _ in range(2)])
    hids = Pool([n.buf(1024) for _ in range(1)])
    hidTs = Pool([n.buf(1024) for _ in range(2)])
    bar = n.barrier()
    tl = n.load([(router, ins["router"]), (iota, ins["iota"]), (slotcol, ins["slotcol"]), (sels[0:16], ins["sels"])], bar)
    to = n.pool(lambda e: e.memset(ones5, 1.0))
    xt = norm.finish("norm_ffn_2", n.xn)
    b, bank, bf = n.banks.take()
    for i in range(4):
        t = n.group(bank[:, i * 16:(i + 1) * 16],
                    [(n.xn[k][:, i * P:(i + 1) * P], router[:, k * 16:(k + 1) * 16], xt[k]) for k in range(KT)], tl, bf)
    l3 = bank[:, 0:64].rearrange("p (i e) -> p i e", i=4)
    aff = small[:, 0:64].rearrange("p (i e) -> p i e", i=4)
    slot = small[:, 64:128].rearrange("p (i e) -> p i e", i=4)
    m4, s4 = small[:, 128:132], small[:, 132:136]
    t1 = n.dve(lambda e: e.tensor_reduce(m4, l3, AX_X, ALU.max), t)
    t = n.dve(lambda e: e.tensor_tensor(aff, l3, m4.unsqueeze(2).to_broadcast([P, 4, 16]), ALU.subtract), t1)
    n.banks.put(b, t)
    t = n.act(lambda e: e.activation(aff, aff, ACT.Exp), t)
    t = n.dve(lambda e: e.tensor_reduce(s4, aff, AX_X, ALU.add), t)
    t = n.dve(lambda e: e.reciprocal(s4, s4), t)
    t_aff = n.dve(lambda e: e.tensor_tensor(aff, aff, s4.unsqueeze(2).to_broadcast([P, 4, 16]), ALU.mult), t)
    b, bank, bf = n.banks.take()
    for i in range(4):
        tok = n.transpose(bank[0:16, i * P:(i + 1) * P], aff[:, i, :], t_aff, bf)
    tT = n.dve(lambda e: e.tensor_copy(affT[0:16], bank[0:16, :]), tok)
    n.banks.put(b, tT)
    for i in range(4):
        for half in range(2):
            b, bank, bf = n.banks.take()
            for j in range(4):
                k = 4 * half + j
                tok = n.transpose(bank[:, j * P:(j + 1) * P], n.xn[k][:, i * P:(i + 1) * P], bf, xt[k], mark=(j == 3))
            th = n.act(lambda e, i=i, half=half, bank=bank: e.activation(hn_tok[:, i, half * 512:(half + 1) * 512], bank[:, :],
                                                                      ACT.Copy), tok)
            n.banks.put(b, th)
    t = tT
    for r in range(8):
        src = affT if r == 0 else work
        t = n.dve(lambda e, src=src: e.max(mx8[0:16], src[0:16]), t)
        t = n.dve(lambda e, src=src: e.match_replace(work[0:16], mx8[0:16], src[0:16], -1.0), t)
    t = n.dve(lambda e: e.tensor_scalar(eq[0:16], work[0:16], 0.0, None, ALU.is_lt), t)
    t = n.dve(lambda e: e.tensor_tensor_scan(slotT[0:16], ones5[0:16], eq[0:16], 0.0, ALU.mult, ALU.add), t, to)
    t = n.dve(lambda e: e.tensor_tensor(slotT[0:16], slotT[0:16], eq[0:16], ALU.mult), t)
    t_slot = n.dve(lambda e: e.tensor_scalar(slotT[0:16], slotT[0:16], -1.0, None, ALU.add), t)
    b, bank, bf = n.banks.take()
    for i in range(4):
        tok = n.transpose(bank[:, i * 16:(i + 1) * 16], slotT[0:16, i * P:(i + 1) * P], t_slot, bf)
    t = n.dve(lambda e: e.tensor_copy(small[:, 64:128], bank[:, 0:64]), tok)
    n.banks.put(b, t)
    for i in range(4):
        tG = n.dve(lambda e, i=i: e.tensor_tensor(G[:, i, :].rearrange("p (a s) -> p a s", a=16),
                                                iota.unsqueeze(1).to_broadcast([P, 16, 64]),
                                                slot[:, i, :].unsqueeze(2).to_broadcast([P, 16, 64]), ALU.is_equal), t, tl)
    txg = {}
    for half in range(2):
        for k in range(KT):
            b, bank, bf = n.banks.take()
            tok = n.group(bank[:, :], [(hn_tok[:, i, k * P:(k + 1) * P], G[:, i, half * 512:(half + 1) * 512]) for i in range(4)],
                          tG, th, bf)
            f = n.act if k % 2 else n.dve
            if k % 2:
                t = n.act(lambda e, k=k, half=half, bank=bank: e.activation(xg[:, k, half * 512:(half + 1) * 512], bank[:, :], ACT.Copy), tok)
            else:
                t = n.dve(lambda e, k=k, half=half, bank=bank: e.tensor_copy(xg[:, k, half * 512:(half + 1) * 512], bank[:, :]), tok)
            n.banks.put(b, t)
            txg[k, half] = t
    t_dispatched = tok
    tgv = []
    for i in range(8):
        sel = sels[0:16, i * P:(i + 1) * P]
        b, bank, bf = n.banks.take()
        tok = n.group(bank[:, :], [(sel, affT[0:16])], bf, tT, tl)
        vi, vb, vf = va.take()
        t1 = n.act(lambda e, vb=vb, bank=bank: e.activation(vb, bank[:, :], ACT.Copy), tok, vf)
        n.banks.put(b, t1)
        b, bank, bf = n.banks.take()
        tok = n.group(bank[:, :], [(sel, slotT[0:16])], bf, t_slot)
        t = n.dve(lambda e, i=i, vb=vb, bank=bank: e.scalar_tensor_tensor(out=gv[i], in0=bank[:, :], scalar=slotcol, in1=vb,
                                                                       op0=ALU.is_equal, op1=ALU.mult), tok, t1)
        n.banks.put(b, t)
        va.put(vi, t)
        tgv.append(t)
    wblk = lambda w, e, j: w[e, j * 256:(j + 1) * 256, :].rearrange("(k p) c -> p k c", p=P)

    def product(src, pair, lhs, waits):
        t0, t1 = n.banks.take(), n.banks.take()
        for j in range(4):
            w = [n.weights(wblk(src, 2 * pair + a, j), 2048) for a in range(2)]
            for kk in range(2):
                k = 2 * j + kk
                for cc, (b, bank, bf) in enumerate((t0, t1)):
                    for a in range(2):
                        tok = n.pe(lambda e, bank=bank, a=a, cc=cc, k=k, kk=kk, w=w: e.matmul(
                            bank[a * 64:a * 64 + 64, :], lhs(k, a), w[a][0][:, kk * 1024 + cc * 512:kk * 1024 + cc * 512 + 512],
                            start=(k == 0), stop=(k == 7)), w[a][1], bf, waits(k, a), mark=(kk == 1 and cc == 1 and a == 1))
            for a in range(2):
                n.wslots.put(w[a][2], tok)
        return (t0[0], t0[1]), (t1[0], t1[1]), tok

    def down(i, hT, ti, tT2):
        y0, y1, tok = product(ins["exp_down"], i, lambda k, a: hT[:, k * P + a * 64:k * P + a * 64 + 64], lambda k, a: tT2)
        hidTs.put(ti, tok)
        ta = n.act(lambda e: e.activation(ys[i][:, 0:512], y0[1][:, :], ACT.Copy), tok, t_dispatched)
        tb = n.dve(lambda e: e.tensor_copy(ys[i][:, 512:1024], y1[1][:, :]), tok, t_dispatched)
        n.banks.put(y0[0], ta)
        n.banks.put(y1[0], tb)
        return [ta, tb]

    ty = []
    pend = None
    for i in range(8):
        lhs = lambda k, a, i=i: xg[:, k, (2 * i + a) * 64:(2 * i + a) * 64 + 64]
        w = lambda k, a, i=i: txg[k, i // 4]
        g0, g1, tg = product(ins["exp_gate"], i, lhs, w)
        hi, hid, hf = hids.take()
        ts = []
        for c, (b, bank) in enumerate((g0, g1)):
            t = n.act(lambda e, c=c, bank=bank, hid=hid: e.activation(hid[:, c * 512:(c + 1) * 512], bank[:, :], ACT.Silu), tg, hf)
            n.banks.put(b, t)
            ts.append(t)
        u0, u1, tu = product(ins["exp_up"], i, lhs, w)
        for c, (b, bank) in enumerate((u0, u1)):
            t = n.dve(lambda e, c=c, bank=bank, hid=hid: e.tensor_tensor(hid[:, c * 512:(c + 1) * 512],
                                                                       hid[:, c * 512:(c + 1) * 512], bank[:, :], ALU.mult), tu, ts[c])
            n.banks.put(b, t)
            ts[c] = t
        if pend is not None:
            ty.append(down(*pend))
        ti, hT, tf = hidTs.take()
        tt = []
        for c in range(2):
            b, bank, bf = n.banks.take()
            for j in range(4):
                tok = n.transpose(bank[:, j * P:(j + 1) * P], hid[:, c * 512 + j * P:c * 512 + (j + 1) * P], ts[c], bf, mark=(j == 3))
            if c:
                t = n.act(lambda e, c=c, bank=bank, hT=hT: e.activation(hT[:, c * 512:(c + 1) * 512], bank[:, :], ACT.Copy), tok, tf)
            else:
                t = n.dve(lambda e, c=c, bank=bank, hT=hT: e.tensor_copy(hT[:, c * 512:(c + 1) * 512], bank[:, :]), tok, tf)
            n.banks.put(b, t)
            tt.append(t)
        hids.put(hi, tok)
        pend = (i, hT, ti, tt)
    ty.append(down(*pend))
    nxt = Norm(n)
    for m in range(KT):
        b, bank, bf = n.banks.take()
        tok = n.group(bank[:, :], [(ys[i][:, m * P:(m + 1) * P], gv[i], [ty[i], tgv[i]]) for i in range(8)], bf)
        nxt.flush()
        t = n.dve(lambda e, m=m, bank=bank: e.tensor_tensor(n.h[m], bank[:, :], n.h[m], ALU.add), tok)
        n.banks.put(b, t)
        nxt.add(n.h[m], t)
        n.ht[m] = t
    n.top = mark
    return nxt


def second_block(n, norm):
    ins = n.ins
    xt = norm.finish("norm_mix_2", n.xn)
    spill = n.nc.dram_tensor("h_spill", (KT, P, S), F32, kind="Internal").ap()
    s = n.sem("s_spill")
    for k in range(KT):
        n.sp(lambda e, k=k: e.dma_start(spill[k], n.h[k]).then_inc(s, 16), xt, n.ht, mark=False)
    spilled = (s, 16 * KT)
    for q in (n.pe, n.act, n.dve, n.pool):
        q.wait(spilled)
    n.top = n.h_base
    yt = rwkv(n, xt)
    n.top = n.h_base + KT * 512 + 2048
    bar = n.barrier()
    n.ht = [n.load([(n.h[k], spill[k]) for k in range(KT)], bar, spilled)] * KT
    n.y_pool = [n.buf(512) for _ in range(4)]
    n.y_att = [n.buf(512) for _ in range(4)]
    top = n.top
    pt = pool_branch(n, xt)
    n.top = top
    at = axial_attention(n, xt)
    n.top = top
    norm = merge(n, xt, yt, pt, at)
    n.top = n.h_base + KT * 512
    n.barrier()
    norm = experts(n, norm)
    return norm


def program(nc, ins, out):
    with ExitStack() as ctx:
        n = make_net(nc, ctx, ins)
        norm = first_block(n)
        norm = second_block(n, norm)
        t = norm.finish("norm_final_2", n.xn)
        s = n.sem("s_out")
        for k in range(KT):
            n.sp(lambda e, k=k: e.dma_start(out[k], n.xn[k]).then_inc(s, 16), t[k], mark=False)
        n.sp.wait((s, 16 * KT))


def _cols(w, cols=None):
    if cols is not None:
        w = w[:, cols]
    k, m = w.shape
    return w.reshape(k // P, P, m // P, P).transpose(2, 1, 0, 3)


def _two(t):
    a, p, k, c = t.shape
    return np.ascontiguousarray(t.reshape(a // 2, 2, p, k, c).transpose(0, 2, 1, 3, 4)).reshape(a // 2, p, 2 * k * c)


def _wide(w):
    k, m = w.shape
    return np.ascontiguousarray(w.reshape(k // P, P, m).transpose(1, 0, 2)).reshape(P, -1)


def _head_cols(tiles):
    return np.concatenate([np.arange(h * 64, h * 64 + 64) for pair in tiles for h in pair])


def _constants():
    c = np.zeros((5, P, P), np.float32)
    c[0] = np.eye(P)
    c[1] = 1.0
    for a in range(2):
        c[2, a * 64:a * 64 + 64, a * 64:a * 64 + 64] = 1.0
        for i in range(32):
            c[3, a * 64 + i + 32, a * 64 + i] = -1.0
            c[3, a * 64 + i, a * 64 + i + 32] = 1.0
            c[4, a * 64 + 2 * i + 1, a * 64 + 2 * i] = -1.0
            c[4, a * 64 + 2 * i, a * 64 + 2 * i + 1] = 1.0
    f32 = np.float32
    inv = (10000.0 ** (-(np.arange(32) / 32))).astype(f32)
    ang = (np.arange(S, dtype=f32)[:, None] * inv[None, :]).astype(f32).astype(np.float64)
    rope1 = np.stack([np.tile(np.cos(ang).T, (4, 1)), np.tile(np.sin(ang).T, (4, 1))]).astype(f32)
    fr = (10000.0 ** (-(np.arange(0, 32, 2) / 32))).astype(f32)
    row = np.repeat(np.arange(8, dtype=f32), 64)
    col = np.tile(np.arange(64, dtype=f32), 8)
    ang = np.concatenate([row[:, None] * fr, col[:, None] * fr], axis=-1).astype(np.float64)
    rope2 = np.stack([np.tile(np.repeat(np.cos(ang).T, 2, axis=0), (2, 1)),
                      np.tile(np.repeat(np.sin(ang).T, 2, axis=0), (2, 1))]).astype(f32)
    i = np.arange(P)[:, None]
    j = np.arange(384)[None, :] - P
    mask_a = np.where(np.abs(i - j) <= 128, 0, NEG).astype(f32)
    mb1 = np.zeros((P, 4, S), f32)
    for r in range(4):
        mb1[:, r] = np.where(np.abs(4 * np.arange(P)[:, None] + r - np.arange(S)[None, :]) <= 64, 0, NEG)
    d = np.arange(P)[:, None] - np.arange(P)[None, :]
    mb23 = np.concatenate([np.where(np.abs(d) <= 64, 0, NEG), np.where(d % 4 == 0, 0, NEG)], 1).astype(f32)
    cq = np.arange(P) % 64
    cs = np.clip(cq - 8, 0, 48)[:, None]
    kc = np.arange(64)[None, :]
    win = np.where((kc >= cs) & (kc < cs + 16), 0, NEG).astype(f32)
    mask_c = np.tile(win, (1, 16))
    reset = np.ones((P, S), f32)
    reset[:, ::64] = 0
    t = np.arange(S)
    icnt = np.zeros((P, 4, S), f32)
    for g, w in enumerate((2, 4, 8, 16)):
        lo, hi = w // 2, w - w // 2 - 1
        icnt[:, g] = 1.0 / (np.clip(t + hi + 1, 0, S) - np.clip(t - lo, 0, S))
    a, b = np.arange(P)[:, None], np.arange(P)[None, :]
    mask_r = np.zeros((2, P, 448), f32)
    for d in range(2):
        head = a // 64 == b // 64
        strict = (a % 64 < b % 64) if d == 0 else (a % 64 > b % 64)
        block = (a % 64) // 16 == (b % 64) // 16
        mask_r[d, :, 0:128] = head & strict & block
        mask_r[d, :, 128:256] = head & strict & ~block
        mask_r[d, :, 256:384] = head & strict
        tt = np.arange(64)[None, :]
        mask_r[d, :, 384:448] = (a % 64 <= tt) if d == 0 else (a % 64 >= tt)
    sels = np.zeros((16, 8, P), f32)
    for e in range(16):
        sels[e, e // 2, (e % 2) * 64:(e % 2) * 64 + 64] = 1
    more = dict(reset=reset, icnt=icnt.reshape(P, -1), mask_r=mask_r, sels=sels.reshape(16, -1),
                iota=np.tile(np.arange(64, dtype=f32), (P, 1)), slotcol=(np.arange(P) % 64).astype(f32).reshape(P, 1))
    return dict(more, consts=c, rope1=rope1, rope2=rope2, mask_a=mask_a, mask_b1=mb1.reshape(P, -1), mask_b23=mb23,
                mask_c=mask_c)


def _layout(x):
    f = {k: np.asarray(v) for k, v in x.items()}
    a = dict(_constants())
    a["x"] = np.ascontiguousarray(f["x"][0].T).reshape(KT, P, S)
    a["p"] = np.ascontiguousarray(f["p"][:, 0].transpose(0, 2, 1)).reshape(2, 2, P, S)
    v = lambda z: z.reshape(-1, P).T
    dup = lambda z: np.concatenate([z, z]).reshape(P, 1)
    parts = [v(f["norm_ffn1"][0]), v(f["norm_ffn1"][1]), v(f["norm_mix"][0]), v(f["norm_mix"][1]),
             v(f["norm_ffn2"][0]), v(f["norm_ffn2"][1]), v(f["norm_ple"][0]), v(f["norm_ple"][1]),
             v(f["norm_final"]), v(f["norm_mix_2"][0]), v(f["norm_ffn_2"][0]), v(f["norm_final_2"]),
             v(f["shift_prev_2"][0]), v(f["shift_next_2"][0]), v(f["rwkv_w0_2"][0, 0]), v(f["rwkv_w0_2"][0, 1]),
             v(f["rwkv_a0_2"][0, 0]), v(f["rwkv_a0_2"][0, 1]), v(f["rwkv_k_k_2"][0]), v(f["rwkv_k_a_2"][0]),
             v(f["rwkv_r_k_2"][0]), v(f["rwkv_ln_w_2"][0]), v(f["rwkv_ln_b_2"][0]), v(f["pool_scale_2"][0]),
             dup(f["q_norm_2"][0]), dup(f["k_norm_2"][0])]
    a["vecs"] = np.ascontiguousarray(np.concatenate(parts, axis=1))
    a["sink_a"] = f["sink_a"].reshape(1, 12)
    gu, dn = [], []
    for layer in range(2):
        for s in ("ffn1", "ffn2"):
            g = _cols(f[f"{s}_w_gate"][layer])
            u = _cols(f[f"{s}_w_up"][layer])
            gu.append(np.stack([g, u], axis=2).reshape(FF, P, 2048))
            dn.append(_cols(f[f"{s}_w_down"][layer]).reshape(KT, P, FF * P))
    a["w_gu"] = np.stack(gu)
    a["w_dn"] = np.stack(dn)
    w = f["w_in_ab"][0]
    ha = _head_cols(A_TILES)
    qk = np.concatenate([ha, np.arange(768, 1024), np.arange(1280, 1280 + 1536)])
    a["w_ab_qk"] = _two(_cols(w, qk))
    a["w_ab_v"] = np.stack([_wide(w[:, 1024:1280])] + [_wide(w[:, 2816 + 256 * g:2816 + 256 * (g + 1)]) for g in range(3)])
    rows = np.concatenate([ha, np.arange(768, 1024)])
    a["w_ab_out"] = _two(_cols(f["w_out_ab"][0][rows]))
    w = f["w_in_c"][0]
    a["w_c_qk"] = _two(_cols(w[:, 0:2048]))
    a["w_c_v"] = np.stack([_wide(w[:, 2048 + 256 * g:2048 + 256 * (g + 1)]) for g in range(4)])
    a["w_c_out"] = _two(_cols(f["w_out_c"][0]))
    rpb = f["rpb_c"][0]
    t = np.zeros((16, P, 16, 64), rpb.dtype)
    for p in range(P):
        half, c = p // 64, p % 64
        lo, hi = max(0, c - 15), min(64, c + 16)
        t[:, p, half:half + 15, lo:hi] = rpb[:, :, lo - c + 15:hi - c + 15]
    a["rpb"] = t.reshape(16, P, 1024)
    a["w_ple"] = np.stack([np.concatenate([_cols(f["w_ple_gate"][i]), _cols(f["w_ple_proj"][i])], axis=2)
                           .reshape(KT, P, 1280) for i in range(2)])
    w = f["w_in_2"][0]
    a["w2_rwkv"] = _two(_cols(w[:, 0:1792]))
    a["w2_rwkv1"] = _cols(w[:, 1792:1920]).reshape(P, 1024)
    a["w2_pool"] = _two(_cols(w[:, 1920:2432]))
    hq = _head_cols(ATT_TILES)
    a["w2_att"] = _two(_cols(w[:, 2432:2944], hq))
    a["w2_att1"] = _cols(w[:, 2944:3072]).reshape(P, 1024)
    a["w2_attv"] = _wide(w[:, 3072:3200])
    gates = _cols(w[:, 3200:6272]).reshape(3, KT, P, KT, P)
    br = np.stack([_cols(f["w_branch_rwkv_2"][0]), _cols(f["w_branch_pool_2"][0]),
                   _cols(f["w_branch_attn_2"][0][hq])])
    a["w2_gate"] = np.concatenate([gates, br], axis=3).transpose(1, 0, 2, 3, 4).reshape(KT, 3, P, 1536)
    a["w2_out"] = _two(_cols(f["w_out_2"][0]))
    lora = np.zeros((2, P, 2, 512), f["rwkv_w2_2"].dtype)
    for z, name in enumerate(("rwkv_w2_2", "rwkv_a2_2")):
        for d in range(2):
            lora[d, d * 64:d * 64 + 64, z] = f[name][0, d]
    a["lora"] = lora.reshape(2, P, 1024)
    a["g2"] = f["rwkv_g2_2"][0]
    a["pool_w"] = np.ascontiguousarray(f["pool_w_2"][0].transpose(1, 0, 2)).reshape(P, 512)
    a["router"] = _wide(f["router_2"][0])
    for name in ("exp_gate", "exp_up", "exp_down"):
        a[name] = f[f"{name}_2"][0]
    return a


def kernel(**inputs):
    import concourse.bacc as _bacc
    from concourse import mybir as _mybir
    from concourse.bass_utils import run_bass_kernel_spmd as _run

    nc = _bacc.Bacc("TRN2", target_bir_lowering=False, num_devices=1)
    feed, ins = {}, {}
    for name, x in _layout(inputs).items():
        x = np.ascontiguousarray(x)
        feed[f"in_{name}"] = x
        ins[name] = nc.dram_tensor(f"in_{name}", x.shape, _mybir.dt.from_np(x.dtype), kind="ExternalInput").ap()
    out = nc.dram_tensor("out_0", (KT, P, S), _mybir.dt.float32, kind="ExternalOutput").ap()
    program(nc, ins, out)
    r = _run(nc, [feed], core_ids=[0])
    return np.ascontiguousarray(r.results[0]["out_0"].reshape(D, S).T).reshape(1, S, D)
```

```python
from contextlib import ExitStack

import numpy as np

import concourse.bass as bass
from concourse import mybir

F32 = mybir.dt.float32
F32R = mybir.dt.float32r
ALU = mybir.AluOpType
ACT = mybir.ActivationFunctionType
AX_X = mybir.AxisListType.X

P = 128
S = 512
D = 1024
KT = 8
FF = 22
EPS = 1e-6
NEG = -1e30
NSLOT = 2
SLOT = 2048

A_TILES = [(0, 3), (1, 4), (2, 5), (6, 9), (7, 10), (8, 11)]
ATT_TILES = [(0, 4), (1, 5), (2, 6), (3, 7)]

VEC = {}
_at = 0
for _name, _n in [("norm_ffn1_0", 8), ("norm_ffn1_1", 8), ("norm_mix_0", 8), ("norm_mix_1", 8),
                  ("norm_ffn2_0", 8), ("norm_ffn2_1", 8), ("norm_ple_0", 8), ("norm_ple_1", 8),
                  ("norm_final", 8), ("norm_mix_2", 8), ("norm_ffn_2", 8), ("norm_final_2", 8),
                  ("shift_prev", 15), ("shift_next", 15), ("w0_0", 4), ("w0_1", 4), ("a0_0", 4), ("a0_1", 4),
                  ("k_k", 4), ("k_a", 4), ("r_k", 4), ("ln_w", 4), ("ln_b", 4), ("pool_scale", 4),
                  ("q_norm", 1), ("k_norm", 1)]:
    VEC[_name] = _at
    _at += _n
NVEC = _at


class Queue:

    def __init__(self, eng, sem, skip_own=False):
        self.eng, self.sem, self.skip_own = eng, sem, skip_own
        self.count, self.seen, self.last = 0, {}, None

    def wait(self, *tokens):
        need = {}
        stack = list(tokens)
        while stack:
            w = stack.pop()
            if isinstance(w, list):
                stack.extend(w)
            elif w is not None and not (self.skip_own and w[0] is self.sem):
                if w[1] > max(self.seen.get(id(w[0]), 0), need.get(id(w[0]), (None, 0))[1]):
                    need[id(w[0])] = w
        for key, (s, v) in need.items():
            self.eng.wait_ge(s, v)
            self.seen[key] = v

    def __call__(self, fn, *waits, mark=True):
        self.wait(*waits)
        self.last = fn(self.eng)
        return self.sealed() if mark else self.now()

    def sealed(self):
        self.last.then_inc(self.sem, 1)
        self.count += 1
        return self.now()

    def now(self):
        return (self.sem, self.count)


class Pool:

    def __init__(self, items):
        self.items = list(items)
        self.ready = [(i, []) for i in range(len(self.items))]

    def take(self):
        i, toks = self.ready.pop(0)
        return i, self.items[i], toks

    def put(self, i, *toks):
        self.ready.append((i, list(toks)))


P_FLOATS = 5 * P + NVEC + 21 + 2 * 512 + 512 + NSLOT * SLOT
TOTAL = 52160


class Net:
    def __init__(self, nc, ctx, ins):
        self.nc, self.ctx, self.ins = nc, ctx, ins
        sem = lambda n: ctx.enter_context(nc.semaphore(n))
        self.sem = sem
        self.pe = Queue(nc.tensor, sem("s_pe"), skip_own=True)
        self.act = Queue(nc.scalar, sem("s_act"))
        self.dve = Queue(nc.vector, sem("s_dve"))
        self.pool = Queue(nc.gpsimd, sem("s_pool"))
        self.sp = Queue(nc.sync, sem("s_sp"))
        self.stack, self.names = [], 0
        self.open(P_FLOATS)
        self.banks = Pool([ctx.enter_context(nc.psum_tensor(f"bank{i}", [P, 512], F32)) for i in range(8)])
        self.nsem = 0
        self.order = weight_order(ins)
        self.fetched = self.split = self.used = 0
        self.wsem, self.wcount, self.where = [], [], {}
        self.wslots = Pool([])
        self.add_slots(NSLOT)
        self.parts = None

    def open(self, floats, dtype=F32):
        self.names += 1
        c = ExitStack()
        t = c.enter_context(self.nc.sbuf_tensor(f"mem{self.names}", [P, floats], dtype))
        self.stack.append((c, t, [0, floats]))
        return len(self.stack) - 1

    def close(self, level):
        while len(self.stack) > level:
            self.stack.pop()[0].close()
        return self.barrier()

    def buf(self, n, level=-1):
        _, t, at = self.stack[level]
        a = t[:, at[0]:at[0] + n]
        at[0] += n
        assert at[0] <= at[1], (at, n)
        return a

    @property
    def top(self):
        return self.stack[-1][2][0]

    @top.setter
    def top(self, v):
        self.stack[-1][2][0] = v

    def pair(self, level=-1, n=512):
        return (self.buf(n, level), self.buf(n, level))

    def add_slots(self, k):
        for _ in range(k):
            self.wslots.items.append(self.buf(SLOT))
            self.wslots.ready.append((len(self.wslots.items) - 1, []))
            self.wsem.append(self.sem(f"s_w{len(self.wsem)}"))
            self.wcount.append(0)

    def open_parts(self, k=2):
        level = self.open(k * 2 * SLOT, F32R)
        self.parts = Pool([(self.buf(SLOT), self.buf(SLOT)) for _ in range(k)])
        return level

    def fetch(self):
        while self.fetched < len(self.order) and self.wslots.ready:
            src, n, _ = self.order[self.fetched]
            i, ap, free = self.wslots.take()
            dst = ap[:, 0:n]
            if len(src.shape) == 3:
                dst = dst.rearrange("p (a b) -> p a b", a=src.shape[1])
            s = self.wsem[i]
            self.wcount[i] += 16
            self.sp(lambda e: e.dma_start(dst, src).then_inc(s, 16), free, mark=False)
            self.where[self.fetched] = (i, ap[:, 0:n], (s, self.wcount[i]))
            self.fetched += 1

    def split_to(self, last):
        while self.split <= last and self.split < len(self.order):
            if self.order[self.split][2]:
                if self.parts is None or not self.parts.ready or self.split not in self.where:
                    return
                i, ap, tok = self.where[self.split]
                n = ap.shape[-1]
                j, (hi, lo), free = self.parts.take()
                hi, lo = hi[:, 0:n], lo[:, 0:n]
                th, tl = self.rsplit(ap, (hi, lo), tok, free)
                self.wslots.put(i, th, tl)
                self.where[self.split] = (j, (hi, lo), [th, tl])
                self.fetch()
            self.split += 1

    def high(self, src, dst, *toks):
        return self.act(lambda e: e.activation(dst[0], src, ACT.Copy), *toks)

    def low(self, src, dst, *toks):
        return self.dve(lambda e: e.tensor_tensor(dst[1], src, dst[0].bitcast(F32), ALU.subtract), *toks)

    def rsplit(self, src, dst, *toks):
        th = self.high(src, dst, *toks)
        return th, self.low(src, dst, th, *toks)

    def weights(self, src, n):
        self.fetch()
        want = self.order[self.used]
        assert want[1] == n and want[0].shape == src.shape and want[0].offset == src.offset, (self.used, want, src)
        self.split_to(self.used + 1)
        assert self.split > self.used
        slot, ap, toks = self.where.pop(self.used)
        kind = want[2]
        self.used += 1
        return ap, toks, (kind, slot)

    def done(self, block, tok):
        kind, slot = block
        if kind:
            self.parts.put(slot, tok)
        else:
            self.wslots.put(slot, tok)
            self.fetch()

    def load(self, pairs, *waits):
        s = self.sem(f"s_ld{self.nsem}")
        self.nsem += 1
        for dst, src in pairs:
            self.sp(lambda e, dst=dst, src=src: e.dma_start(dst, src).then_inc(s, 16), *waits, mark=False)
        return (s, 16 * len(pairs))

    def barrier(self):
        toks = [q.now() for q in (self.pe, self.act, self.dve, self.pool)]
        for q in (self.pe, self.act, self.dve, self.pool):
            q.wait(toks)
        return toks

    def group(self, out, pairs, *waits):
        n = len(pairs)
        for j, pr in enumerate(pairs):
            lhsT, rhs = pr[0], pr[1]
            own = pr[2] if len(pr) > 2 else None
            tok = self.pe(lambda e, l=lhsT, r=rhs, j=j: e.matmul(out, l, r, start=(j == 0), stop=(j == n - 1)),
                          own, waits and list(waits), mark=(j == n - 1))
        return tok

    def group3(self, out, pairs, *waits):
        if not isinstance(pairs[0][0], tuple):
            return self.group(out, pairs, *waits)
        flat = []
        for pr in pairs:
            (lh, ll), (rh, rl) = pr[0], pr[1]
            own = pr[2] if len(pr) > 2 else None
            flat += [(lh, rh, own), (lh, rl, own), (ll, rh, own)]
        return self.group(out, flat, *waits)

    def transpose(self, out, src, *waits, mark=True):
        k = src.shape[0]
        return self.pe(lambda e: e.transpose(out, src, self.ident[0:k, 0:k]), *waits, mark=mark)


class Norm:

    def __init__(self, n):
        self.n, self.pend, self.k = n, [], 0
        self.b, self.bank, self.free = n.banks.take()

    def add(self, ap, tok):
        n = self.n
        i, sq, free = n.sq.take()
        t = n.act(lambda e: e.activation(sq, ap, ACT.Square), tok, free)
        self.pend.append((i, sq, t))

    def flush(self):
        n = self.n
        for i, sq, t in self.pend:
            k = self.k
            tok = n.pe(lambda e, k=k, sq=sq: e.matmul(self.bank[:, :], n.ones, sq, start=(k == 0), stop=(k == KT - 1)),
                       t, self.free)
            n.sq.put(i, tok)
            self.k += 1
            self.tok = tok
        self.pend = []

    def finish(self, gain, dst, *waits, split=True):
        n = self.n
        self.flush()
        assert self.k == KT
        r = n.rstd
        t = n.dve(lambda e: e.tensor_scalar(r, self.bank[:, :], 1.0 / D, EPS, ALU.mult, ALU.add), self.tok, n.rstd_free)
        n.banks.put(self.b, t)
        t = n.act(lambda e: e.activation(r, r, ACT.Sqrt), t)
        t = n.dve(lambda e: e.reciprocal(r, r), t)
        toks, last = [], None
        for k in range(KT):
            g = n.vec(gain, k)
            scale = lambda e, o: e.scalar_tensor_tensor(out=o, in0=n.h[k], scalar=g, in1=r, op0=ALU.mult, op1=ALU.mult)
            if not split:
                tx = n.dve(lambda e: scale(e, dst[k]), t, *waits)
                toks.append(tx)
                continue
            i, tmp, free = n.sq.take()
            tx = n.dve(lambda e: scale(e, tmp), t, free, *waits)
            th = n.high(tmp, dst[k], tx)
            if last:
                toks.append(self.low(*last))
            last = (i, tmp, dst[k], th)
        if split:
            toks.append(self.low(*last))
        n.rstd_free = tx
        return toks

    def low(self, i, tmp, dst, th):
        tl = self.n.low(tmp, dst, th)
        self.n.sq.put(i, th, tl)
        return [th, tl]


def make_net(nc, ctx, ins):
    n = Net(nc, ctx, ins)
    n.ident, n.ones, n.bones, n.rot1, n.rot2 = (n.buf(P) for _ in range(5))
    n.vecs = n.buf(NVEC)
    n.cc = n.buf(15 + 4 + 2)
    n.sq = Pool([n.buf(512) for _ in range(2)])
    n.rstd = n.buf(512)
    n.rstd_free = None
    n.open(KT * 512)
    n.h = [n.buf(512) for _ in range(KT)]
    n.open_parts()
    n.vec = lambda name, k=0: n.vecs[:, VEC[name] + k:VEC[name] + k + 1]
    n.base = len(n.stack)
    c = ins["consts"]
    n.t_const = n.load([(n.ident, c[0]), (n.ones, c[1]), (n.bones, c[2]), (n.rot1, c[3]), (n.rot2, c[4]),
                        (n.vecs, ins["vecs"])])
    n.fetch()
    for q in (n.pe, n.act, n.dve, n.pool):
        q.wait(n.t_const)
    return n


def open_xn(n):
    level = n.open(KT * 1024, F32R)
    n.xn = [n.pair() for _ in range(KT)]
    return level


def ffn(n, w_gu, w_dn, norm, gain):
    open_xn(n)
    n.open(FF * 1024, F32R)
    hid = [n.pair() for _ in range(FF)]
    n.open(2048)
    sgs = Pool([n.buf(512) for _ in range(4)])
    xt = norm.finish(gain, n.xn)
    ht = []
    for m in range(FF):
        w, wt, ws = n.weights(w_gu[m], 2048)
        w = views(w, "p (g k c) -> p g k c", g=2, k=KT)
        gb, g, gf = n.banks.take()
        ub, u, uf = n.banks.take()
        tg = n.group3(g[:, :], [(at(w, 0, k), n.xn[k], xt[k]) for k in range(KT)], wt, gf)
        tu = n.group3(u[:, :], [(at(w, 1, k), n.xn[k]) for k in range(KT)], uf)
        n.done(ws, tu)
        i, sg, sf = sgs.take()
        t = n.act(lambda e, sg=sg, g=g: e.activation(sg, g[:, :], ACT.Silu), tg, sf)
        n.banks.put(gb, t)
        t = n.dve(lambda e: e.tensor_tensor(sg, sg, u[:, :], ALU.mult), t, tu)
        n.banks.put(ub, t)
        th, tl = n.rsplit(sg, hid[m], t)
        sgs.put(i, th, tl)
        ht.append([th, tl])
    nxt = Norm(n)
    for m in range(KT):
        b, bank, bf = n.banks.take()
        for half in range(2):
            w, wt, ws = n.weights(w_dn[m, :, half * 1408:(half + 1) * 1408], 1408)
            w = views(w, "p (k c) -> p k c", k=11)
            for k in range(11):
                for z, (l, r) in enumerate(((0, 0), (0, 1), (1, 0))):
                    first, last = half == 0 and k == 0 and z == 0, half == 1 and k == 10 and z == 2
                    tok = n.pe(lambda e: e.matmul(bank[:, :], w[l][:, k, :], hid[half * 11 + k][r], start=first, stop=last),
                               bf, wt, ht[half * 11 + k], mark=(k == 10 and z == 2))
            n.done(ws, tok)
        nxt.flush()
        t = n.dve(lambda e, m=m, bank=bank: e.scalar_tensor_tensor(out=n.h[m], in0=bank[:, :], scalar=0.5, in1=n.h[m],
                                                                 op0=ALU.mult, op1=ALU.add), tok)
        n.banks.put(b, t)
        nxt.add(n.h[m], t)
        n.ht[m] = t
    n.close(n.base)
    return nxt


def each(f, w):
    return tuple(f(p) for p in w) if isinstance(w, tuple) else f(w)


def views(w, pattern, **sizes):
    return each(lambda p: p.rearrange(pattern, **sizes), w)


def at(w, *ix):
    return each(lambda p: p[:, ix[0], :] if len(ix) == 1 else p[:, ix[0], ix[1], :], w)


def cols(w, c):
    return each(lambda p: p[:, c], w)


def out_proj(n, wsrc, rhs, toks):
    nxt = Norm(n)
    for m2 in range(4):
        w, wt, ws = n.weights(wsrc[m2], 2048)
        w = views(w, "p (a k c) -> p a k c", a=2, k=KT)
        for a in range(2):
            m = 2 * m2 + a
            b, bank, bf = n.banks.take()
            tok = n.group3(bank[:, :], [(at(w, a, k), rhs[k], toks[k]) for k in range(KT)], wt, bf)
            nxt.flush()
            t = n.dve(lambda e, m=m, bank=bank: e.tensor_tensor(n.h[m], bank[:, :], n.h[m], ALU.add), tok)
            n.banks.put(b, t)
            nxt.add(n.h[m], t)
            n.ht[m] = t
        n.done(ws, tok)
    return nxt


def rope(n, raw, rawt, rot, cos, sin, tmps, dst, *waits):
    b, bank, bf = n.banks.take()
    tr = n.group(bank[:, :], [(rot, raw)], rawt, bf)
    i, tmp, tf = tmps.take()
    t1 = n.pool(lambda e: e.tensor_tensor(dst, raw, cos, ALU.mult), rawt, *waits)
    t2 = n.dve(lambda e: e.tensor_tensor(tmp, bank[:, :], sin, ALU.mult), tr, tf, *waits)
    n.banks.put(b, t2)
    t = n.dve(lambda e: e.tensor_tensor(dst, dst, tmp, ALU.add), t1, t2)
    tmps.put(i, t)
    return t, [tr, t1]


def heads_fm(n, blocks, xt, use):
    m = 0
    for src, cnt in blocks:
        w, wt, ws = n.weights(src, cnt * 1024)
        w = views(w, "p (a k c) -> p a k c", a=cnt, k=KT)
        for a in range(cnt):
            b, bank, bf = n.banks.take()
            tok = n.group3(bank[:, :], [(at(w, a, k), n.xn[k], xt[k]) for k in range(KT)], wt, bf)
            n.banks.put(b, use(m, bank, tok))
            m += 1
        n.done(ws, tok)


def values_tm(n, src, cols, xt, sel, dst):
    w, wt, ws = n.weights(src, KT * cols)
    w = views(w, "p (k c) -> p k c", k=KT)
    toks = []
    for i in range(4):
        b, bank, bf = n.banks.take()
        tok = n.group3(bank[:, 0:cols], [(each(lambda x: sel(x, i), n.xn[k]), at(w, k), xt[k]) for k in range(KT)], wt, bf)
        t = n.act(lambda e, i=i, bank=bank: e.activation(dst(i), bank[:, 0:cols], ACT.Copy), tok)
        n.banks.put(b, t)
        toks.append(t)
    n.done(ws, tok)
    return toks


ATT_FLOATS = lambda width, queries=1: 6 * width + 80 + 3 * P + 2 * PADS * queries * P
PADS = 2


class Attention:

    def __init__(self, n, width, queries=1):
        self.n = n
        self.sc = Pool([n.buf(width) for _ in range(4)])
        self.pt = Pool([n.buf(width) for _ in range(2)])
        self.st = Pool([n.buf(8) for _ in range(10)])
        self.ot = Pool([n.buf(P) for _ in range(3)])
        self.toks = []
        pads = [[n.buf(queries * P) for _ in range(PADS)] for _ in range(2)]
        for x in pads[0] + pads[1]:
            tz = n.pool(lambda e: e.memset(x, 0.0))
        self.pads = [Pool(x) for x in pads]
        n.pool.wait(tz)

    def run(self, units):
        steps = [self.padded, self.scores, self.biased, self.exps, self.scaled, self.turned, self.copied, self.values, self.stored, self.flipped,
                 self.written]
        units = [dict(u) for u in units]
        for t in range(len(units) + len(steps) - 1):
            for s in range(len(steps) - 1, -1, -1):
                if 0 <= t - s < len(units):
                    steps[s](units[t - s])

    def padded(self, u):
        n = self.n
        i, pad, free = self.pads[u["par"]].take()
        ps = slice(u["par"] * 64, u["par"] * 64 + 64)
        u["pad"] = (i, pad)
        for j, q in enumerate(u["q"]):
            t = n.pool(lambda e: e.tensor_copy(pad[ps, j * P:(j + 1) * P], q), u["waits"], free, n.pool.now())
        u["tq"] = t

    def scores(self, u):
        n = self.n
        u["sb"] = []
        if "before" in u:
            u["before"]()
        i, pad = u["pad"]
        j = 0
        for part in u["keys"]:
            b, bank, bf = n.banks.take()
            off = 0
            for kap in part:
                w = kap.shape[-1]
                q = pad[:, j * P:(j + 1) * P]
                tok = n.pe(lambda e: e.matmul(bank[:, off:off + w], q, kap, start=True, stop=True), bf, u["waits"], u["tq"])
                off += w
                j += 1
            u["sb"].append((b, bank, off, tok))
        self.pads[u["par"]].put(i, tok)

    def biased(self, u):
        n = self.n
        u["sci"], sc, scf = self.sc.take()
        u["sti"], st, stf = self.st.take()
        u["sc"], u["st"] = sc, st
        off = 0
        u["first"] = []
        for j, (b, bank, w, tok) in enumerate(u["sb"]):
            o = sc[:, off:off + w]
            m = st[:, j:j + 1]
            if u["mask"] is None:
                t = n.dve(lambda e: e.tensor_reduce(m, bank[:, 0:w], AX_X, ALU.max), tok, scf, stf)
                u["raw"] = (b, bank, t)
            else:
                init = u["sink"] if j == 0 and u["sink"] is not None else (st[:, j - 1:j] if j else -3e38)
                prev = u["first"][-1] if j else None
                t = n.dve(lambda e, o=o, bank=bank, w=w, m=m, j=j, init=init: e.tensor_tensor_reduce(
                    o, bank[:, 0:w], u["mask"][j], 1.0, init, ALU.add, ALU.max, m), tok, scf, stf, prev, u["waits"])
                n.banks.put(b, t)
            u["first"].append(t)
            off += w
        u["w"] = off
        j = len(u["sb"]) - 1
        u["t"] = n.dve(lambda e: e.tensor_scalar(st[:, 2:3], st[:, j:j + 1], -1.0, None, ALU.mult), u["first"])

    def exps(self, u):
        n = self.n
        sc, st, w = u["sc"], u["st"], u["w"]
        src = sc[:, 0:w] if u["mask"] is not None else u["raw"][1][:, 0:w]
        u["te"] = n.act(lambda e: e.activation(sc[:, 0:w], src, ACT.Exp, bias=st[:, 2:3], accum_out=st[:, 3:4]),
                        u["t"])
        if u["mask"] is None:
            n.banks.put(u["raw"][0], u["te"])
        if u["sink"] is not None:
            u["ts"] = n.act(lambda e: e.activation(st[:, 5:6], u["sink"], ACT.Exp, bias=st[:, 2:3]), u["t"])

    def scaled(self, u):
        n = self.n
        st = u["st"]
        t = u["te"]
        if u["sink"] is not None:
            t = n.dve(lambda e: e.tensor_tensor(st[:, 3:4], st[:, 3:4], st[:, 5:6], ALU.add), t, u["ts"])
        u["tr"] = n.dve(lambda e: e.reciprocal(st[:, 4:5], st[:, 3:4]), t)

    def turned(self, u):
        n = self.n
        sc = u["sc"]
        nb = u["w"] // P
        u["tb"] = []
        for g in range(0, nb, 4):
            b, bank, bf = n.banks.take()
            c = min(4, nb - g)
            for j in range(c):
                tok = n.transpose(bank[:, j * P:(j + 1) * P], sc[:, (g + j) * P:(g + j + 1) * P], u["te"], bf,
                                  mark=(j == c - 1))
            u["tb"].append((b, bank, c, tok))
        self.sc.put(u["sci"], tok)

    def copied(self, u):
        n = self.n
        u["pti"], pt, pf = self.pt.take()
        u["pt"] = pt
        off = 0
        u["tc"] = []
        for b, bank, c, tok in u["tb"]:
            w = c * P
            t = n.act(lambda e, off=off, w=w, bank=bank: e.activation(pt[:, off:off + w], bank[:, 0:w], ACT.Copy),
                      tok, pf)
            n.banks.put(b, t)
            u["tc"].append(t)
            off += w

    def values(self, u):
        n = self.n
        b, bank, bf = n.banks.take()
        o = bank[:, 0:64]
        tok = n.group(o, [(u["pt"][:, j * P:(j + 1) * P], v) for j, v in enumerate(u["v"])], bf, u["tc"], u["waits"])
        self.pt.put(u["pti"], tok)
        u["pv"] = (b, o, tok)

    def stored(self, u):
        n = self.n
        b, o, tok = u["pv"]
        if u["par"] == 0:
            self.open_tile = self.ot.take()
            self.first_half = None
        i, ot, free = self.open_tile
        u["ot"] = (i, ot)
        t = n.dve(lambda e: e.tensor_scalar(ot[:, u["par"] * 64:u["par"] * 64 + 64], o, u["st"][:, 4:5], None, ALU.mult),
                  tok, u["tr"], free)
        n.banks.put(b, t)
        self.st.put(u["sti"], t)
        u["th"] = [t, self.first_half]
        self.first_half = t

    def flipped(self, u):
        if u["par"] == 0:
            return
        n = self.n
        i, ot = u["ot"]
        b, bank, bf = n.banks.take()
        tok = n.transpose(bank[:, 0:P], ot, u["th"], bf)
        self.ot.put(i, tok)
        u["fl"] = (b, bank, tok)

    def written(self, u):
        if u["par"] == 0:
            return
        n = self.n
        b, bank, tok = u["fl"]
        if isinstance(u["out"], tuple):
            t = list(n.rsplit(bank[:, 0:P], u["out"], tok))
        else:
            t = [n.act(lambda e: e.activation(u["out"], bank[:, 0:P], ACT.Copy), tok)]
        n.banks.put(b, t)
        self.toks += t


def ab_mixer(n, norm):
    ins = n.ins
    n.open(14336)
    qa = [n.buf(512) for _ in range(6)]
    ka = [n.buf(512) for _ in range(2)]
    va = n.buf(1024).rearrange("p (i c) -> p i c", i=4)
    qb = [n.buf(512) for _ in range(6)]
    kb = [n.buf(512) for _ in range(6)]
    vb = n.buf(3072).rearrange("p (g i c) -> p g i c", g=3, i=4)
    inner = open_xn(n)
    n.open(5 * 512)
    cos, sin = n.buf(512), n.buf(512)
    raws = Pool([n.buf(512) for _ in range(2)])
    tmps = Pool([n.buf(512) for _ in range(1)])
    bar = n.barrier()
    tl = n.load([(cos, ins["rope1"][0]), (sin, ins["rope1"][1])], bar)
    xt = norm.finish("norm_mix_0", n.xn)
    dsts = qa + ka + qb + kb
    rt = {}

    def use(m, bank, tok):
        i, raw, rf = raws.take()
        scale = 0.125 if m < 6 or 8 <= m < 14 else 1.0
        t = n.act(lambda e: e.activation(raw, bank[:, :], ACT.Copy, scale=scale), tok, rf)
        done, reads = rope(n, raw, t, n.rot1, cos, sin, tmps, dsts[m], tl)
        raws.put(i, done, *reads)
        rt[m] = done
        return t

    heads_fm(n, [(ins["w_ab_qk"][j], 2) for j in range(10)], xt, use)
    tv = values_tm(n, ins["w_ab_v"][0], 256, xt, lambda x, i: x[:, i * P:(i + 1) * P], lambda i: va[:, i, :])
    tvb = []
    for g in range(3):
        if g == 0:
            sel = lambda x, i: x[:, i * P:(i + 1) * P]
        else:
            sel = lambda x, i: x.rearrange("p (m r) -> p r m", r=4)[:, i, :]
        tvb += values_tm(n, ins["w_ab_v"][1 + g], 256, xt, sel, lambda i, g=g: vb[:, g, i, :])
    bar = n.close(inner)
    n.open(8192, F32R)
    o = [n.pair() for _ in range(8)]
    n.open(384 + 2048 + 256 + 12 + ATT_FLOATS(768, 3))
    ma = n.buf(384)
    mb1 = n.buf(2048)
    mb23 = n.buf(256)
    sink = n.buf(12)
    tl = n.load([(ma, ins["mask_a"]), (mb1, ins["mask_b1"]), (mb23, ins["mask_b23"]),
                 (sink, ins["sink_a"].to_broadcast([P, 12]))], bar)
    n.att = Attention(n, 768, 3)
    units = []
    for t, pair in enumerate(A_TILES):
        for i in range(4):
            for par, h in enumerate(pair):
                g = h // 3
                ps = slice(par * 64, par * 64 + 64)
                lo, hi = max(0, i - 1), min(4, i + 2)
                ms = P * (lo - i + 1)
                units.append(dict(q=[qa[t][ps, i * P:(i + 1) * P]], keys=[[ka[g // 2][:, lo * P:hi * P]]],
                                  mask=[ma[:, ms:ms + (hi - lo) * P]], sink=sink[:, h:h + 1], par=par,
                                  v=[va[:, j, g * 64:g * 64 + 64] for j in range(lo, hi)],
                                  out=cols(o[t], slice(i * P, (i + 1) * P)), waits=[rt[t], rt[6 + g // 2], tl] + tv))
    cls = lambda ap: ap.rearrange("p (m r) -> p r m", r=4)
    for s2 in range(2):
        for r, par in [(r, par) for r in range(4) for par in range(2)]:
            s = 2 * s2 + par
            ps = slice(par * 64, par * 64 + 64)
            t = [(g * 4 + s) // 2 for g in range(3)]
            units.append(dict(
                q=[cls(qb[t[g]][ps, :])[:, r, :] for g in range(3)],
                keys=[[kb[t[0]]], [cls(kb[t[1]])[:, r, :], cls(kb[t[2]])[:, r, :]]],
                mask=[mb1[:, r * 512:(r + 1) * 512], mb23], sink=None, par=par,
                v=[vb[:, 0, j, s * 64:s * 64 + 64] for j in range(4)] + [vb[:, g, r, s * 64:s * 64 + 64] for g in (1, 2)],
                out=tuple(cls(x)[:, r, :] for x in o[6 + s // 2]),
                waits=[rt[8 + x] for x in t] + [rt[14 + x] for x in t] + [tl] + tvb))
    n.att.run(units)
    nxt = out_proj(n, ins["w_ab_out"], o, [n.att.toks] * 8)
    n.close(n.base)
    return nxt


def c_mixer(n, norm):
    ins = n.ins
    n.open(12288)
    q = [n.buf(512) for _ in range(8)]
    k = [n.buf(512) for _ in range(8)]
    v = n.buf(4096).rearrange("p (i c) -> p i c", i=4)
    inner = open_xn(n)
    n.barrier()
    xt = norm.finish("norm_mix_1", n.xn)
    dsts = q + k
    rt = {}

    def use(m, bank, tok):
        rt[m] = n.act(lambda e: e.activation(dsts[m], bank[:, :], ACT.Copy, scale=0.125 if m < 8 else 1.0), tok)
        return rt[m]

    heads_fm(n, [(ins["w_c_qk"][j], 2) for j in range(8)], xt, use)
    tv = []
    for g in range(4):
        tv.append(values_tm(n, ins["w_c_v"][g], 256, xt, lambda x, i: x[:, i * P:(i + 1) * P],
                            lambda i, g=g: v[:, i, g * 256:(g + 1) * 256]))
    bar = n.close(inner)
    n.open(8192, F32R)
    o = [n.pair() for _ in range(8)]
    n.open(1024 + 4096 + ATT_FLOATS(512))
    cm = n.buf(1024)
    bias = Pool([n.buf(1024) for _ in range(4)])
    tl = n.load([(cm, ins["mask_c"])], bar)
    att = Attention(n, 512)
    units = []
    bsem = n.sem("s_bias")
    bcount = [0]
    for t in range(8):
        for i, par in [(i, par) for i in range(4) for par in range(2)]:
            h = 2 * t + par
            ps = slice(par * 64, par * 64 + 64)
            u = dict(q=[q[t][ps, i * P:(i + 1) * P]], keys=[[k[t]]], sink=None, par=par,
                     v=[v[:, j, h * 64:h * 64 + 64] for j in range(4)], out=cols(o[t], slice(i * P, (i + 1) * P)),
                     mask=[None], waits=[rt[t], rt[8 + t]] + tv[h // 4], hi=(h, i))
            units.append(u)
    real = att.biased
    real_scores = att.scores
    cur = {}

    def fetch(h):
        i, ap, free = bias.take()
        bcount[0] += 16
        want = bcount[0]
        n.sp(lambda e: e.dma_start(ap, ins["rpb"][h]).then_inc(bsem, 16), free, cur.get("last"), bar, mark=False)
        t = n.pool(lambda e: e.tensor_tensor(ap, ap, cm, ALU.add), (bsem, want), tl, n.pool.now())
        cur["last"] = t
        cur[h] = (i, ap, t)

    def scores(u):
        h, i = u["hi"]
        if i == 0 and h < 2:
            fetch(h)
        if i == 1 and h + 2 < 16:
            fetch(h + 2)
        real_scores(u)

    def biased(u):
        h, i = u["hi"]
        bi, ap, t = cur[h]
        u["mask"] = [ap[:, (7 - 2 * i) * 64:(15 - 2 * i) * 64]]
        u["waits"] = u["waits"] + [t]
        real(u)
        if i == 3:
            bias.put(bi, u["t"])

    att.scores, att.biased = scores, biased
    att.run(units)
    nxt = out_proj(n, ins["w_c_out"], o, [att.toks] * 8)
    n.close(n.base)
    return nxt


def ple(n, layer, norm):
    ins = n.ins
    open_xn(n)
    n.open(2048, F32R)
    pp = [n.pair() for _ in range(2)]
    n.open(2048)
    p = [n.buf(512) for _ in range(2)]
    sgs = Pool([n.buf(512) for _ in range(2)])
    tl = n.load([(p[j], ins["p"][layer, j]) for j in range(2)], n.barrier())
    tp = [n.rsplit(p[j], pp[j], tl) for j in range(2)]
    tl = [list(x) for x in tp]
    xt = norm.finish(f"norm_ple_{layer}", n.xn)
    nxt = Norm(n)
    for m in range(KT):
        w, wt, ws = n.weights(ins["w_ple"][layer, m], 1280)
        w = views(w, "p (k c) -> p k c", k=10)
        gb, g, gf = n.banks.take()
        ub, u, uf = n.banks.take()
        tg = n.group3(g[:, :], [(at(w, k), n.xn[k], xt[k]) for k in range(KT)], wt, gf)
        tu = n.group3(u[:, :], [(at(w, KT + k), pp[k]) for k in range(2)], uf, tl)
        n.done(ws, tu)
        nxt.flush()
        i, sg, sf = sgs.take()
        t = n.act(lambda e, sg=sg, g=g: e.activation(sg, g[:, :], ACT.Sigmoid), tg, sf)
        n.banks.put(gb, t)
        t = n.dve(lambda e, sg=sg, u=u: e.tensor_tensor(sg, sg, u[:, :], ALU.mult), t, tu)
        n.banks.put(ub, t)
        t = n.dve(lambda e, sg=sg, m=m: e.tensor_tensor(n.h[m], n.h[m], sg, ALU.add), t)
        sgs.put(i, t)
        nxt.add(n.h[m], t)
        n.ht[m] = t
    n.close(n.base)
    return nxt


def first_block(n):
    ins = n.ins
    tx = n.load([(n.h[k], ins["x"][k]) for k in range(KT)])
    norm = Norm(n)
    n.ht = [tx] * KT
    for k in range(KT):
        norm.add(n.h[k], tx)
        norm.flush()
    n.split_to(1)
    for layer in range(2):
        norm = ffn(n, ins["w_gu"][2 * layer], ins["w_dn"][2 * layer], norm, f"norm_ffn1_{layer}")
        norm = (ab_mixer if layer == 0 else c_mixer)(n, norm)
        norm = ffn(n, ins["w_gu"][2 * layer + 1], ins["w_dn"][2 * layer + 1], norm, f"norm_ffn2_{layer}")
        norm = ple(n, layer, norm)
    n.ht = norm.finish("norm_final", n.h, split=False)
    norm = Norm(n)
    for k in range(KT):
        norm.add(n.h[k], n.ht[k])
        norm.flush()
    return norm


def shift_tokens(n, raw, c0, mp, mn, dst, tok, free):
    x, p, q = raw[:, 1:513], raw[:, 0:512], raw[:, 2:514]
    t = n.dve(lambda e: e.tensor_scalar(dst, x, c0, None, ALU.mult), tok, free)
    t = n.dve(lambda e: e.scalar_tensor_tensor(out=dst, in0=p, scalar=mp, in1=dst, op0=ALU.mult, op1=ALU.add), t)
    t = n.dve(lambda e: e.scalar_tensor_tensor(out=dst, in0=q, scalar=mn, in1=dst, op0=ALU.mult, op1=ALU.add), t)
    return t


def rwkv(n, xt):
    ins = n.ins
    v4 = lambda b: b.rearrange("p (a t) -> p a t", a=4)
    R, K = n.buf(2048), n.buf(2048)
    Y = n.y_rwkv
    V, KK, BON = (n.buf(2048) for _ in range(3))
    lora = [n.buf(512) for _ in range(3)]
    reset = n.buf(512)
    masks = n.buf(448)
    ptc = v4(n.buf(32))
    state = n.buf(512)
    AL, RT, BT, KTL = (n.buf(2048) for _ in range(4))
    work = n.top
    raws = Pool([n.buf(514) for _ in range(2)])
    bar = n.barrier()
    tl = n.load([(reset, ins["reset"])], bar)
    mp, mn, c0 = n.vec("shift_prev"), n.vec("shift_next"), n.cc[:, 0:15]
    omka = n.cc[:, 15:19]
    vv = lambda name, k: n.vecs[:, VEC[name]:VEC[name] + k]
    t = n.dve(lambda e: e.tensor_tensor(c0, vv("shift_prev", 15), vv("shift_next", 15), ALU.add))
    t = n.dve(lambda e: e.tensor_scalar(c0, c0, -1.0, 1.0, ALU.mult, ALU.add), t)
    tc = n.dve(lambda e: e.tensor_scalar(omka, vv("k_a", 4), -1.0, 1.0, ALU.mult, ALU.add), t)
    tz = []
    for r in raws.items:
        n.pool(lambda e, r=r: e.memset(r[:, 0:1], 0.0))
        tz = n.pool(lambda e, r=r: e.memset(r[:, 513:514], 0.0))
    dsts = [b[:, j * 512:(j + 1) * 512] for b in (R, K, V) for j in range(4)] + lora
    done = {}

    def use(m, bank, tok):
        i, raw, rf = raws.take()
        t = n.act(lambda e: e.activation(raw[:, 1:513], bank[:, :], ACT.Copy), tok, rf)
        done[m] = shift_tokens(n, raw, n.cc[:, m:m + 1], n.vec("shift_prev", m), n.vec("shift_next", m), dsts[m],
                               [t, tz, tc], None)
        raws.put(i, done[m])
        return t

    heads_fm(n, [(ins["w2_rwkv"][j], 2) for j in range(7)] + [(ins["w2_rwkv1"], 1)], xt, use)
    t_wd = n.act(lambda e: e.activation(lora[0], lora[0], ACT.Tanh), done[12])
    t_gd = n.act(lambda e: e.activation(lora[2], lora[2], ACT.Sigmoid), done[14])
    ct = lambda b: b.rearrange("p (c t) -> p c t", t=64)
    col = lambda b, j: b[:, j * 512:(j + 1) * 512]
    T = range(4)
    kk_t = []
    for d in range(2):
        n.top = work
        lw, av, C, X, P1, IP = ([n.buf(512) for _ in T] for _ in range(6))
        bar = n.barrier()
        tm = n.load([(masks, ins["mask_r"][d])], bar)
        w, wt, ws = n.weights(ins["lora"][d], 1024)
        low = []
        for z in range(2):
            for j in T:
                b, bank, bf = n.banks.take()
                c = slice(z * 512 + j * 128, z * 512 + (j + 1) * 128)
                low.append((b, bank, n.group(bank[:, :], [(w[:, c], lora[z])], wt, t_wd, bf)))
        n.done(ws, low[7][2])
        ts, ta = [], []
        for z, (dst, toks, bias) in enumerate(((lw, ts, f"w0_{d}"), (av, ta, f"a0_{d}"))):
            for j in T:
                b, bank, tok = low[4 * z + j]
                toks.append(n.act(lambda e: e.activation(dst[j], bank[:, :], ACT.Sigmoid, bias=n.vec(bias, j)), tok))
                n.banks.put(b, toks[j])
        if d == 0:
            tk = [n.dve(lambda e: e.tensor_scalar(col(KK, j), col(K, j), n.vec("k_k", j), None, ALU.mult)) for j in T]
            sq = [col(BON, j) for j in T]
            tq = [n.act(lambda e: e.activation(sq[j], col(KK, j), ACT.Square), tk[j]) for j in T]
            tr = []
            for j in T:
                b, bank, bf = n.banks.take()
                tok = n.group(bank[:, :], [(n.bones, sq[j])], tq[j], bf)
                tr.append(n.act(lambda e: e.activation(sq[j], bank[:, :], ACT.Sqrt), tok))
                n.banks.put(b, tr[j])
        tlw = [n.dve(lambda e: e.tensor_scalar(lw[j], lw[j], -float(np.exp(-0.5)), None, ALU.mult), ts[j]) for j in T]
        tC = [n.dve(lambda e: e.tensor_tensor_scan(C[j], reset, lw[j], 0.0, ALU.mult, ALU.add), tlw[j], tl) for j in T]
        if d == 0:
            tX = [n.dve(lambda e: e.tensor_tensor(X[j], C[j], lw[j], ALU.subtract), tC[j]) for j in T]
            ti = tC
        else:
            tX = [n.dve(lambda e: e.tensor_tensor(ct(X[j]), ct(C[j])[:, :, 63:64].to_broadcast([P, 8, 64]), ct(C[j]),
                                                  ALU.subtract), tC[j]) for j in T]
            ti = [n.dve(lambda e: e.tensor_tensor(C[j], X[j], lw[j], ALU.add), tX[j]) for j in T]
        end = 63 if d == 0 else 0
        tP, tPe, tIP, t3 = [], [], [], []
        for j in T:
            tP.append(n.act(lambda e: e.activation(P1[j], C[j], ACT.Exp), ti[j]))
            tPe.append(n.act(lambda e: e.activation(X[j], X[j], ACT.Exp), tX[j], ti[j]))
            tIP.append(n.act(lambda e: e.activation(IP[j], C[j], ACT.Exp, scale=-1.0), ti[j]))
        if d == 0:
            tr = [n.dve(lambda e: e.tensor_scalar(sq[j], sq[j], 1e-12, None, ALU.max), tr[j]) for j in T]
            tr = [n.dve(lambda e: e.reciprocal(sq[j], sq[j]), tr[j]) for j in T]
            kk_t = [n.dve(lambda e: e.tensor_tensor(col(KK, j), col(KK, j), sq[j], ALU.mult), tr[j]) for j in T]
        for j in T:
            n.pool(lambda e: e.tensor_copy(ptc[:, j, :], ct(P1[j])[:, :, end]), tP[j])
            n.dve(lambda e: e.tensor_tensor(col(RT, j), col(R, j), P1[j], ALU.mult), tP[j])
        t4 = [n.dve(lambda e: e.tensor_tensor(lw[j], col(KK, j), av[j], ALU.mult), ta[j], ti[j], tX[j], kk_t) for j in T]
        for j in T:
            n.dve(lambda e: e.scalar_tensor_tensor(out=col(AL, j), in0=col(KK, j), scalar=-1.0, in1=X[j], op0=ALU.mult,
                                                   op1=ALU.mult), tPe[j])
            n.pool(lambda e: e.tensor_tensor(col(BT, j), lw[j], IP[j], ALU.mult), t4[j], tIP[j])
        t5 = [n.dve(lambda e: e.tensor_scalar(av[j], av[j], n.vec("k_a", j), n.cc[:, 15 + j:16 + j], ALU.mult, ALU.add),
                    t4[j], tc) for j in T]
        key = av if d else [col(BON, j) for j in T]
        t5 = [n.dve(lambda e: e.tensor_tensor(key[j], av[j], col(K, j), ALU.mult), t5[j], kk_t) for j in T]
        for j in T:
            n.dve(lambda e: e.tensor_tensor(col(KTL, j), key[j], IP[j], ALU.mult), t5[j], tIP[j])
            if d:
                n.pool(lambda e: e.tensor_tensor(col(BON, j), col(BON, j), av[j], ALU.add), t5[j])
        n.top = work
        chunks(n, d, dict(R=R, V=V, AL=AL, RT=RT, BT=BT, KT=KTL, Y=Y, masks=masks, ptc=ptc, state=state, tm=tm))
    n.top = work
    bar = n.barrier()
    mu, yc, sq, bo = ([n.buf(512) for _ in T] for _ in range(4))
    gw, gwt, gs = n.weights(ins["g2"], 512)

    def sums(src, toks):
        r = []
        for j in T:
            b, bank, bf = n.banks.take()
            r.append((b, bank, n.group(bank[:, :], [(n.bones, src[j])], toks[j], bf)))
        return r

    def read(out, fn, *toks):
        b, bank, tok = out
        t = n.dve(lambda e: fn(e, bank[:, :]), tok, *toks)
        n.banks.put(b, t)
        return t

    Ys = [col(Y, j) for j in T]
    s1 = sums(Ys, [None] * 4)
    tb = [n.dve(lambda e: e.scalar_tensor_tensor(out=bo[j], in0=col(BON, j), scalar=n.vec("r_k", j), in1=col(R, j),
                                                 op0=ALU.mult, op1=ALU.mult)) for j in T]
    s2 = sums(bo, tb)
    ty = [read(s1[j], lambda e, x: e.scalar_tensor_tensor(out=yc[j], in0=x, scalar=-1.0 / 64, in1=Ys[j], op0=ALU.mult,
                                                          op1=ALU.add)) for j in T]
    t = [n.act(lambda e: e.activation(sq[j], yc[j], ACT.Square), ty[j]) for j in T]
    s3 = sums(sq, t)
    tb = [read(s2[j], lambda e, x: e.tensor_tensor(bo[j], x, col(V, j), ALU.mult)) for j in T]
    t = [read(s3[j], lambda e, x: e.tensor_scalar(mu[j], x, 1.0 / 64, 64e-5, ALU.mult, ALU.add)) for j in T]
    s4 = []
    for j in T:
        b, bank, bf = n.banks.take()
        s4.append((b, bank, n.group(bank[:, :], [(gw[:, j * 128:(j + 1) * 128], lora[2])], gwt, t_gd, bf)))
    n.done(gs, s4[3][2])
    t = [n.act(lambda e: e.activation(mu[j], mu[j], ACT.Sqrt), t[j]) for j in T]
    yt = []
    for j in T:
        tm = n.dve(lambda e: e.reciprocal(mu[j], mu[j]), t[j])
        tm = n.dve(lambda e: e.tensor_tensor(yc[j], yc[j], mu[j], ALU.mult), tm, ty[j])
        tm = n.pool(lambda e: e.tensor_scalar(yc[j], yc[j], n.vec("ln_w", j), n.vec("ln_b", j), ALU.mult, ALU.add), tm)
        tm = n.pool(lambda e: e.tensor_tensor(yc[j], yc[j], bo[j], ALU.add), tm, tb[j])
        yt.append(tm)
    return [read(s4[j], lambda e, x: e.tensor_tensor(Ys[j], yc[j], x, ALU.mult), yt[j]) for j in T]


def chunks(n, d, q):
    NT = 12
    assert n.top + 24 * 512 <= n.stack[-1][2][1]
    bufs = [[n.buf(512) for _ in range(NT)] for _ in range(2)]
    f4 = lambda b: b.rearrange("p (a t) -> p a t", a=4)
    bar = n.barrier()
    last = [None] * 2
    for s in range(2):
        for i in range(4):
            (n.dve if s else n.pool)(lambda e: e.memset(bufs[s][i], 0.0))
    tz = n.pool(lambda e: e.memset(q["state"], 0.0))
    n.barrier()
    Dm = q["masks"][:, 0:128].unsqueeze(1).to_broadcast([P, 4, 128])
    Om = q["masks"][:, 128:256].unsqueeze(1).to_broadcast([P, 4, 128])
    Sm = q["masks"][:, 256:384].unsqueeze(1).to_broadcast([P, 4, 128])
    Im = q["masks"][:, 384:448].unsqueeze(1).to_broadcast([P, 8, 64])
    Id = n.ident.unsqueeze(1).to_broadcast([P, 4, 128])
    ST = q["state"]
    seq = dict(st=tz, y=None)

    def mul4(lhs, rhs, waits, lhs2=None, rhs2=None):
        b, bank, bf = n.banks.take()
        for p in range(4):
            c = slice(p * 128, (p + 1) * 128)
            n.pe(lambda e, c=c: e.matmul(bank[:, c], lhs[:, c], rhs[:, c], start=True, stop=lhs2 is None), bf, waits,
                 mark=False)
            if lhs2 is not None:
                n.pe(lambda e, c=c: e.matmul(bank[:, c], lhs2[:, c], rhs2[:, c], start=False, stop=True), mark=False)
        return b, bank

    def turn4(src, waits):
        b, bank, bf = n.banks.take()
        for p in range(4):
            c = slice(p * 128, (p + 1) * 128)
            n.transpose(bank[:, c], src[:, c], bf, waits, mark=False)
        return b, bank

    def sealed():
        return n.pe.sealed()

    def out_act(pair, dst, *waits):
        b, bank = pair
        t = n.act(lambda e: e.activation(dst, bank[:, :], ACT.Copy), *waits)
        n.banks.put(b, t)
        return t

    def out_dve(pair, dst, *waits):
        b, bank = pair
        t = n.dve(lambda e: e.tensor_copy(dst, bank[:, :]), *waits)
        n.banks.put(b, t)
        return t

    def add_dve(pair, dst, *waits):
        b, bank = pair
        t = n.dve(lambda e: e.tensor_tensor(dst, bank[:, :], dst, ALU.add), *waits)
        n.banks.put(b, t)
        return t

    def s0(u):
        c = u["c"]
        B = u["B"]
        cs = slice(c * 64, (c + 1) * 64)
        prev = last[u["s"]]
        toks = []
        for i, (name, eng) in enumerate((("AL", "p"), ("BT", "p"), ("KT", "a"), ("V", "a"))):
            src = f4(q[name])[:, :, cs]
            dst = B[i].rearrange("p (a h t) -> p a h t", a=4, h=2)
            for h in range(2):
                hs = slice(h * 64, h * 64 + 64)
                if eng == "p":
                    toks.append(n.pool(lambda e, src=src, dst=dst, hs=hs, h=h: e.tensor_copy(dst[hs, :, h, :], src[hs]), prev))
                else:
                    toks.append(n.act(lambda e, src=src, dst=dst, hs=hs, h=h: e.activation(dst[hs, :, h, :], src[hs], ACT.Copy), prev))
        u["t0"] = toks
        r = f4(q["RT"])[:, :, cs]
        u["r"] = r
        m1 = mul4(B[1], B[0], toks)
        m2 = mul4(B[2], B[0], toks)
        b, bank, bf = n.banks.take()
        for z in range(2):
            for p in range(4):
                n.pe(lambda e, z=z, p=p: e.matmul(bank[:, z * 256 + p * 64:z * 256 + p * 64 + 64],
                                                B[1 + z][:, p * 128:(p + 1) * 128], r[:, p, :], start=True, stop=True),
                     bf, mark=False)
        t = sealed()
        w = [t, q["tm"], prev]
        n.dve(lambda e: e.tensor_tensor(f4(B[4]), f4(m1[1][:, :]), Dm, ALU.mult), w)
        ta = n.dve(lambda e: e.tensor_tensor(f4(B[5]), f4(m1[1][:, :]), Om, ALU.mult), w)
        n.banks.put(m1[0], ta)
        tb = n.dve(lambda e: e.tensor_tensor(f4(B[6]), f4(m2[1][:, :]), Sm, ALU.mult), w)
        n.banks.put(m2[0], tb)
        e8 = lambda x: x.rearrange("p (a t) -> p a t", a=8)
        tc = n.dve(lambda e: e.tensor_tensor(e8(B[7]), e8(bank[:, :]), Im, ALU.mult), w)
        n.banks.put(b, tc)
        u["tN"], u["t6"], u["t7"] = ta, tb, tc

    def s1(u):
        B = u["B"]
        a = turn4(B[4], u["tN"])
        b = turn4(B[1], u["t0"])
        k = turn4(B[2], None)
        v = turn4(B[3], None)
        t = sealed()
        u["tA"] = out_dve(a, B[8], t)
        u["tb"] = out_act(b, B[9], t, last[u["s"]])
        u["tk"] = out_act(k, B[10], t)
        u["tv"] = out_act(v, B[11], t)
        u["tP"] = n.dve(lambda e: e.tensor_tensor(f4(B[1]), f4(B[4]), Id, ALU.add), t)

    def s2(u):
        B = u["B"]
        x = mul4(B[8], B[4], [u["tA"]])
        y = mul4(B[4], B[8], None)
        t = sealed()
        u["tx"] = out_act(x, B[2], t)
        u["ty"] = out_dve(y, B[3], t)

    def s3(u):
        B = u["B"]
        x = mul4(B[3], B[2], [u["tx"], u["ty"]])
        y = mul4(B[2], B[3], None)
        p = mul4(B[3], B[1], [u["tP"]])
        t = sealed()
        u["tx"] = out_act(x, B[4], t)
        u["ty"] = out_act(y, B[8], t)
        u["tP"] = add_dve(p, B[1], t)

    def s4(u):
        B = u["B"]
        y = mul4(B[4], B[8], [u["tx"], u["ty"]])
        p = mul4(B[8], B[1], [u["tP"]])
        t = sealed()
        u["ty"] = out_act(y, B[2], t)
        u["tP"] = add_dve(p, B[1], t)

    def s5(u):
        B = u["B"]
        p = mul4(B[2], B[1], [u["ty"], u["tP"]])
        u["tP"] = add_dve(p, B[1], sealed())

    def s6(u):
        B = u["B"]
        p = turn4(B[1], [u["tP"]])
        u["tPT"] = out_act(p, B[3], sealed())

    def s7(u):
        B = u["B"]
        z = mul4(B[3], B[5], [u["tPT"]])
        y = mul4(B[5], B[3], None)
        t = sealed()
        u["tx"] = out_act(z, B[4], t)
        u["ty"] = out_dve(y, B[8], t)

    def s8(u):
        B = u["B"]
        y = mul4(B[4], B[8], [u["tx"], u["ty"]])
        u["tz"] = out_act(y, B[2], sealed())

    def s9(u):
        B = u["B"]
        p = mul4(B[2], B[1], [u["tz"], u["tP"]])
        u["tP"] = add_dve(p, B[1], sealed())

    def s10(u):
        B = u["B"]
        p = mul4(B[8], B[1], [u["tP"], u["ty"]])
        u["tP"] = add_dve(p, B[1], sealed())

    def s11(u):
        B = u["B"]
        x = mul4(B[0], ST, [seq["st"], u["t6"], u["tv"], u["t0"]], B[6], B[11])
        u["tX"] = out_act(x, B[3], sealed())

    def s12(u):
        B = u["B"]
        x = mul4(B[1], B[3], [u["tX"], u["tP"]])
        u["tU"] = out_dve(x, B[5], sealed())

    def s13(u):
        B, c = u["B"], u["c"]
        waits = [u["tU"], u["tb"], u["tk"], u["tv"], u["t7"], seq["st"]]
        x = mul4(B[9], B[5], waits, B[10], B[11])
        b, bank, bf = n.banks.take()
        for p in range(4):
            c2 = slice(p * 128, (p + 1) * 128)
            o = bank[:, p * 64:(p + 1) * 64]
            prods = [(ST[:, c2], u["r"][:, p, :]), (B[5][:, c2], B[7][:, p * 64:(p + 1) * 64]),
                     (B[11][:, c2], B[7][:, 256 + p * 64:256 + (p + 1) * 64])]
            for j, (l, r) in enumerate(prods):
                n.pe(lambda e, o=o, l=l, r=r, j=j: e.matmul(o, l, r, start=(j == 0), stop=(j == 2)), bf, waits, mark=False)
        t = sealed()
        ta = n.dve(lambda e: e.tensor_tensor(ST, x[1][:, :], ST, ALU.add), t)
        n.banks.put(x[0], ta)
        pt = q["ptc"][:, :, c:c + 1].to_broadcast([P, 4, 128])
        seq["st"] = n.dve(lambda e: e.tensor_tensor(f4(ST), f4(ST), pt, ALU.mult), ta)
        y = f4(q["Y"])[:, :, c * 64:(c + 1) * 64]
        ps = bank[:, 0:256].rearrange("p (a t) -> p a t", a=4)
        if d == 0:
            ty = n.act(lambda e: e.activation(y, ps, ACT.Copy), t)
        else:
            ty = n.dve(lambda e: e.tensor_tensor(y, ps, y, ALU.add), t)
        n.banks.put(b, ty)
        last[u["s"]] = [t]

    steps = [s0, s1, s2, s3, s4, s5, s6, s7, s8, s9, s10, s11, s12, s13]
    order = range(8) if d == 0 else range(7, -1, -1)
    units = [dict(c=c, s=i % 2, B=bufs[i % 2]) for i, c in enumerate(order)]
    L = 7
    for tau in range(L * (len(units) - 1) + len(steps)):
        for i in range(len(units)):
            s = tau - L * i
            if 0 <= s < len(steps):
                steps[s](units[i])


def pool_branch(n, xt):
    ins = n.ins
    a = Pool([n.buf(528) for _ in range(2)])
    bufs = [n.buf(528) for _ in range(2)]
    icnt = n.buf(2048)
    pooled = [n.buf(512) for _ in range(4)]
    bar = n.barrier()
    tl = n.load([(icnt, ins["icnt"])], bar)
    tz = None
    for r in a.items:
        n.pool(lambda e, r=r: e.memset(r[:, 0:8], 0.0))
        tz = n.pool(lambda e, r=r: e.memset(r[:, 520:528], 0.0))
    w, wt, ws = n.weights(ins["pool_w"], 512)
    out = []

    def use(m, bank, tok):
        i, z, zf = a.take()
        tz1 = n.act(lambda e: e.activation(z[:, 8:520], bank[:, :], ACT.Copy), tok, zf)
        wd = (2, 4, 8, 16)[m]
        src, ln, t = z, 528, [tz1, tz]
        for s in range(m + 1):
            st = 1 << s
            ln -= st
            dst = bufs[s % 2]
            t = n.dve(lambda e, src=src, dst=dst, st=st, ln=ln: e.tensor_tensor(dst[:, 0:ln], src[:, 0:ln], src[:, st:st + ln],
                                                                              ALU.add), t)
            src = dst
        x0 = 8 - wd // 2
        t = n.dve(lambda e, src=src: e.tensor_tensor(pooled[m], src[:, x0:x0 + 512], icnt[:, m * 512:(m + 1) * 512], ALU.mult), t, tl)
        t = n.dve(lambda e: e.tensor_tensor(pooled[m], pooled[m], z[:, 8:520], ALU.subtract), t)
        a.put(i, t)
        out.append(t)
        return tz1

    heads_fm(n, [(ins["w2_pool"][j], 2) for j in range(2)], xt, use)
    toks = []
    for m in range(4):
        b, bank, bf = n.banks.take()
        tok = n.group(bank[:, :], [(w[:, m * 128:(m + 1) * 128], pooled[m])], wt, out[m], bf)
        y = pooled[m]
        t = n.dve(lambda e: e.tensor_scalar(y, bank[:, :], n.vec("pool_scale", m), None, ALU.mult), tok)
        n.banks.put(b, t)
        toks.append(list(n.rsplit(y, n.y_pool[m], t)))
    n.done(ws, tok)
    return toks


def axial_attention(n, xt):
    ins = n.ins
    n.open(3072)
    q = [n.buf(512) for _ in range(4)]
    k = n.buf(512)
    v = n.buf(512).rearrange("p (i c) -> p i c", i=4)
    inner = n.open(4096)
    cos, sin = n.buf(512), n.buf(512)
    raws = Pool([n.buf(512) for _ in range(2)])
    tmps = Pool([n.buf(512) for _ in range(2)])
    rs = Pool([n.buf(512) for _ in range(2)])
    bar = n.barrier()
    tl = n.load([(cos, ins["rope2"][0]), (sin, ins["rope2"][1])], bar)
    dsts = q + [k]
    rt = {}

    def use(m, bank, tok):
        i, raw, rf = raws.take()
        j, r, rrf = rs.take()
        t0 = n.act(lambda e: e.activation(raw, bank[:, :], ACT.Copy), tok, rf)
        t = n.act(lambda e: e.activation(r, raw, ACT.Square), t0, rrf)
        b, bk, bf = n.banks.take()
        tk = n.group(bk[:, :], [(n.bones, r)], t, bf)
        t = n.dve(lambda e: e.tensor_scalar(r, bk[:, :], 1.0 / 64, EPS, ALU.mult, ALU.add), tk)
        n.banks.put(b, t)
        t = n.act(lambda e: e.activation(r, r, ACT.Sqrt, scale=64.0 if m < 4 else 1.0), t)
        t = n.dve(lambda e: e.reciprocal(r, r), t)
        g = n.vec("q_norm" if m < 4 else "k_norm")
        t = n.dve(lambda e: e.scalar_tensor_tensor(out=raw, in0=raw, scalar=g, in1=r, op0=ALU.mult, op1=ALU.mult), t)
        rs.put(j, t)
        done, reads = rope(n, raw, t, n.rot2, cos, sin, tmps, dsts[m], tl)
        raws.put(i, done, *reads)
        rt[m] = done
        return t0

    heads_fm(n, [(ins["w2_att"][0], 2), (ins["w2_att"][1], 2), (ins["w2_att1"], 1)], xt, use)
    tv = values_tm(n, ins["w2_attv"], 128, xt, lambda x, i: x[:, i * P:(i + 1) * P], lambda i: v[:, i, :])
    n.close(inner)
    n.open(ATT_FLOATS(512))
    att = Attention(n, 512)
    units = []
    for t, pair in enumerate(ATT_TILES):
        for i in range(4):
            for par in range(2):
                ps = slice(par * 64, par * 64 + 64)
                units.append(dict(q=[q[t][ps, i * P:(i + 1) * P]], keys=[[k]], mask=None, sink=None, par=par,
                                  v=[v[:, j, par * 64:par * 64 + 64] for j in range(4)],
                                  out=cols(n.y_att[t], slice(i * P, (i + 1) * P)), waits=[rt[t], rt[4]] + tv))
    att.run(units)
    return att.toks


def merge(n, xt, yt, pt, ct):
    n.open(4096, F32R)
    yr = [n.pair() for _ in range(4)]
    n.open(11 * 512)
    sgs = Pool([n.buf(512) for _ in range(3)])
    mg = [n.buf(512) for _ in range(KT)]
    yt = [list(n.rsplit(n.y_rwkv[:, j * 512:(j + 1) * 512], yr[j], yt[j])) for j in range(4)]
    ys = [(yr, yt), (n.y_pool, pt), (n.y_att, [ct] * 4)]
    mt = []
    for m in range(KT):
        for z in range(3):
            w, wt, ws = n.weights(n.ins["w2_gate"][m, z], 1536)
            w = views(w, "p (k c) -> p k c", k=12)
            gb, g, gf = n.banks.take()
            ub, u, uf = n.banks.take()
            tg = n.group3(g[:, :], [(at(w, k), n.xn[k], xt[k]) for k in range(KT)], wt, gf)
            tu = n.group3(u[:, :], [(at(w, KT + k), ys[z][0][k], ys[z][1][k]) for k in range(4)], uf)
            n.done(ws, tu)
            i, sg, sf = sgs.take()
            t = n.act(lambda e, sg=sg, g=g: e.activation(sg, g[:, :], ACT.Sigmoid), tg, sf)
            n.banks.put(gb, t)
            if z == 0:
                t = n.dve(lambda e, m=m, sg=sg, u=u: e.tensor_tensor(mg[m], sg, u[:, :], ALU.mult), t, tu)
                n.banks.put(ub, t)
                ta = t
            else:
                t = n.dve(lambda e, sg=sg, u=u: e.tensor_tensor(sg, sg, u[:, :], ALU.mult), t, tu)
                n.banks.put(ub, t)
                t = ta = n.dve(lambda e, m=m, sg=sg: e.tensor_tensor(mg[m], mg[m], sg, ALU.add), t, ta)
            sgs.put(i, t)
        mt.append(ta)
    mt = [list(n.rsplit(mg[m], n.xn[m], mt[m], tg)) for m in range(KT)]
    return out_proj(n, n.ins["w2_out"], n.xn, mt)


def experts(n, norm):
    ins = n.ins
    router = n.buf(128)
    iota = n.buf(64)
    slotcol = n.buf(1)
    sels = n.buf(1024)
    small = n.buf(4 * 16 * 4 + 16)
    affT, work, slotT, eq = (n.buf(512) for _ in range(4))
    mx8 = n.buf(8)
    ones5 = n.buf(512)
    big = n.buf(8192)
    hn_tok = big[:, 0:4096].rearrange("p (i f) -> p i f", i=4)
    G = big[:, 4096:8192].rearrange("p (i s) -> p i s", i=4)
    ys = [big[:, i * 1024:(i + 1) * 1024] for i in range(8)]
    xg = n.buf(8192).rearrange("p (k s) -> p k s", k=KT)
    gv = [n.buf(512) for _ in range(8)]
    hids = Pool([n.buf(1024) for _ in range(1)])
    hidTs = Pool([n.buf(1024) for _ in range(2)])
    n.add_slots(2)
    bar = n.barrier()
    tl = n.load([(router, ins["router"]), (iota, ins["iota"]), (slotcol, ins["slotcol"]), (sels, ins["sels"])], bar)
    n.pool(lambda e: e.memset(affT, 0.0))
    n.pool(lambda e: e.memset(slotT, 0.0))
    to = n.pool(lambda e: e.memset(ones5, 1.0))
    n.dve.wait(to)
    xt = norm.finish("norm_ffn_2", n.xn, split=False)
    b, bank, bf = n.banks.take()
    for i in range(4):
        t = n.group(bank[:, i * 16:(i + 1) * 16],
                    [(n.xn[k][:, i * P:(i + 1) * P], router[:, k * 16:(k + 1) * 16], xt[k]) for k in range(KT)], tl, bf)
    l3 = bank[:, 0:64].rearrange("p (i e) -> p i e", i=4)
    aff = small[:, 0:64].rearrange("p (i e) -> p i e", i=4)
    slot = small[:, 64:128].rearrange("p (i e) -> p i e", i=4)
    m4, s4 = small[:, 128:132], small[:, 132:136]
    t1 = n.dve(lambda e: e.tensor_reduce(m4, l3, AX_X, ALU.max), t)
    t = n.dve(lambda e: e.tensor_tensor(aff, l3, m4.unsqueeze(2).to_broadcast([P, 4, 16]), ALU.subtract), t1)
    n.banks.put(b, t)
    t = n.act(lambda e: e.activation(aff, aff, ACT.Exp), t)
    t = n.dve(lambda e: e.tensor_reduce(s4, aff, AX_X, ALU.add), t)
    t = n.dve(lambda e: e.reciprocal(s4, s4), t)
    t_aff = n.dve(lambda e: e.tensor_tensor(aff, aff, s4.unsqueeze(2).to_broadcast([P, 4, 16]), ALU.mult), t)
    b, bank, bf = n.banks.take()
    for i in range(4):
        tok = n.transpose(bank[0:16, i * P:(i + 1) * P], aff[:, i, :], t_aff, bf)
    tT = n.dve(lambda e: e.tensor_copy(affT[0:16], bank[0:16, :]), tok)
    n.banks.put(b, tT)
    for i in range(4):
        for half in range(2):
            b, bank, bf = n.banks.take()
            for j in range(4):
                k = 4 * half + j
                tok = n.transpose(bank[:, j * P:(j + 1) * P], n.xn[k][:, i * P:(i + 1) * P], bf, xt[k], mark=(j == 3))
            th = n.act(lambda e, i=i, half=half, bank=bank: e.activation(hn_tok[:, i, half * 512:(half + 1) * 512], bank[:, :],
                                                                      ACT.Copy), tok)
            n.banks.put(b, th)
    tv = []
    for i in range(8):
        b, bank, bf = n.banks.take()
        tok = n.group(bank[:, :], [(sels[:, i * P:(i + 1) * P], affT)], bf, tT, tl)
        tv.append(n.act(lambda e: e.activation(gv[i], bank[:, :], ACT.Copy), tok))
        n.banks.put(b, tv[i])
    t = tT
    for r in range(8):
        src = affT if r == 0 else work
        t = n.dve(lambda e, src=src: e.max(mx8[0:16], src[0:16]), t)
        t = n.dve(lambda e, src=src: e.match_replace(work[0:16], mx8[0:16], src[0:16], -1.0), t)
    t = n.dve(lambda e: e.tensor_scalar(eq[0:16], work[0:16], 0.0, None, ALU.is_lt), t)
    t = n.dve(lambda e: e.tensor_tensor_scan(slotT[0:16], ones5[0:16], eq[0:16], 0.0, ALU.mult, ALU.add), t, to)
    t = n.dve(lambda e: e.tensor_tensor(slotT[0:16], slotT[0:16], eq[0:16], ALU.mult), t)
    t_slot = n.dve(lambda e: e.tensor_scalar(slotT[0:16], slotT[0:16], -1.0, None, ALU.add), t)
    b, bank, bf = n.banks.take()
    for i in range(4):
        tok = n.transpose(bank[:, i * 16:(i + 1) * 16], slotT[0:16, i * P:(i + 1) * P], t_slot, bf)
    t = n.dve(lambda e: e.tensor_copy(small[:, 64:128], bank[:, 0:64]), tok)
    n.banks.put(b, t)
    for i in range(4):
        tG = n.dve(lambda e, i=i: e.tensor_tensor(G[:, i, :].rearrange("p (a s) -> p a s", a=16),
                                                iota.unsqueeze(1).to_broadcast([P, 16, 64]),
                                                slot[:, i, :].unsqueeze(2).to_broadcast([P, 16, 64]), ALU.is_equal), t, tl)
    txg = {}
    for half in range(2):
        for k in range(KT):
            b, bank, bf = n.banks.take()
            tok = n.group(bank[:, :], [(hn_tok[:, i, k * P:(k + 1) * P], G[:, i, half * 512:(half + 1) * 512]) for i in range(4)],
                          tG, th, bf)
            f = n.act if k % 2 else n.dve
            if k % 2:
                t = n.act(lambda e, k=k, half=half, bank=bank: e.activation(xg[:, k, half * 512:(half + 1) * 512], bank[:, :], ACT.Copy), tok)
            else:
                t = n.dve(lambda e, k=k, half=half, bank=bank: e.tensor_copy(xg[:, k, half * 512:(half + 1) * 512], bank[:, :]), tok)
            n.banks.put(b, t)
            txg[k, half] = t
    t_dispatched = tok
    tgv = []
    for i in range(8):
        b, bank, bf = n.banks.take()
        tok = n.group(bank[:, :], [(sels[:, i * P:(i + 1) * P], slotT)], bf, t_slot)
        t = n.dve(lambda e: e.scalar_tensor_tensor(out=gv[i], in0=bank[:, :], scalar=slotcol, in1=gv[i], op0=ALU.is_equal,
                                                   op1=ALU.mult), tok, tv[i])
        n.banks.put(b, t)
        tgv.append(t)

    def product(src, pair, lhs, waits):
        t0, t1 = n.banks.take(), n.banks.take()
        for j in range(4):
            w = [n.weights(expert_block(src, 2 * pair + a, j), 2048) for a in range(2)]
            for kk in range(2):
                k = 2 * j + kk
                for cc, (b, bank, bf) in enumerate((t0, t1)):
                    for a in range(2):
                        tok = n.pe(lambda e, bank=bank, a=a, cc=cc, k=k, kk=kk, w=w: e.matmul(
                            bank[a * 64:a * 64 + 64, :], lhs(k, a), w[a][0][:, kk * 1024 + cc * 512:kk * 1024 + cc * 512 + 512],
                            start=(k == 0), stop=(k == 7)), w[a][1], bf, waits(k, a), mark=(kk == 1 and cc == 1 and a == 1))
            for a in range(2):
                n.done(w[a][2], tok)
        return (t0[0], t0[1]), (t1[0], t1[1]), tok

    def down(i, hT, ti, tT2):
        y0, y1, tok = product(ins["exp_down"], i, lambda k, a: hT[:, k * P + a * 64:k * P + a * 64 + 64], lambda k, a: tT2)
        hidTs.put(ti, tok)
        ta = n.act(lambda e: e.activation(ys[i][:, 0:512], y0[1][:, :], ACT.Copy), tok, t_dispatched)
        tb = n.dve(lambda e: e.tensor_copy(ys[i][:, 512:1024], y1[1][:, :]), tok, t_dispatched)
        n.banks.put(y0[0], ta)
        n.banks.put(y1[0], tb)
        return [ta, tb]

    ty = []
    pend = None
    for i in range(8):
        lhs = lambda k, a, i=i: xg[:, k, (2 * i + a) * 64:(2 * i + a) * 64 + 64]
        w = lambda k, a, i=i: txg[k, i // 4]
        g0, g1, tg = product(ins["exp_gate"], i, lhs, w)
        hi, hid, hf = hids.take()
        ts = []
        for c, (b, bank) in enumerate((g0, g1)):
            t = n.act(lambda e, c=c, bank=bank, hid=hid: e.activation(hid[:, c * 512:(c + 1) * 512], bank[:, :], ACT.Silu), tg, hf)
            n.banks.put(b, t)
            ts.append(t)
        u0, u1, tu = product(ins["exp_up"], i, lhs, w)
        for c, (b, bank) in enumerate((u0, u1)):
            t = n.dve(lambda e, c=c, bank=bank, hid=hid: e.tensor_tensor(hid[:, c * 512:(c + 1) * 512],
                                                                       hid[:, c * 512:(c + 1) * 512], bank[:, :], ALU.mult), tu, ts[c])
            n.banks.put(b, t)
            ts[c] = t
        if pend is not None:
            ty.append(down(*pend))
        ti, hT, tf = hidTs.take()
        tt = []
        for c in range(2):
            b, bank, bf = n.banks.take()
            for j in range(4):
                tok = n.transpose(bank[:, j * P:(j + 1) * P], hid[:, c * 512 + j * P:c * 512 + (j + 1) * P], ts[c], bf, mark=(j == 3))
            if c:
                t = n.act(lambda e, c=c, bank=bank, hT=hT: e.activation(hT[:, c * 512:(c + 1) * 512], bank[:, :], ACT.Copy), tok, tf)
            else:
                t = n.dve(lambda e, c=c, bank=bank, hT=hT: e.tensor_copy(hT[:, c * 512:(c + 1) * 512], bank[:, :]), tok, tf)
            n.banks.put(b, t)
            tt.append(t)
        hids.put(hi, tok)
        pend = (i, hT, ti, tt)
    ty.append(down(*pend))
    nxt = Norm(n)
    for m in range(KT):
        b, bank, bf = n.banks.take()
        tok = n.group(bank[:, :], [(ys[i][:, m * P:(m + 1) * P], gv[i], [ty[i], tgv[i]]) for i in range(8)], bf)
        nxt.flush()
        t = n.dve(lambda e, m=m, bank=bank: e.tensor_tensor(n.h[m], bank[:, :], n.h[m], ALU.add), tok)
        n.banks.put(b, t)
        nxt.add(n.h[m], t)
        n.ht[m] = t
    return nxt


def expert_block(w, e, j):
    return w[e, j * 256:(j + 1) * 256, :].rearrange("(k p) c -> p k c", p=P)


def weight_order(ins):
    order = []

    def add(blocks, floats, split=True):
        order.extend((b, floats, split) for b in blocks)

    def add_ffn(i):
        add([ins["w_gu"][i][m] for m in range(FF)], 2048)
        add([ins["w_dn"][i][m, :, z * 1408:(z + 1) * 1408] for m in range(KT) for z in range(2)], 1408)

    def add_ple(i):
        add([ins["w_ple"][i, m] for m in range(KT)], 1280)

    add_ffn(0)
    add([ins["w_ab_qk"][j] for j in range(10)], 2048)
    add([ins["w_ab_v"][j] for j in range(4)], 2048)
    add([ins["w_ab_out"][j] for j in range(4)], 2048)
    add_ffn(1)
    add_ple(0)
    add_ffn(2)
    add([ins["w_c_qk"][j] for j in range(8)], 2048)
    add([ins["w_c_v"][j] for j in range(4)], 2048)
    add([ins["w_c_out"][j] for j in range(4)], 2048)
    add_ffn(3)
    add_ple(1)
    add([ins["w2_rwkv"][j] for j in range(7)], 2048, False)
    add([ins["w2_rwkv1"], ins["lora"][0], ins["lora"][1]], 1024, False)
    add([ins["g2"]], 512, False)
    add([ins["pool_w"]], 512, False)
    add([ins["w2_pool"][j] for j in range(2)], 2048)
    add([ins["w2_att"][0], ins["w2_att"][1]], 2048)
    add([ins["w2_att1"], ins["w2_attv"]], 1024)
    add([ins["w2_gate"][m, z] for m in range(KT) for z in range(3)], 1536)
    add([ins["w2_out"][j] for j in range(4)], 2048)
    for i in range(9):
        for name, pair in (("exp_gate", i), ("exp_up", i), ("exp_down", i - 1)):
            if 0 <= pair < 8:
                add([expert_block(ins[name], 2 * pair + a, j) for j in range(4) for a in range(2)], 2048, False)
    return order


def second_block(n, norm):
    ins = n.ins
    spill = n.nc.dram_tensor("h_spill", (KT, P, S), F32, kind="Internal").ap()
    s = n.sem("s_spill")
    for k in range(KT):
        n.sp(lambda e, k=k: e.dma_start(spill[k], n.h[k]).then_inc(s, 16), n.ht, mark=False)
    spilled = (s, 16 * KT)
    n.close(2)
    n.parts = None
    n.open(2 * SLOT)
    n.add_slots(2)
    n.xn = n.h
    xt = norm.finish("norm_mix_2", n.xn, spilled, split=False)
    n.open(2048)
    n.y_rwkv = n.buf(2048)
    inner = n.open(TOTAL - P_FLOATS - KT * 512 - 2 * SLOT - 2048)
    yt = rwkv(n, xt)
    n.close(inner)
    n.open(8192, F32R)
    n.y_pool, n.y_att = ([n.pair() for _ in range(4)] for _ in range(2))
    xn = n.xn
    open_xn(n)
    n.open_parts()
    tx = [list(n.rsplit(xn[k], n.xn[k])) for k in range(KT)]
    n.ht = [n.load([(n.h[k], spill[k]) for k in range(KT)], spilled, tx)] * KT
    work = len(n.stack)
    n.open(6400)
    pt = pool_branch(n, tx)
    n.close(work)
    at = axial_attention(n, tx)
    n.close(work)
    norm = merge(n, tx, yt, pt, at)
    n.close(inner - 1)
    n.parts = None
    n.open(TOTAL - P_FLOATS - KT * 512 - 2 * SLOT)
    n.xn = [n.buf(512) for _ in range(KT)]
    return experts(n, norm)


def program(nc, ins, out):
    with ExitStack() as ctx:
        n = make_net(nc, ctx, ins)
        norm = first_block(n)
        norm = second_block(n, norm)
        t = norm.finish("norm_final_2", n.xn, split=False)
        s = n.sem("s_out")
        for k in range(KT):
            n.sp(lambda e, k=k: e.dma_start(out[k], n.xn[k]).then_inc(s, 16), t[k], mark=False)
        n.sp.wait((s, 16 * KT))


def _cols(w, cols=None):
    if cols is not None:
        w = w[:, cols]
    k, m = w.shape
    return w.reshape(k // P, P, m // P, P).transpose(2, 1, 0, 3)


def _two(t):
    a, p, k, c = t.shape
    return np.ascontiguousarray(t.reshape(a // 2, 2, p, k, c).transpose(0, 2, 1, 3, 4)).reshape(a // 2, p, 2 * k * c)


def _wide(w):
    k, m = w.shape
    return np.ascontiguousarray(w.reshape(k // P, P, m).transpose(1, 0, 2)).reshape(P, -1)


def _head_cols(tiles):
    return np.concatenate([np.arange(h * 64, h * 64 + 64) for pair in tiles for h in pair])


def _constants():
    c = np.zeros((5, P, P), np.float32)
    c[0] = np.eye(P)
    c[1] = 1.0
    for a in range(2):
        c[2, a * 64:a * 64 + 64, a * 64:a * 64 + 64] = 1.0
        for i in range(32):
            c[3, a * 64 + i + 32, a * 64 + i] = -1.0
            c[3, a * 64 + i, a * 64 + i + 32] = 1.0
            c[4, a * 64 + 2 * i + 1, a * 64 + 2 * i] = -1.0
            c[4, a * 64 + 2 * i, a * 64 + 2 * i + 1] = 1.0
    f32 = np.float32
    inv = (10000.0 ** (-(np.arange(32) / 32))).astype(f32)
    ang = (np.arange(S, dtype=f32)[:, None] * inv[None, :]).astype(f32).astype(np.float64)
    rope1 = np.stack([np.tile(np.cos(ang).T, (4, 1)), np.tile(np.sin(ang).T, (4, 1))]).astype(f32)
    fr = (10000.0 ** (-(np.arange(0, 32, 2) / 32))).astype(f32)
    row = np.repeat(np.arange(8, dtype=f32), 64)
    col = np.tile(np.arange(64, dtype=f32), 8)
    ang = np.concatenate([row[:, None] * fr, col[:, None] * fr], axis=-1).astype(np.float64)
    rope2 = np.stack([np.tile(np.repeat(np.cos(ang).T, 2, axis=0), (2, 1)),
                      np.tile(np.repeat(np.sin(ang).T, 2, axis=0), (2, 1))]).astype(f32)
    i = np.arange(P)[:, None]
    j = np.arange(384)[None, :] - P
    mask_a = np.where(np.abs(i - j) <= 128, 0, NEG).astype(f32)
    mb1 = np.zeros((P, 4, S), f32)
    for r in range(4):
        mb1[:, r] = np.where(np.abs(4 * np.arange(P)[:, None] + r - np.arange(S)[None, :]) <= 64, 0, NEG)
    d = np.arange(P)[:, None] - np.arange(P)[None, :]
    mb23 = np.concatenate([np.where(np.abs(d) <= 64, 0, NEG), np.where(d % 4 == 0, 0, NEG)], 1).astype(f32)
    cq = np.arange(P) % 64
    cs = np.clip(cq - 8, 0, 48)[:, None]
    kc = np.arange(64)[None, :]
    win = np.where((kc >= cs) & (kc < cs + 16), 0, NEG).astype(f32)
    mask_c = np.tile(win, (1, 16))
    reset = np.ones((P, S), f32)
    reset[:, ::64] = 0
    t = np.arange(S)
    icnt = np.zeros((P, 4, S), f32)
    for g, w in enumerate((2, 4, 8, 16)):
        lo, hi = w // 2, w - w // 2 - 1
        icnt[:, g] = 1.0 / (np.clip(t + hi + 1, 0, S) - np.clip(t - lo, 0, S))
    a, b = np.arange(P)[:, None], np.arange(P)[None, :]
    mask_r = np.zeros((2, P, 448), f32)
    for d in range(2):
        head = a // 64 == b // 64
        strict = (a % 64 < b % 64) if d == 0 else (a % 64 > b % 64)
        block = (a % 64) // 16 == (b % 64) // 16
        mask_r[d, :, 0:128] = head & strict & block
        mask_r[d, :, 128:256] = head & strict & ~block
        mask_r[d, :, 256:384] = head & strict
        tt = np.arange(64)[None, :]
        mask_r[d, :, 384:448] = (a % 64 <= tt) if d == 0 else (a % 64 >= tt)
    sels = np.zeros((P, 8, P), f32)
    for e in range(16):
        sels[e, e // 2, (e % 2) * 64:(e % 2) * 64 + 64] = 1
    more = dict(reset=reset, icnt=icnt.reshape(P, -1), mask_r=mask_r, sels=sels.reshape(P, -1),
                iota=np.tile(np.arange(64, dtype=f32), (P, 1)), slotcol=(np.arange(P) % 64).astype(f32).reshape(P, 1))
    return dict(more, consts=c, rope1=rope1, rope2=rope2, mask_a=mask_a, mask_b1=mb1.reshape(P, -1), mask_b23=mb23,
                mask_c=mask_c)


def _layout(x):
    f = {k: np.asarray(v) for k, v in x.items()}
    a = dict(_constants())
    a["x"] = np.ascontiguousarray(f["x"][0].T).reshape(KT, P, S)
    a["p"] = np.ascontiguousarray(f["p"][:, 0].transpose(0, 2, 1)).reshape(2, 2, P, S)
    v = lambda z: z.reshape(-1, P).T
    dup = lambda z: np.concatenate([z, z]).reshape(P, 1)
    parts = [v(f["norm_ffn1"][0]), v(f["norm_ffn1"][1]), v(f["norm_mix"][0]), v(f["norm_mix"][1]),
             v(f["norm_ffn2"][0]), v(f["norm_ffn2"][1]), v(f["norm_ple"][0]), v(f["norm_ple"][1]),
             v(f["norm_final"]), v(f["norm_mix_2"][0]), v(f["norm_ffn_2"][0]), v(f["norm_final_2"]),
             v(f["shift_prev_2"][0]), v(f["shift_next_2"][0]), v(f["rwkv_w0_2"][0, 0]), v(f["rwkv_w0_2"][0, 1]),
             v(f["rwkv_a0_2"][0, 0]), v(f["rwkv_a0_2"][0, 1]), v(f["rwkv_k_k_2"][0]), v(f["rwkv_k_a_2"][0]),
             v(f["rwkv_r_k_2"][0]), v(f["rwkv_ln_w_2"][0]), v(f["rwkv_ln_b_2"][0]), v(f["pool_scale_2"][0]),
             dup(f["q_norm_2"][0]), dup(f["k_norm_2"][0])]
    a["vecs"] = np.ascontiguousarray(np.concatenate(parts, axis=1))
    a["sink_a"] = f["sink_a"].reshape(1, 12)
    gu, dn = [], []
    for layer in range(2):
        for s in ("ffn1", "ffn2"):
            g = _cols(f[f"{s}_w_gate"][layer])
            u = _cols(f[f"{s}_w_up"][layer])
            gu.append(np.stack([g, u], axis=2).reshape(FF, P, 2048))
            dn.append(_cols(f[f"{s}_w_down"][layer]).reshape(KT, P, FF * P))
    a["w_gu"] = np.stack(gu)
    a["w_dn"] = np.stack(dn)
    w = f["w_in_ab"][0]
    ha = _head_cols(A_TILES)
    qk = np.concatenate([ha, np.arange(768, 1024), np.arange(1280, 1280 + 1536)])
    a["w_ab_qk"] = _two(_cols(w, qk))
    a["w_ab_v"] = np.stack([_wide(w[:, 1024:1280])] + [_wide(w[:, 2816 + 256 * g:2816 + 256 * (g + 1)]) for g in range(3)])
    rows = np.concatenate([ha, np.arange(768, 1024)])
    a["w_ab_out"] = _two(_cols(f["w_out_ab"][0][rows]))
    w = f["w_in_c"][0]
    a["w_c_qk"] = _two(_cols(w[:, 0:2048]))
    a["w_c_v"] = np.stack([_wide(w[:, 2048 + 256 * g:2048 + 256 * (g + 1)]) for g in range(4)])
    a["w_c_out"] = _two(_cols(f["w_out_c"][0]))
    rpb = f["rpb_c"][0]
    t = np.zeros((16, P, 16, 64), rpb.dtype)
    for p in range(P):
        half, c = p // 64, p % 64
        lo, hi = max(0, c - 15), min(64, c + 16)
        t[:, p, half:half + 15, lo:hi] = rpb[:, :, lo - c + 15:hi - c + 15]
    a["rpb"] = t.reshape(16, P, 1024)
    a["w_ple"] = np.stack([np.concatenate([_cols(f["w_ple_gate"][i]), _cols(f["w_ple_proj"][i])], axis=2)
                           .reshape(KT, P, 1280) for i in range(2)])
    w = f["w_in_2"][0]
    a["w2_rwkv"] = _two(_cols(w[:, 0:1792]))
    a["w2_rwkv1"] = _cols(w[:, 1792:1920]).reshape(P, 1024)
    a["w2_pool"] = _two(_cols(w[:, 1920:2432]))
    hq = _head_cols(ATT_TILES)
    a["w2_att"] = _two(_cols(w[:, 2432:2944], hq))
    a["w2_att1"] = _cols(w[:, 2944:3072]).reshape(P, 1024)
    a["w2_attv"] = _wide(w[:, 3072:3200])
    gates = _cols(w[:, 3200:6272]).reshape(3, KT, P, KT, P)
    br = np.stack([_cols(f["w_branch_rwkv_2"][0]), _cols(f["w_branch_pool_2"][0]),
                   _cols(f["w_branch_attn_2"][0][hq])])
    a["w2_gate"] = np.concatenate([gates, br], axis=3).transpose(1, 0, 2, 3, 4).reshape(KT, 3, P, 1536)
    a["w2_out"] = _two(_cols(f["w_out_2"][0]))
    lora = np.zeros((2, P, 2, 512), f["rwkv_w2_2"].dtype)
    for z, name in enumerate(("rwkv_w2_2", "rwkv_a2_2")):
        for d in range(2):
            lora[d, d * 64:d * 64 + 64, z] = f[name][0, d]
    a["lora"] = lora.reshape(2, P, 1024)
    a["g2"] = f["rwkv_g2_2"][0]
    a["pool_w"] = np.ascontiguousarray(f["pool_w_2"][0].transpose(1, 0, 2)).reshape(P, 512)
    a["router"] = _wide(f["router_2"][0])
    for name in ("exp_gate", "exp_up", "exp_down"):
        a[name] = f[f"{name}_2"][0]
    return a


def kernel(**inputs):
    import concourse.bacc as _bacc
    from concourse import mybir as _mybir
    from concourse.bass_utils import run_bass_kernel_spmd as _run

    nc = _bacc.Bacc("TRN2", target_bir_lowering=False, num_devices=1)
    feed, ins = {}, {}
    for name, x in _layout(inputs).items():
        x = np.ascontiguousarray(x)
        feed[f"in_{name}"] = x
        ins[name] = nc.dram_tensor(f"in_{name}", x.shape, _mybir.dt.from_np(x.dtype), kind="ExternalInput").ap()
    out = nc.dram_tensor("out_0", (KT, P, S), _mybir.dt.float32, kind="ExternalOutput").ap()
    program(nc, ins, out)
    r = _run(nc, [feed], core_ids=[0])
    return np.ascontiguousarray(r.results[0]["out_0"].reshape(D, S).T).reshape(1, S, D)
```

```python
from contextlib import ExitStack

import numpy as np

import concourse.bass as bass
from concourse import mybir

F32 = mybir.dt.float32
F32R = mybir.dt.float32r
ALU = mybir.AluOpType
ACT = mybir.ActivationFunctionType
AX_X = mybir.AxisListType.X

P = 128
S = 512
D = 1024
KT = 8
FF = 22
EPS = 1e-6
NEG = -1e30
NSLOT = 2
SLOT = 2048

A_TILES = [(0, 3), (1, 4), (2, 5), (6, 9), (7, 10), (8, 11)]
ATT_TILES = [(0, 4), (1, 5), (2, 6), (3, 7)]

VEC = {}
_at = 0
for _name, _n in [("norm_ffn1_0", 8), ("norm_ffn1_1", 8), ("norm_mix_0", 8), ("norm_mix_1", 8),
                  ("norm_ffn2_0", 8), ("norm_ffn2_1", 8), ("norm_ple_0", 8), ("norm_ple_1", 8),
                  ("norm_final", 8), ("norm_mix_2", 8), ("norm_ffn_2", 8), ("norm_final_2", 8),
                  ("shift_prev", 15), ("shift_next", 15), ("w0_0", 4), ("w0_1", 4), ("a0_0", 4), ("a0_1", 4),
                  ("k_k", 4), ("k_a", 4), ("r_k", 4), ("ln_w", 4), ("ln_b", 4), ("pool_scale", 4),
                  ("q_norm", 1), ("k_norm", 1)]:
    VEC[_name] = _at
    _at += _n
NVEC = _at


class Queue:

    def __init__(self, eng, sem, skip_own=False):
        self.eng, self.sem, self.skip_own = eng, sem, skip_own
        self.count, self.seen, self.last = 0, {}, None

    def wait(self, *tokens):
        need = {}
        stack = list(tokens)
        while stack:
            w = stack.pop()
            if isinstance(w, list):
                stack.extend(w)
            elif w is not None and not (self.skip_own and w[0] is self.sem):
                if w[1] > max(self.seen.get(id(w[0]), 0), need.get(id(w[0]), (None, 0))[1]):
                    need[id(w[0])] = w
        for key, (s, v) in need.items():
            self.eng.wait_ge(s, v)
            self.seen[key] = v

    def __call__(self, fn, *waits, mark=True):
        self.wait(*waits)
        self.last = fn(self.eng)
        return self.sealed() if mark else self.now()

    def sealed(self):
        self.last.then_inc(self.sem, 1)
        self.count += 1
        return self.now()

    def now(self):
        return (self.sem, self.count)


class Pool:

    def __init__(self, items):
        self.items = list(items)
        self.ready = [(i, []) for i in range(len(self.items))]

    def take(self):
        i, toks = self.ready.pop(0)
        return i, self.items[i], toks

    def put(self, i, *toks):
        self.ready.append((i, list(toks)))


P_FLOATS = 5 * P + NVEC + 24 + 2 * 512 + 512 + NSLOT * SLOT
TOTAL = 52160


class Net:
    def __init__(self, nc, ctx, ins):
        self.nc, self.ctx, self.ins = nc, ctx, ins
        sem = lambda n: ctx.enter_context(nc.semaphore(n))
        self.sem = sem
        self.pe = Queue(nc.tensor, sem("s_pe"), skip_own=True)
        self.act = Queue(nc.scalar, sem("s_act"))
        self.dve = Queue(nc.vector, sem("s_dve"))
        self.pool = Queue(nc.gpsimd, sem("s_pool"))
        self.sp = Queue(nc.sync, sem("s_sp"))
        self.stack, self.names = [], 0
        self.open(P_FLOATS)
        self.base = None
        self.banks = Pool([ctx.enter_context(nc.psum_tensor(f"bank{i}", [P, 512], F32)) for i in range(8)])
        self.nsem = 0
        self.order, self.fence = weight_order(ins)
        self.fetched = self.split = self.used = 0
        self.wsem, self.wcount, self.where = [], [], {}
        self.wslots = Pool([])
        self.add_slots(NSLOT)
        self.parts = None

    def open(self, floats, dtype=F32):
        self.names += 1
        c = ExitStack()
        t = c.enter_context(self.nc.sbuf_tensor(f"mem{self.names}", [P, floats], dtype))
        self.stack.append((c, t, [0, floats]))
        return len(self.stack) - 1

    def close(self, level):
        while len(self.stack) > level:
            self.stack.pop()[0].close()
        return self.barrier()

    def buf(self, n, level=-1):
        _, t, at = self.stack[level]
        a = t[:, at[0]:at[0] + n]
        at[0] += n
        assert at[0] <= at[1], (at, n)
        return a

    @property
    def top(self):
        return self.stack[-1][2][0]

    @top.setter
    def top(self, v):
        self.stack[-1][2][0] = v

    def pair(self, level=-1, n=512):
        return (self.buf(n, level), self.buf(n, level))

    def add_slots(self, k):
        for _ in range(k):
            self.add_slot(self.buf(SLOT))

    def add_slot(self, ap, *toks):
        self.wslots.items.append(ap)
        self.wslots.ready.append((len(self.wslots.items) - 1, list(toks)))
        self.wsem.append(self.sem(f"s_w{len(self.wsem)}"))
        self.wcount.append(0)

    def open_parts(self, k=2):
        level = self.open(k * 2 * SLOT, F32R)
        self.parts = Pool([(self.buf(SLOT), self.buf(SLOT)) for _ in range(k)])
        return level

    def fetch(self, upto=10 ** 6):
        while self.fetched < min(upto, len(self.order)) and self.wslots.ready:
            src, n, _ = self.order[self.fetched]
            i, ap, free = self.wslots.take()
            dst = ap[:, 0:n]
            if len(src.shape) == 3:
                dst = dst.rearrange("p (a b) -> p a b", a=src.shape[1])
            s = self.wsem[i]
            self.wcount[i] += 16
            self.sp(lambda e: e.dma_start(dst, src).then_inc(s, 16), free, mark=False)
            self.where[self.fetched] = (i, ap[:, 0:n], (s, self.wcount[i]))
            self.fetched += 1

    def split_to(self, last):
        while self.split <= last and self.split < self.fence:
            if self.order[self.split][2]:
                if self.parts is None or not self.parts.ready or self.split not in self.where:
                    return
                i, ap, tok = self.where[self.split]
                n = ap.shape[-1]
                j, (hi, lo), free = self.parts.take()
                hi, lo = hi[:, 0:n], lo[:, 0:n]
                th, tl = self.rsplit(ap, (hi, lo), tok, free)
                self.wslots.put(i, th, tl)
                self.where[self.split] = (j, (hi, lo), [th, tl])
                self.fetch()
            self.split += 1

    def high(self, src, dst, *toks):
        return self.act(lambda e: e.activation(dst[0], src, ACT.Copy), *toks)

    def low(self, src, dst, *toks):
        return self.dve(lambda e: e.tensor_tensor(dst[1], src, dst[0].bitcast(F32), ALU.subtract), *toks)

    def rsplit(self, src, dst, *toks):
        th = self.high(src, dst, *toks)
        return th, self.low(src, dst, th, *toks)

    def weights(self, src, n):
        self.fetch()
        want = self.order[self.used]
        assert want[1] == n and want[0].shape == src.shape and want[0].offset == src.offset, (self.used, want, src)
        self.split_to(self.used + 1)
        assert self.split > self.used
        slot, ap, toks = self.where.pop(self.used)
        kind = want[2]
        self.used += 1
        return ap, toks, (kind, slot)

    def done(self, block, tok):
        kind, slot = block
        if kind:
            self.parts.put(slot, tok)
        else:
            self.wslots.put(slot, tok)
            self.fetch()

    def load(self, pairs, *waits):
        s = self.sem(f"s_ld{self.nsem}")
        self.nsem += 1
        for dst, src in pairs:
            self.sp(lambda e, dst=dst, src=src: e.dma_start(dst, src).then_inc(s, 16), *waits, mark=False)
        return (s, 16 * len(pairs))

    def barrier(self):
        toks = [q.now() for q in (self.pe, self.act, self.dve, self.pool)]
        for q in (self.pe, self.act, self.dve, self.pool):
            q.wait(toks)
        return toks

    def group(self, out, pairs, *waits):
        n = len(pairs)
        for j, pr in enumerate(pairs):
            lhsT, rhs = pr[0], pr[1]
            own = pr[2] if len(pr) > 2 else None
            tok = self.pe(lambda e, l=lhsT, r=rhs, j=j: e.matmul(out, l, r, start=(j == 0), stop=(j == n - 1)),
                          own, waits and list(waits), mark=(j == n - 1))
        return tok

    def group3(self, out, pairs, *waits):
        if not isinstance(pairs[0][0], tuple):
            return self.group(out, pairs, *waits)
        flat = []
        for pr in pairs:
            (lh, ll), (rh, rl) = pr[0], pr[1]
            own = pr[2] if len(pr) > 2 else None
            flat += [(lh, rh, own), (lh, rl, own), (ll, rh, own)]
        return self.group(out, flat, *waits)

    def transpose(self, out, src, *waits, mark=True):
        k = src.shape[0]
        return self.pe(lambda e: e.transpose(out, src, self.ident[0:k, 0:k]), *waits, mark=mark)


class Norm:

    def __init__(self, n, gain=None, dst=None, *free):
        self.n, self.pend, self.k = n, [], 0
        self.b, self.bank, self.free = n.banks.take()
        self.gain, self.dst, self.dst_free, self.xt = gain, dst, list(free), []

    def add(self, ap, tok):
        n = self.n
        i, sq, free = n.sq.take()
        t = n.act(lambda e: e.activation(sq, ap, ACT.Square), tok, free)
        self.pend.append((i, sq, t))
        if self.gain:
            k = len(self.xt)
            g, (hi, lo) = n.vec(self.gain, k), self.dst[k]
            th = n.act(lambda e: e.activation(hi, ap, ACT.Copy, scale=g), tok, self.dst_free)
            tl = n.dve(lambda e: e.scalar_tensor_tensor(out=lo, in0=ap, scalar=g, in1=hi.bitcast(F32), op0=ALU.mult,
                                                        op1=ALU.subtract), th, tok, self.dst_free)
            self.xt.append([th, tl])

    def flush(self):
        n = self.n
        for i, sq, t in self.pend:
            k = self.k
            tok = n.pe(lambda e, k=k, sq=sq: e.matmul(self.bank[:, :], n.ones, sq, start=(k == 0), stop=(k == KT - 1)),
                       t, self.free)
            n.sq.put(i, tok)
            self.k += 1
            self.tok = tok
        self.pend = []

    def rms(self):
        n = self.n
        self.flush()
        assert self.k == KT
        r = n.rstd
        t = n.act(lambda e: e.activation(r, self.bank[:, :], ACT.Sqrt, scale=1.0 / D, bias=n.eps), self.tok, n.rstd_free)
        n.banks.put(self.b, t)
        t = n.dve(lambda e: e.reciprocal(r, r), t)
        n.rstd_free = None
        return r, t

    def finish(self, gain, dst, *waits):
        n = self.n
        r, t = self.rms()
        toks = []
        for k in range(KT):
            toks.append(n.dve(lambda e: e.scalar_tensor_tensor(out=dst[k], in0=n.h[k], scalar=n.vec(gain, k), in1=r, op0=ALU.mult,
                                                               op1=ALU.mult), t, *waits))
        n.rstd_free = toks[-1]
        return toks


def make_net(nc, ctx, ins):
    n = Net(nc, ctx, ins)
    n.ident, n.ones, n.bones, n.rot1, n.rot2 = (n.buf(P) for _ in range(5))
    n.vecs = n.buf(NVEC)
    n.cc = n.buf(15 + 4 + 2)
    n.sq = Pool([n.buf(512) for _ in range(2)])
    n.rstd = n.buf(512)
    n.rstd_free = None
    n.eps, n.eps_q, n.eps_y = n.buf(1), n.buf(1), n.buf(1)
    n.open(KT * 512)
    n.h = [n.buf(512) for _ in range(KT)]
    n.open_parts()
    n.vec = lambda name, k=0: n.vecs[:, VEC[name] + k:VEC[name] + k + 1]
    n.base = len(n.stack)
    c = ins["consts"]
    n.t_const = n.load([(n.ident, c[0]), (n.ones, c[1]), (n.bones, c[2]), (n.rot1, c[3]), (n.rot2, c[4]),
                        (n.vecs, ins["vecs"])])
    n.fetch(1)
    for ap, v in ((n.eps, EPS), (n.eps_q, 64 * EPS), (n.eps_y, 64e-5)):
        te = n.pool(lambda e: e.memset(ap, v))
    for q in (n.pe, n.act, n.dve, n.pool):
        q.wait(n.t_const, te)
    open_xn(n)
    n.base += 1
    return n


def open_xn(n):
    level = n.open(KT * 1024, F32R)
    n.xn = [n.pair() for _ in range(KT)]
    return level


def second_xn(n):
    level = n.open(KT * 1024, F32R)
    assert level == n.base
    n.xa = n.xn
    n.xn = [n.pair() for _ in range(KT)]


def ffn(n, w_gu, w_dn, norm, nxt_gain):
    level = len(n.stack)
    spare = list(n.xa) if level > n.base else []
    n.open((FF - len(spare)) * 1024, F32R)
    hid = spare + [n.pair() for _ in range(FF - len(spare))]
    n.open(2048)
    sgs = Pool([n.buf(512) for _ in range(4)])
    xt = norm.xt
    r, tr = norm.rms()
    ht = []
    for m in range(FF):
        w, wt, ws = n.weights(w_gu[m], 2048)
        w = views(w, "p (g k c) -> p g k c", g=2, k=KT)
        gb, g, gf = n.banks.take()
        ub, u, uf = n.banks.take()
        tg = n.group3(g[:, :], [(at(w, 0, k), n.xn[k], xt[k]) for k in range(KT)], wt, gf)
        tu = n.group3(u[:, :], [(at(w, 1, k), n.xn[k]) for k in range(KT)], uf)
        n.done(ws, tu)
        i, sg, sf = sgs.take()
        t = n.dve(lambda e: e.tensor_tensor(sg, g[:, :], r, ALU.mult), tg, tr, sf)
        n.banks.put(gb, t)
        ta = n.act(lambda e: e.activation(sg, sg, ACT.Silu), t)
        j, up, pf = sgs.take()
        t = n.dve(lambda e: e.tensor_tensor(up, u[:, :], r, ALU.mult), tu, pf)
        n.banks.put(ub, t)
        t = n.dve(lambda e: e.tensor_tensor(sg, sg, up, ALU.mult), ta, t)
        sgs.put(j, t)
        th, tl = n.rsplit(sg, hid[m], t)
        sgs.put(i, th, tl)
        ht.append([th, tl])
    n.rstd_free = t
    nxt = Norm(n, nxt_gain, n.xn, tu)
    for m in range(KT):
        b, bank, bf = n.banks.take()
        for half in range(2):
            w, wt, ws = n.weights(w_dn[m, :, half * 1408:(half + 1) * 1408], 1408)
            w = views(w, "p (k c) -> p k c", k=11)
            for k in range(11):
                for z, (l, r) in enumerate(((0, 0), (0, 1), (1, 0))):
                    first, last = half == 0 and k == 0 and z == 0, half == 1 and k == 10 and z == 2
                    tok = n.pe(lambda e: e.matmul(bank[:, :], w[l][:, k, :], hid[half * 11 + k][r], start=first, stop=last),
                               bf, wt, ht[half * 11 + k], mark=(k == 10 and z == 2))
            n.done(ws, tok)
        nxt.flush()
        t = n.dve(lambda e, m=m, bank=bank: e.scalar_tensor_tensor(out=n.h[m], in0=bank[:, :], scalar=0.5, in1=n.h[m],
                                                                 op0=ALU.mult, op1=ALU.add), tok)
        n.banks.put(b, t)
        nxt.add(n.h[m], t)
        n.ht[m] = t
    n.close(level)
    return nxt


def each(f, w):
    return tuple(f(p) for p in w) if isinstance(w, tuple) else f(w)


def views(w, pattern, **sizes):
    return each(lambda p: p.rearrange(pattern, **sizes), w)


def at(w, *ix):
    return each(lambda p: p[:, ix[0], :] if len(ix) == 1 else p[:, ix[0], ix[1], :], w)


def cols(w, c):
    return each(lambda p: p[:, c], w)


def out_proj(n, wsrc, rhs, toks, gain=None):
    nxt = Norm(n, gain, n.xn)
    for m2 in range(4):
        w, wt, ws = n.weights(wsrc[m2], 2048)
        w = views(w, "p (a k c) -> p a k c", a=2, k=KT)
        for a in range(2):
            m = 2 * m2 + a
            b, bank, bf = n.banks.take()
            tok = n.group3(bank[:, :], [(at(w, a, k), rhs[k], toks[k]) for k in range(KT)], wt, bf)
            nxt.flush()
            t = n.dve(lambda e, m=m, bank=bank: e.tensor_tensor(n.h[m], bank[:, :], n.h[m], ALU.add), tok)
            n.banks.put(b, t)
            nxt.add(n.h[m], t)
            n.ht[m] = t
        n.done(ws, tok)
    return nxt


def by_token(n, r, tr):
    rT = n.buf(8)
    b, bank, bf = n.banks.take()
    b2, bank2, bf2 = n.banks.take()
    for i in range(4):
        tok = n.transpose(bank[:, i * P:(i + 1) * P], r[:, i * P:(i + 1) * P], tr, bf)
    for i in range(4):
        tok = n.transpose(bank2[:, i * P:(i + 1) * P], r.rearrange("p (m r) -> p r m", r=4)[:, i, :], tr, bf2)
    first = lambda x: x[:, :].rearrange("p (i c) -> p i c", i=4)[:, :, 0]
    n.dve(lambda e: e.tensor_copy(rT[:, 0:4], first(bank)), tok)
    t = n.dve(lambda e: e.tensor_copy(rT[:, 4:8], first(bank2)), tok)
    n.banks.put(b, t)
    n.banks.put(b2, t)
    return rT, t


def rope(n, raw, rawt, rot, cos, sin, tmps, dst, *waits):
    b, bank, bf = n.banks.take()
    tr = n.group(bank[:, :], [(rot, raw)], rawt, bf)
    i, tmp, tf = tmps.take()
    t1 = n.pool(lambda e: e.tensor_tensor(dst, raw, cos, ALU.mult), rawt, *waits)
    t2 = n.dve(lambda e: e.tensor_tensor(tmp, bank[:, :], sin, ALU.mult), tr, tf, *waits)
    n.banks.put(b, t2)
    t = n.dve(lambda e: e.tensor_tensor(dst, dst, tmp, ALU.add), t1, t2)
    tmps.put(i, t)
    return t, [tr, t1]


def heads_fm(n, blocks, xt, use):
    m, rest = 0, None
    for src, cnt in blocks:
        w, wt, ws = n.weights(src, cnt * 1024)
        w = views(w, "p (a k c) -> p a k c", a=cnt, k=KT)
        for a in range(cnt):
            b, bank, bf = n.banks.take()
            tok = n.group3(bank[:, :], [(at(w, a, k), n.xn[k], xt[k]) for k in range(KT)], wt, bf)
            if rest:
                rest()
            t, rest = use(m, bank, tok)
            n.banks.put(b, t)
            m += 1
        n.done(ws, tok)
    if rest:
        rest()


def values_tm(n, src, cols, xt, sel, dst, scale=None):
    w, wt, ws = n.weights(src, KT * cols)
    w = views(w, "p (k c) -> p k c", k=KT)
    toks = []
    for i in range(4):
        b, bank, bf = n.banks.take()
        tok = n.group3(bank[:, 0:cols], [(each(lambda x: sel(x, i), n.xn[k]), at(w, k), xt[k]) for k in range(KT)], wt, bf)
        if scale is None:
            t = n.act(lambda e: e.activation(dst(i), bank[:, 0:cols], ACT.Copy), tok)
        else:
            t = n.act(lambda e: e.activation(dst(i), bank[:, 0:cols], ACT.Copy, scale=scale[0](i)), tok, scale[1])
        n.banks.put(b, t)
        toks.append(t)
    n.done(ws, tok)
    return toks


ATT_FLOATS = lambda width, queries=1: 6 * width + 80 + 3 * P + 2 * PADS * queries * P
PADS = 2


class Attention:

    def __init__(self, n, width, queries=1):
        self.n = n
        self.sc = Pool([n.buf(width) for _ in range(4)])
        self.pt = Pool([n.buf(width) for _ in range(2)])
        self.st = Pool([n.buf(8) for _ in range(10)])
        self.ot = Pool([n.buf(P) for _ in range(3)])
        self.toks = []
        pads = [[n.buf(queries * P) for _ in range(PADS)] for _ in range(2)]
        for x in pads[0] + pads[1]:
            tz = n.pool(lambda e: e.memset(x, 0.0))
        self.pads = [Pool(x) for x in pads]
        n.pool.wait(tz)

    def run(self, units):
        steps = [self.padded, self.scores, self.biased, self.exps, self.scaled, self.turned, self.copied, self.values, self.stored, self.flipped,
                 self.written]
        units = [dict(u) for u in units]
        for t in range(len(units) + len(steps) - 1):
            for s in range(len(steps) - 1, -1, -1):
                if 0 <= t - s < len(units):
                    steps[s](units[t - s])

    def padded(self, u):
        n = self.n
        i, pad, free = self.pads[u["par"]].take()
        ps = slice(u["par"] * 64, u["par"] * 64 + 64)
        u["pad"] = (i, pad)
        for j, q in enumerate(u["q"]):
            t = n.pool(lambda e: e.tensor_copy(pad[ps, j * P:(j + 1) * P], q), u["waits"], free, n.pool.now())
        u["tq"] = t

    def scores(self, u):
        n = self.n
        u["sb"] = []
        if "before" in u:
            u["before"]()
        i, pad = u["pad"]
        j = 0
        for part in u["keys"]:
            b, bank, bf = n.banks.take()
            off = 0
            for kap in part:
                w = kap.shape[-1]
                q = pad[:, j * P:(j + 1) * P]
                tok = n.pe(lambda e: e.matmul(bank[:, off:off + w], q, kap, start=True, stop=True), bf, u["waits"], u["tq"])
                off += w
                j += 1
            u["sb"].append((b, bank, off, tok))
        self.pads[u["par"]].put(i, tok)

    def biased(self, u):
        n = self.n
        u["sci"], sc, scf = self.sc.take()
        u["sti"], st, stf = self.st.take()
        u["sc"], u["st"] = sc, st
        off = 0
        u["first"] = []
        for j, (b, bank, w, tok) in enumerate(u["sb"]):
            o = sc[:, off:off + w]
            m = st[:, j:j + 1]
            if u["mask"] is None:
                t = n.dve(lambda e: e.tensor_reduce(m, bank[:, 0:w], AX_X, ALU.max), tok, scf, stf)
                u["raw"] = (b, bank, t)
            else:
                init = u["sink"] if j == 0 and u["sink"] is not None else (st[:, j - 1:j] if j else -3e38)
                prev = u["first"][-1] if j else None
                t = n.dve(lambda e, o=o, bank=bank, w=w, m=m, j=j, init=init: e.tensor_tensor_reduce(
                    o, bank[:, 0:w], u["mask"][j], 1.0, init, ALU.add, ALU.max, m), tok, scf, stf, prev, u["waits"])
                n.banks.put(b, t)
            u["first"].append(t)
            off += w
        u["w"] = off
        j = len(u["sb"]) - 1
        u["t"] = n.dve(lambda e: e.tensor_scalar(st[:, 2:3], st[:, j:j + 1], -1.0, None, ALU.mult), u["first"])

    def exps(self, u):
        n = self.n
        sc, st, w = u["sc"], u["st"], u["w"]
        src = sc[:, 0:w] if u["mask"] is not None else u["raw"][1][:, 0:w]
        u["te"] = n.act(lambda e: e.activation(sc[:, 0:w], src, ACT.Exp, bias=st[:, 2:3], accum_out=st[:, 3:4]),
                        u["t"])
        if u["mask"] is None:
            n.banks.put(u["raw"][0], u["te"])
        if u["sink"] is not None:
            u["ts"] = n.act(lambda e: e.activation(st[:, 5:6], u["sink"], ACT.Exp, bias=st[:, 2:3]), u["t"])

    def scaled(self, u):
        n = self.n
        st = u["st"]
        t = u["te"]
        if u["sink"] is not None:
            t = n.dve(lambda e: e.tensor_tensor(st[:, 3:4], st[:, 3:4], st[:, 5:6], ALU.add), t, u["ts"])
        u["tr"] = n.dve(lambda e: e.reciprocal(st[:, 4:5], st[:, 3:4]), t)

    def turned(self, u):
        n = self.n
        sc = u["sc"]
        nb = u["w"] // P
        u["tb"] = []
        for g in range(0, nb, 4):
            b, bank, bf = n.banks.take()
            c = min(4, nb - g)
            for j in range(c):
                tok = n.transpose(bank[:, j * P:(j + 1) * P], sc[:, (g + j) * P:(g + j + 1) * P], u["te"], bf,
                                  mark=(j == c - 1))
            u["tb"].append((b, bank, c, tok))
        self.sc.put(u["sci"], tok)

    def copied(self, u):
        n = self.n
        u["pti"], pt, pf = self.pt.take()
        u["pt"] = pt
        off = 0
        u["tc"] = []
        for b, bank, c, tok in u["tb"]:
            w = c * P
            t = n.act(lambda e, off=off, w=w, bank=bank: e.activation(pt[:, off:off + w], bank[:, 0:w], ACT.Copy),
                      tok, pf)
            n.banks.put(b, t)
            u["tc"].append(t)
            off += w

    def values(self, u):
        n = self.n
        b, bank, bf = n.banks.take()
        o = bank[:, 0:64]
        tok = n.group(o, [(u["pt"][:, j * P:(j + 1) * P], v) for j, v in enumerate(u["v"])], bf, u["tc"], u["waits"])
        self.pt.put(u["pti"], tok)
        u["pv"] = (b, o, tok)

    def stored(self, u):
        n = self.n
        b, o, tok = u["pv"]
        if u["par"] == 0:
            self.open_tile = self.ot.take()
            self.first_half = None
        i, ot, free = self.open_tile
        u["ot"] = (i, ot)
        t = n.dve(lambda e: e.tensor_scalar(ot[:, u["par"] * 64:u["par"] * 64 + 64], o, u["st"][:, 4:5], None, ALU.mult),
                  tok, u["tr"], free)
        n.banks.put(b, t)
        self.st.put(u["sti"], t)
        u["th"] = [t, self.first_half]
        self.first_half = t

    def flipped(self, u):
        if u["par"] == 0:
            return
        n = self.n
        i, ot = u["ot"]
        b, bank, bf = n.banks.take()
        tok = n.transpose(bank[:, 0:P], ot, u["th"], bf)
        self.ot.put(i, tok)
        u["fl"] = (b, bank, tok)

    def written(self, u):
        if u["par"] == 0:
            return
        n = self.n
        b, bank, tok = u["fl"]
        if isinstance(u["out"], tuple):
            t = list(n.rsplit(bank[:, 0:P], u["out"], tok))
        else:
            t = [n.act(lambda e: e.activation(u["out"], bank[:, 0:P], ACT.Copy), tok)]
        n.banks.put(b, t)
        self.toks += t


def ab_mixer(n, norm):
    ins = n.ins
    n.open(14336)
    qa = [n.buf(512) for _ in range(6)]
    ka = [n.buf(512) for _ in range(2)]
    va = n.buf(1024).rearrange("p (i c) -> p i c", i=4)
    qb = [n.buf(512) for _ in range(6)]
    kb = [n.buf(512) for _ in range(6)]
    vb = n.buf(3072).rearrange("p (g i c) -> p g i c", g=3, i=4)
    n.open(384 + 2048 + 256 + 12)
    ma = n.buf(384)
    mb1 = n.buf(2048)
    mb23 = n.buf(256)
    sink = n.buf(12)
    inner = n.open(5 * 512 + 8)
    cos, sin = n.buf(512), n.buf(512)
    raws = Pool([n.buf(512) for _ in range(2)])
    tmps = Pool([n.buf(512) for _ in range(1)])
    bar = n.barrier()
    tl = n.load([(cos, ins["rope1"][0]), (sin, ins["rope1"][1])], bar)
    tm = n.load([(ma, ins["mask_a"]), (mb1, ins["mask_b1"]), (mb23, ins["mask_b23"]),
                 (sink, ins["sink_a"].to_broadcast([P, 12]))], bar)
    xt = norm.xt
    r, tr = norm.rms()
    dsts = qa + ka + qb + kb
    rt = {}

    def use(m, bank, tok):
        i, raw, rf = raws.take()
        scale = 0.125 if m < 6 or 8 <= m < 14 else 1.0
        t = n.dve(lambda e: e.scalar_tensor_tensor(out=raw, in0=bank[:, :], scalar=scale, in1=r, op0=ALU.mult, op1=ALU.mult),
                  tok, tr, rf)

        def rest():
            done, reads = rope(n, raw, t, n.rot1, cos, sin, tmps, dsts[m], tl)
            raws.put(i, done, *reads)
            rt[m] = done

        return t, rest

    heads_fm(n, [(ins["w_ab_qk"][j], 2) for j in range(10)], xt, use)
    rT, trT = by_token(n, r, tr)
    tv = values_tm(n, ins["w_ab_v"][0], 256, xt, lambda x, i: x[:, i * P:(i + 1) * P], lambda i: va[:, i, :],
                   (lambda i: rT[:, i:i + 1], trT))
    tvb = []
    for g in range(3):
        if g == 0:
            sel = lambda x, i: x[:, i * P:(i + 1) * P]
        else:
            sel = lambda x, i: x.rearrange("p (m r) -> p r m", r=4)[:, i, :]
        tvb += values_tm(n, ins["w_ab_v"][1 + g], 256, xt, sel, lambda i, g=g: vb[:, g, i, :],
                         (lambda i, g=g: rT[:, 4 * (g > 0) + i:4 * (g > 0) + i + 1], trT))
    n.rstd_free = bar = n.close(inner)
    o = n.xn
    n.open(ATT_FLOATS(768, 3))
    tl = tm
    n.att = Attention(n, 768, 3)
    units = []
    for t, pair in enumerate(A_TILES):
        for i in range(4):
            for par, h in enumerate(pair):
                g = h // 3
                ps = slice(par * 64, par * 64 + 64)
                lo, hi = max(0, i - 1), min(4, i + 2)
                ms = P * (lo - i + 1)
                units.append(dict(q=[qa[t][ps, i * P:(i + 1) * P]], keys=[[ka[g // 2][:, lo * P:hi * P]]],
                                  mask=[ma[:, ms:ms + (hi - lo) * P]], sink=sink[:, h:h + 1], par=par,
                                  v=[va[:, j, g * 64:g * 64 + 64] for j in range(lo, hi)],
                                  out=cols(o[t], slice(i * P, (i + 1) * P)), waits=[rt[t], rt[6 + g // 2], tl] + tv))
    cls = lambda ap: ap.rearrange("p (m r) -> p r m", r=4)
    for s2 in range(2):
        for r, par in [(r, par) for r in range(4) for par in range(2)]:
            s = 2 * s2 + par
            ps = slice(par * 64, par * 64 + 64)
            t = [(g * 4 + s) // 2 for g in range(3)]
            units.append(dict(
                q=[cls(qb[t[g]][ps, :])[:, r, :] for g in range(3)],
                keys=[[kb[t[0]]], [cls(kb[t[1]])[:, r, :], cls(kb[t[2]])[:, r, :]]],
                mask=[mb1[:, r * 512:(r + 1) * 512], mb23], sink=None, par=par,
                v=[vb[:, 0, j, s * 64:s * 64 + 64] for j in range(4)] + [vb[:, g, r, s * 64:s * 64 + 64] for g in (1, 2)],
                out=tuple(cls(x)[:, r, :] for x in o[6 + s // 2]),
                waits=[rt[8 + x] for x in t] + [rt[14 + x] for x in t] + [tl] + tvb))
    n.att.run(units)
    n.close(n.base)
    second_xn(n)
    return out_proj(n, ins["w_ab_out"], o, [n.att.toks] * 8, "norm_ffn2_0")


def c_mixer(n, norm):
    ins = n.ins
    n.open(12288)
    q = [n.buf(512) for _ in range(8)]
    k = [n.buf(512) for _ in range(8)]
    v = n.buf(4096).rearrange("p (i c) -> p i c", i=4)
    n.open(1024 + 4096)
    cm = n.buf(1024)
    bias = Pool([n.buf(1024) for _ in range(4)])
    tl = n.load([(cm, ins["mask_c"])], n.barrier())
    inner = n.open(8)
    xt = norm.xt
    r, tr = norm.rms()
    dsts = q + k
    rt = {}

    def use(m, bank, tok):
        rt[m] = n.dve(lambda e: e.scalar_tensor_tensor(out=dsts[m], in0=bank[:, :], scalar=0.125 if m < 8 else 1.0, in1=r,
                                                       op0=ALU.mult, op1=ALU.mult), tok, tr)
        return rt[m], None

    heads_fm(n, [(ins["w_c_qk"][j], 2) for j in range(8)], xt, use)
    bsem = n.sem("s_bias")
    bcount = [0]
    cur = {}

    def fetch(h):
        i, ap, free = bias.take()
        bcount[0] += 16
        want = bcount[0]
        n.sp(lambda e: e.dma_start(ap, ins["rpb"][h]).then_inc(bsem, 16), free, cur.get("last"), tl, mark=False)
        t = n.pool(lambda e: e.tensor_tensor(ap, ap, cm, ALU.add), (bsem, want), tl, n.pool.now())
        cur["last"] = t
        cur[h] = (i, ap, t)

    for h in range(3):
        fetch(h)
    rT, trT = by_token(n, r, tr)
    tv = []
    for g in range(4):
        tv.append(values_tm(n, ins["w_c_v"][g], 256, xt, lambda x, i: x[:, i * P:(i + 1) * P],
                            lambda i, g=g: v[:, i, g * 256:(g + 1) * 256],
                            (lambda i: rT[:, i:i + 1], trT)))
    n.rstd_free = bar = n.close(inner)
    o = n.xn
    n.open(ATT_FLOATS(512))
    att = Attention(n, 512)
    units = []
    for t in range(8):
        for i, par in [(i, par) for i in range(4) for par in range(2)]:
            h = 2 * t + par
            ps = slice(par * 64, par * 64 + 64)
            u = dict(q=[q[t][ps, i * P:(i + 1) * P]], keys=[[k[t]]], sink=None, par=par,
                     v=[v[:, j, h * 64:h * 64 + 64] for j in range(4)], out=cols(o[t], slice(i * P, (i + 1) * P)),
                     mask=[None], waits=[rt[t], rt[8 + t]] + tv[h // 4], hi=(h, i))
            units.append(u)
    real = att.biased
    real_scores = att.scores
    def scores(u):
        h, i = u["hi"]
        if i == 1 and 3 <= h + 2 < 16:
            fetch(h + 2)
        real_scores(u)

    def biased(u):
        h, i = u["hi"]
        bi, ap, t = cur[h]
        u["mask"] = [ap[:, (7 - 2 * i) * 64:(15 - 2 * i) * 64]]
        u["waits"] = u["waits"] + [t]
        real(u)
        if i == 3:
            bias.put(bi, u["t"])

    att.scores, att.biased = scores, biased
    att.run(units)
    n.close(n.base)
    second_xn(n)
    return out_proj(n, ins["w_c_out"], o, [att.toks] * 8, "norm_ffn2_1")


def ple(n, layer, norm):
    ins = n.ins
    level = len(n.stack)
    n.open(2048, F32R)
    pp = [n.pair() for _ in range(2)]
    n.open(2048)
    p = [n.buf(512) for _ in range(2)]
    sgs = Pool([n.buf(512) for _ in range(2)])
    tl = n.load([(p[j], ins["p"][layer, j]) for j in range(2)], n.barrier())
    tp = [n.rsplit(p[j], pp[j], tl) for j in range(2)]
    tl = [list(x) for x in tp]
    xt = norm.xt
    r, tr = norm.rms()
    nxt = Norm(n, None if layer else "norm_ffn1_1", n.xa)
    for m in range(KT):
        w, wt, ws = n.weights(ins["w_ple"][layer, m], 1280)
        w = views(w, "p (k c) -> p k c", k=10)
        gb, g, gf = n.banks.take()
        ub, u, uf = n.banks.take()
        tg = n.group3(g[:, :], [(at(w, k), n.xn[k], xt[k]) for k in range(KT)], wt, gf)
        tu = n.group3(u[:, :], [(at(w, KT + k), pp[k]) for k in range(2)], uf, tl)
        n.done(ws, tu)
        nxt.flush()
        i, sg, sf = sgs.take()
        t = n.dve(lambda e: e.tensor_tensor(sg, g[:, :], r, ALU.mult), tg, tr, sf)
        n.banks.put(gb, t)
        t = n.act(lambda e: e.activation(sg, sg, ACT.Sigmoid), t)
        t = n.dve(lambda e, sg=sg, u=u: e.tensor_tensor(sg, sg, u[:, :], ALU.mult), t, tu)
        n.banks.put(ub, t)
        t = n.dve(lambda e, sg=sg, m=m: e.tensor_tensor(n.h[m], n.h[m], sg, ALU.add), t)
        sgs.put(i, t)
        nxt.add(n.h[m], t)
        n.ht[m] = t
    n.close(n.base)
    n.xn = n.xa
    return nxt


def first_block(n):
    ins = n.ins
    n.ht = [n.load([(n.h[k], ins["x"][k])]) for k in range(KT)]
    norm = Norm(n, "norm_ffn1_0", n.xn)
    n.split_to(0)
    for k in range(KT):
        norm.add(n.h[k], n.ht[k])
        norm.flush()
    n.split_to(1)
    for layer in range(2):
        norm = ffn(n, ins["w_gu"][2 * layer], ins["w_dn"][2 * layer], norm, f"norm_mix_{layer}")
        norm = (ab_mixer if layer == 0 else c_mixer)(n, norm)
        norm = ffn(n, ins["w_gu"][2 * layer + 1], ins["w_dn"][2 * layer + 1], norm, f"norm_ple_{layer}")
        norm = ple(n, layer, norm)
    n.ht = norm.finish("norm_final", n.h)
    return None


def shift_tokens(n, raw, c0, mp, mn, dst, tok, free):
    x, p, q = raw[:, 1:513], raw[:, 0:512], raw[:, 2:514]
    t = n.dve(lambda e: e.tensor_scalar(dst, x, c0, None, ALU.mult), tok, free)
    t = n.dve(lambda e: e.scalar_tensor_tensor(out=dst, in0=p, scalar=mp, in1=dst, op0=ALU.mult, op1=ALU.add), t)
    t = n.dve(lambda e: e.scalar_tensor_tensor(out=dst, in0=q, scalar=mn, in1=dst, op0=ALU.mult, op1=ALU.add), t)
    return t


def rwkv(n):
    ins = n.ins
    v4 = lambda b: b.rearrange("p (a t) -> p a t", a=4)
    Y = n.y_rwkv
    level = n.open(13280)
    R, K = n.buf(2048), n.buf(2048)
    V, KK, BON = (n.buf(2048) for _ in range(3))
    lora = [n.buf(512) for _ in range(3)]
    reset = n.buf(512)
    masks = n.buf(448)
    ptc = v4(n.buf(32))
    state = n.buf(512)
    inner = open_xn(n)
    n.open_parts()
    n.open(4 * 514)
    raws = Pool([n.buf(514) for _ in range(4)])
    bar = n.barrier()
    norm = Norm(n, "norm_mix_2", n.xn)
    for k in range(KT):
        norm.add(n.h[k], n.ht[k])
        norm.flush()
    xt = norm.xt
    n.r, n.tr = norm.rms()
    tl = n.load([(reset, ins["reset"])], bar)
    mp, mn, c0 = n.vec("shift_prev"), n.vec("shift_next"), n.cc[:, 0:15]
    omka = n.cc[:, 15:19]
    vv = lambda name, k: n.vecs[:, VEC[name]:VEC[name] + k]
    t = n.dve(lambda e: e.tensor_tensor(c0, vv("shift_prev", 15), vv("shift_next", 15), ALU.add))
    t = n.dve(lambda e: e.tensor_scalar(c0, c0, -1.0, 1.0, ALU.mult, ALU.add), t)
    tc = n.dve(lambda e: e.tensor_scalar(omka, vv("k_a", 4), -1.0, 1.0, ALU.mult, ALU.add), t)
    tz = []
    for r in raws.items:
        n.pool(lambda e, r=r: e.memset(r[:, 0:1], 0.0))
        tz = n.pool(lambda e, r=r: e.memset(r[:, 513:514], 0.0))
    dsts = [b[:, j * 512:(j + 1) * 512] for b in (R, K, V) for j in range(4)] + lora
    done = {}

    def use(m, bank, tok):
        i, raw, rf = raws.take()
        t = n.dve(lambda e: e.tensor_tensor(raw[:, 1:513], bank[:, :], n.r, ALU.mult), tok, rf, n.tr)
        done[m] = shift_tokens(n, raw, n.cc[:, m:m + 1], n.vec("shift_prev", m), n.vec("shift_next", m), dsts[m],
                               [t, tz, tc], None)
        raws.put(i, done[m])
        return t, (lambda: unit_key(m - 8)) if 8 <= m < 12 else None

    col = lambda b, j: b[:, j * 512:(j + 1) * 512]
    kk_t = []

    def unit_key(j):
        kk, sq = col(KK, j), col(BON, j)
        t = n.act(lambda e: e.activation(kk, col(K, j), ACT.Copy, scale=n.vec("k_k", j)), done[4 + j])
        t = n.act(lambda e: e.activation(sq, kk, ACT.Square), t)
        b, bank, bf = n.banks.take()
        tok = n.group(bank[:, :], [(n.bones, sq)], t, bf)
        t = n.act(lambda e: e.activation(sq, bank[:, :], ACT.Sqrt), tok)
        n.banks.put(b, t)
        t = n.dve(lambda e: e.tensor_scalar(sq, sq, 1e-12, None, ALU.max), t)
        t = n.dve(lambda e: e.reciprocal(sq, sq), t)
        kk_t.append(n.dve(lambda e: e.tensor_tensor(kk, kk, sq, ALU.mult), t))

    heads_fm(n, [(ins["w2_rwkv"][j], 2) for j in range(7)] + [(ins["w2_rwkv1"], 1)], xt, use)
    t_wd = n.act(lambda e: e.activation(lora[0], lora[0], ACT.Tanh), done[12])
    t_gd = n.act(lambda e: e.activation(lora[2], lora[2], ACT.Sigmoid), done[14])
    n.close(inner)
    n.parts = None
    n.open(8192 + 24 * 512)
    AL, RT, BT, KTL = (n.buf(2048) for _ in range(4))
    work = n.top
    ct = lambda b: b.rearrange("p (c t) -> p c t", t=64)
    T = range(4)
    for d in range(2):
        n.top = work
        lw, av, C, X, P1, IP = ([n.buf(512) for _ in T] for _ in range(6))
        bar = n.barrier()
        tm = n.load([(masks, ins["mask_r"][d])], bar)
        w, wt, ws = n.weights(ins["lora"][d], 1024)
        low = []
        for z in range(2):
            for j in T:
                b, bank, bf = n.banks.take()
                c = slice(z * 512 + j * 128, z * 512 + (j + 1) * 128)
                low.append((b, bank, n.group(bank[:, :], [(w[:, c], lora[z])], wt, t_wd, bf)))
        n.done(ws, low[7][2])
        ts, ta = [], []
        for z, (dst, toks, bias) in enumerate(((lw, ts, f"w0_{d}"), (av, ta, f"a0_{d}"))):
            for j in T:
                b, bank, tok = low[4 * z + j]
                toks.append(n.act(lambda e: e.activation(dst[j], bank[:, :], ACT.Sigmoid, bias=n.vec(bias, j)), tok))
                n.banks.put(b, toks[j])
        dec = float(np.exp(-0.5))
        tC = [n.dve(lambda e: e.tensor_tensor_scan(C[j], reset, lw[j], 0.0, ALU.mult, ALU.add), ts[j], tl) for j in T]
        if d == 0:
            tX = [n.dve(lambda e: e.tensor_tensor(X[j], C[j], lw[j], ALU.subtract), tC[j]) for j in T]
            ti = tC
        else:
            tX = [n.dve(lambda e: e.tensor_tensor(ct(X[j]), ct(C[j])[:, :, 63:64].to_broadcast([P, 8, 64]), ct(C[j]),
                                                  ALU.subtract), tC[j]) for j in T]
            ti = [n.dve(lambda e: e.tensor_tensor(C[j], X[j], lw[j], ALU.add), tX[j]) for j in T]
        end = 63 if d == 0 else 0
        tP, tPe, tIP, t3 = [], [], [], []
        for j in T:
            tP.append(n.act(lambda e: e.activation(P1[j], C[j], ACT.Exp, scale=-dec), ti[j]))
            tPe.append(n.act(lambda e: e.activation(X[j], X[j], ACT.Exp, scale=-dec), tX[j], ti[j]))
            tIP.append(n.act(lambda e: e.activation(IP[j], C[j], ACT.Exp, scale=dec), ti[j]))
        for j in T:
            n.pool(lambda e: e.tensor_copy(ptc[:, j, :], ct(P1[j])[:, :, end]), tP[j])
            (n.pool if j < 2 else n.dve)(lambda e: e.tensor_tensor(col(RT, j), col(R, j), P1[j], ALU.mult), tP[j])
        t4 = [n.dve(lambda e: e.tensor_tensor(lw[j], col(KK, j), av[j], ALU.mult), ta[j], ti[j], tX[j], kk_t) for j in T]
        for j in T:
            n.dve(lambda e: e.scalar_tensor_tensor(out=col(AL, j), in0=col(KK, j), scalar=-1.0, in1=X[j], op0=ALU.mult,
                                                   op1=ALU.mult), tPe[j])
            n.pool(lambda e: e.tensor_tensor(col(BT, j), lw[j], IP[j], ALU.mult), t4[j], tIP[j])
        t5 = [n.act(lambda e: e.activation(av[j], av[j], ACT.Identity, scale=n.vec("k_a", j), bias=n.cc[:, 15 + j:16 + j]),
                    t4[j], tc) for j in T]
        key = av if d else [col(BON, j) for j in T]
        t5 = [n.dve(lambda e: e.tensor_tensor(key[j], av[j], col(K, j), ALU.mult), t5[j], kk_t) for j in T]
        for j in T:
            n.dve(lambda e: e.tensor_tensor(col(KTL, j), key[j], IP[j], ALU.mult), t5[j], tIP[j])
            if d:
                (n.dve if j < 2 else n.pool)(lambda e: e.tensor_tensor(col(BON, j), col(BON, j), av[j], ALU.add), t5[j])
        n.top = work
        chunks(n, d, dict(R=R, V=V, AL=AL, RT=RT, BT=BT, KT=KTL, Y=Y, masks=masks, ptc=ptc, state=state, tm=tm))
    n.top = work
    bar = n.barrier()
    mu, yc, sq, bo = ([n.buf(512) for _ in T] for _ in range(4))
    gw, gwt, gs = n.weights(ins["g2"], 512)

    def sums(src, toks):
        r = []
        for j in T:
            b, bank, bf = n.banks.take()
            r.append((b, bank, n.group(bank[:, :], [(n.bones, src[j])], toks[j], bf)))
        return r

    def read(out, fn, *toks):
        b, bank, tok = out
        t = n.dve(lambda e: fn(e, bank[:, :]), tok, *toks)
        n.banks.put(b, t)
        return t

    Ys = [col(Y, j) for j in T]
    s1 = sums(Ys, [None] * 4)
    tb = [n.pool(lambda e: e.tensor_tensor(bo[j], col(BON, j), col(R, j), ALU.mult)) for j in T]
    tb = [n.act(lambda e: e.activation(bo[j], bo[j], ACT.Copy, scale=n.vec("r_k", j)), tb[j]) for j in T]
    s2 = sums(bo, tb)
    ty = [read(s1[j], lambda e, x: e.scalar_tensor_tensor(out=yc[j], in0=x, scalar=-1.0 / 64, in1=Ys[j], op0=ALU.mult,
                                                          op1=ALU.add)) for j in T]
    t = [n.act(lambda e: e.activation(sq[j], yc[j], ACT.Square), ty[j]) for j in T]
    s3 = sums(sq, t)
    tb = [read(s2[j], lambda e, x: e.tensor_tensor(bo[j], x, col(V, j), ALU.mult)) for j in T]
    t = []
    for b, bank, tok in s3:
        t.append(n.act(lambda e: e.activation(mu[len(t)], bank[:, :], ACT.Sqrt, scale=1.0 / 64, bias=n.eps_y), tok))
        n.banks.put(b, t[-1])
    s4 = []
    for j in T:
        b, bank, bf = n.banks.take()
        s4.append((b, bank, n.group(bank[:, :], [(gw[:, j * 128:(j + 1) * 128], lora[2])], gwt, t_gd, bf)))
    n.done(gs, s4[3][2])
    yt = []
    for j in T:
        tm = n.dve(lambda e: e.reciprocal(mu[j], mu[j]), t[j])
        tm = n.dve(lambda e: e.tensor_tensor(yc[j], yc[j], mu[j], ALU.mult), tm, ty[j])
        tm = n.pool(lambda e: e.tensor_scalar(yc[j], yc[j], n.vec("ln_w", j), n.vec("ln_b", j), ALU.mult, ALU.add), tm)
        tm = n.pool(lambda e: e.tensor_tensor(yc[j], yc[j], bo[j], ALU.add), tm, tb[j])
        yt.append(tm)
    yt = [read(s4[j], lambda e, x: e.tensor_tensor(Ys[j], yc[j], x, ALU.mult), yt[j]) for j in T]
    n.close(level)
    return yt


def chunks(n, d, q):
    NT = 12
    assert n.top + 24 * 512 <= n.stack[-1][2][1]
    bufs = [[n.buf(512) for _ in range(NT)] for _ in range(2)]
    f4 = lambda b: b.rearrange("p (a t) -> p a t", a=4)
    bar = n.barrier()
    last = [None] * 2
    for s in range(2):
        for i in range(4):
            (n.dve if s else n.pool)(lambda e: e.memset(bufs[s][i], 0.0))
    tz = n.pool(lambda e: e.memset(q["state"], 0.0))
    n.barrier()
    Dm = q["masks"][:, 0:128].unsqueeze(1).to_broadcast([P, 4, 128])
    Om = q["masks"][:, 128:256].unsqueeze(1).to_broadcast([P, 4, 128])
    Sm = q["masks"][:, 256:384].unsqueeze(1).to_broadcast([P, 4, 128])
    Im = q["masks"][:, 384:448].unsqueeze(1).to_broadcast([P, 8, 64])
    Id = n.ident.unsqueeze(1).to_broadcast([P, 4, 128])
    ST = q["state"]
    seq = dict(st=tz, y=None)

    def mul4(lhs, rhs, waits, lhs2=None, rhs2=None):
        b, bank, bf = n.banks.take()
        for p in range(4):
            c = slice(p * 128, (p + 1) * 128)
            n.pe(lambda e, c=c: e.matmul(bank[:, c], lhs[:, c], rhs[:, c], start=True, stop=lhs2 is None), bf, waits,
                 mark=False)
            if lhs2 is not None:
                n.pe(lambda e, c=c: e.matmul(bank[:, c], lhs2[:, c], rhs2[:, c], start=False, stop=True), mark=False)
        return b, bank

    def turn4(src, waits):
        b, bank, bf = n.banks.take()
        for p in range(4):
            c = slice(p * 128, (p + 1) * 128)
            n.transpose(bank[:, c], src[:, c], bf, waits, mark=False)
        return b, bank

    def sealed():
        return n.pe.sealed()

    def out_act(pair, dst, *waits):
        b, bank = pair
        t = n.act(lambda e: e.activation(dst, bank[:, :], ACT.Copy), *waits)
        n.banks.put(b, t)
        return t

    def out_dve(pair, dst, *waits):
        b, bank = pair
        t = n.dve(lambda e: e.tensor_copy(dst, bank[:, :]), *waits)
        n.banks.put(b, t)
        return t

    def add_dve(pair, dst, *waits):
        b, bank = pair
        t = n.dve(lambda e: e.tensor_tensor(dst, bank[:, :], dst, ALU.add), *waits)
        n.banks.put(b, t)
        return t

    def s0(u):
        c = u["c"]
        B = u["B"]
        cs = slice(c * 64, (c + 1) * 64)
        prev = last[u["s"]]
        toks = []
        for i, (name, eng) in enumerate((("AL", "p"), ("BT", "p"), ("KT", "a"), ("V", "a"))):
            src = f4(q[name])[:, :, cs]
            dst = B[i].rearrange("p (a h t) -> p a h t", a=4, h=2)
            for h in range(2):
                hs = slice(h * 64, h * 64 + 64)
                if eng == "p":
                    toks.append(n.pool(lambda e, src=src, dst=dst, hs=hs, h=h: e.tensor_copy(dst[hs, :, h, :], src[hs]), prev))
                else:
                    toks.append(n.act(lambda e, src=src, dst=dst, hs=hs, h=h: e.activation(dst[hs, :, h, :], src[hs], ACT.Copy), prev))
        u["t0"] = toks
        r = f4(q["RT"])[:, :, cs]
        u["r"] = r
        m1 = mul4(B[1], B[0], toks)
        m2 = mul4(B[2], B[0], toks)
        b, bank, bf = n.banks.take()
        for z in range(2):
            for p in range(4):
                n.pe(lambda e, z=z, p=p: e.matmul(bank[:, z * 256 + p * 64:z * 256 + p * 64 + 64],
                                                B[1 + z][:, p * 128:(p + 1) * 128], r[:, p, :], start=True, stop=True),
                     bf, mark=False)
        t = sealed()
        w = [t, q["tm"], prev]
        n.dve(lambda e: e.tensor_tensor(f4(B[4]), f4(m1[1][:, :]), Dm, ALU.mult), w)
        ta = n.dve(lambda e: e.tensor_tensor(f4(B[5]), f4(m1[1][:, :]), Om, ALU.mult), w)
        n.banks.put(m1[0], ta)
        tb = n.dve(lambda e: e.tensor_tensor(f4(B[6]), f4(m2[1][:, :]), Sm, ALU.mult), w)
        n.banks.put(m2[0], tb)
        e8 = lambda x: x.rearrange("p (a t) -> p a t", a=8)
        tc = n.dve(lambda e: e.tensor_tensor(e8(B[7]), e8(bank[:, :]), Im, ALU.mult), w)
        n.banks.put(b, tc)
        u["tN"], u["t6"], u["t7"] = ta, tb, tc

    def s1(u):
        B = u["B"]
        a = turn4(B[4], u["tN"])
        b = turn4(B[1], u["t0"])
        k = turn4(B[2], None)
        v = turn4(B[3], None)
        t = sealed()
        u["tA"] = out_dve(a, B[8], t)
        u["tb"] = out_act(b, B[9], t, last[u["s"]])
        u["tk"] = out_act(k, B[10], t)
        u["tv"] = out_act(v, B[11], t)
        u["tP"] = n.dve(lambda e: e.tensor_tensor(f4(B[1]), f4(B[4]), Id, ALU.add), t)

    def s2(u):
        B = u["B"]
        x = mul4(B[8], B[4], [u["tA"]])
        y = mul4(B[4], B[8], None)
        t = sealed()
        u["tx"] = out_act(x, B[2], t)
        u["ty"] = out_dve(y, B[3], t)

    def s3(u):
        B = u["B"]
        x = mul4(B[3], B[2], [u["tx"], u["ty"]])
        y = mul4(B[2], B[3], None)
        p = mul4(B[3], B[1], [u["tP"]])
        t = sealed()
        u["tx"] = out_act(x, B[4], t)
        u["ty"] = out_act(y, B[8], t)
        u["tP"] = add_dve(p, B[1], t)

    def s4(u):
        B = u["B"]
        y = mul4(B[4], B[8], [u["tx"], u["ty"]])
        p = mul4(B[8], B[1], [u["tP"]])
        t = sealed()
        u["ty"] = out_act(y, B[2], t)
        u["tP"] = add_dve(p, B[1], t)

    def s5(u):
        B = u["B"]
        p = mul4(B[2], B[1], [u["ty"], u["tP"]])
        u["tP"] = add_dve(p, B[1], sealed())

    def s6(u):
        B = u["B"]
        p = turn4(B[1], [u["tP"]])
        u["tPT"] = out_act(p, B[3], sealed())

    def s7(u):
        B = u["B"]
        z = mul4(B[3], B[5], [u["tPT"]])
        y = mul4(B[5], B[3], None)
        t = sealed()
        u["tx"] = out_act(z, B[4], t)
        u["ty"] = out_dve(y, B[8], t)

    def s8(u):
        B = u["B"]
        y = mul4(B[4], B[8], [u["tx"], u["ty"]])
        u["tz"] = out_act(y, B[2], sealed())

    def s9(u):
        B = u["B"]
        p = mul4(B[2], B[1], [u["tz"], u["tP"]])
        u["tP"] = add_dve(p, B[1], sealed())

    def s10(u):
        B = u["B"]
        p = mul4(B[8], B[1], [u["tP"], u["ty"]])
        u["tP"] = add_dve(p, B[1], sealed())

    def s11(u):
        B = u["B"]
        x = mul4(B[0], ST, [seq["st"], u["t6"], u["tv"], u["t0"]], B[6], B[11])
        u["tX"] = out_act(x, B[3], sealed())

    def s12(u):
        B = u["B"]
        x = mul4(B[1], B[3], [u["tX"], u["tP"]])
        u["tU"] = out_dve(x, B[5], sealed())

    def s13(u):
        B, c = u["B"], u["c"]
        waits = [u["tU"], u["tb"], u["tk"], u["tv"], u["t7"], seq["st"]]
        x = mul4(B[9], B[5], waits, B[10], B[11])
        b, bank, bf = n.banks.take()
        for p in range(4):
            c2 = slice(p * 128, (p + 1) * 128)
            o = bank[:, p * 64:(p + 1) * 64]
            prods = [(ST[:, c2], u["r"][:, p, :]), (B[5][:, c2], B[7][:, p * 64:(p + 1) * 64]),
                     (B[11][:, c2], B[7][:, 256 + p * 64:256 + (p + 1) * 64])]
            for j, (l, r) in enumerate(prods):
                n.pe(lambda e, o=o, l=l, r=r, j=j: e.matmul(o, l, r, start=(j == 0), stop=(j == 2)), bf, waits, mark=False)
        t = sealed()
        ta = n.dve(lambda e: e.tensor_tensor(ST, x[1][:, :], ST, ALU.add), t)
        n.banks.put(x[0], ta)
        pt = q["ptc"][:, :, c:c + 1].to_broadcast([P, 4, 128])
        seq["st"] = n.dve(lambda e: e.tensor_tensor(f4(ST), f4(ST), pt, ALU.mult), ta)
        y = f4(q["Y"])[:, :, c * 64:(c + 1) * 64]
        ps = bank[:, 0:256].rearrange("p (a t) -> p a t", a=4)
        if d == 0:
            ty = n.act(lambda e: e.activation(y, ps, ACT.Copy), t)
        else:
            ty = n.dve(lambda e: e.tensor_tensor(y, ps, y, ALU.add), t)
        n.banks.put(b, ty)
        last[u["s"]] = [t]

    steps = [s0, s1, s2, s3, s4, s5, s6, s7, s8, s9, s10, s11, s12, s13]
    order = range(8) if d == 0 else range(7, -1, -1)
    units = [dict(c=c, s=i % 2, B=bufs[i % 2]) for i, c in enumerate(order)]
    L = 7
    for tau in range(L * (len(units) - 1) + len(steps)):
        for i in range(len(units)):
            s = tau - L * i
            if 0 <= s < len(steps):
                steps[s](units[i])


def pool_branch(n, xt):
    ins = n.ins
    a = Pool([n.buf(528) for _ in range(2)])
    bufs = [n.buf(528) for _ in range(2)]
    icnt = n.buf(2048)
    pooled = [n.buf(512) for _ in range(4)]
    bar = n.barrier()
    tl = n.load([(icnt, ins["icnt"])], bar)
    tz = None
    for r in a.items:
        n.pool(lambda e, r=r: e.memset(r[:, 0:8], 0.0))
        tz = n.pool(lambda e, r=r: e.memset(r[:, 520:528], 0.0))
    w, wt, ws = n.weights(ins["pool_w"], 512)
    out = []

    def use(m, bank, tok):
        i, z, zf = a.take()
        tz1 = n.dve(lambda e: e.tensor_tensor(z[:, 8:520], bank[:, :], n.r, ALU.mult), tok, zf, n.tr)
        wd = (2, 4, 8, 16)[m]
        src, ln, t = z, 528, [tz1, tz]
        for s in range(m + 1):
            st = 1 << s
            ln -= st
            dst = bufs[s % 2]
            t = n.dve(lambda e, src=src, dst=dst, st=st, ln=ln: e.tensor_tensor(dst[:, 0:ln], src[:, 0:ln], src[:, st:st + ln],
                                                                              ALU.add), t)
            src = dst
        x0 = 8 - wd // 2
        t = n.dve(lambda e, src=src: e.tensor_tensor(pooled[m], src[:, x0:x0 + 512], icnt[:, m * 512:(m + 1) * 512], ALU.mult), t, tl)
        t = n.dve(lambda e: e.tensor_tensor(pooled[m], pooled[m], z[:, 8:520], ALU.subtract), t)
        a.put(i, t)
        out.append(t)
        return tz1, None

    heads_fm(n, [(ins["w2_pool"][j], 2) for j in range(2)], xt, use)
    toks = []
    for m in range(4):
        b, bank, bf = n.banks.take()
        tok = n.group(bank[:, :], [(w[:, m * 128:(m + 1) * 128], pooled[m])], wt, out[m], bf)
        y = pooled[m]
        t = n.dve(lambda e: e.tensor_scalar(y, bank[:, :], n.vec("pool_scale", m), None, ALU.mult), tok)
        n.banks.put(b, t)
        toks.append(list(n.rsplit(y, n.y_pool[m], t)))
    n.done(ws, tok)
    return toks


def axial_attention(n, xt):
    ins = n.ins
    n.open(3072)
    q = [n.buf(512) for _ in range(4)]
    k = n.buf(512)
    v = n.buf(512).rearrange("p (i c) -> p i c", i=4)
    inner = n.open(4096 + 8)
    cos, sin = n.buf(512), n.buf(512)
    raws = Pool([n.buf(512) for _ in range(2)])
    tmps = Pool([n.buf(512) for _ in range(2)])
    rs = Pool([n.buf(512) for _ in range(2)])
    bar = n.barrier()
    tl = n.load([(cos, ins["rope2"][0]), (sin, ins["rope2"][1])], bar)
    dsts = q + [k]
    rt = {}

    def use(m, bank, tok):
        i, raw, rf = raws.take()
        j, r, rrf = rs.take()
        t0 = n.dve(lambda e: e.tensor_tensor(raw, bank[:, :], n.r, ALU.mult), tok, rf, n.tr)
        ts = n.act(lambda e: e.activation(r, raw, ACT.Square), t0, rrf)

        def rest():
            if m:
                turn()
            b, bk, bf = n.banks.take()
            tk = n.group(bk[:, :], [(n.bones, r)], ts, bf)
            t = n.act(lambda e: e.activation(r, bk[:, :], ACT.Sqrt, scale=1.0 if m < 4 else 1.0 / 64,
                                             bias=n.eps_q if m < 4 else n.eps), tk)
            n.banks.put(b, t)
            t = n.dve(lambda e: e.reciprocal(r, r), t)
            g = n.vec("q_norm" if m < 4 else "k_norm")
            t = n.dve(lambda e: e.scalar_tensor_tensor(out=raw, in0=raw, scalar=g, in1=r, op0=ALU.mult, op1=ALU.mult), t)
            rs.put(j, t)
            normed.append((m, i, raw, t))
            if m == 4:
                turn()

        return t0, rest

    normed = []

    def turn():
        m, i, raw, t = normed.pop()
        done, reads = rope(n, raw, t, n.rot2, cos, sin, tmps, dsts[m], tl)
        raws.put(i, done, *reads)
        rt[m] = done

    heads_fm(n, [(ins["w2_att"][0], 2), (ins["w2_att"][1], 2), (ins["w2_att1"], 1)], xt, use)
    rT, trT = by_token(n, n.r, n.tr)
    tv = values_tm(n, ins["w2_attv"], 128, xt, lambda x, i: x[:, i * P:(i + 1) * P], lambda i: v[:, i, :],
                   (lambda i: rT[:, i:i + 1], trT))
    n.close(inner)
    n.open(ATT_FLOATS(512))
    att = Attention(n, 512)
    units = []
    for t, pair in enumerate(ATT_TILES):
        for i in range(4):
            for par in range(2):
                ps = slice(par * 64, par * 64 + 64)
                units.append(dict(q=[q[t][ps, i * P:(i + 1) * P]], keys=[[k]], mask=None, sink=None, par=par,
                                  v=[v[:, j, par * 64:par * 64 + 64] for j in range(4)],
                                  out=cols(n.y_att[t], slice(i * P, (i + 1) * P)), waits=[rt[t], rt[4]] + tv))
    att.run(units)
    return att.toks


def merge(n, xt, yt, pt, ct):
    n.open(4096, F32R)
    yr = [n.pair() for _ in range(4)]
    n.open(11 * 512)
    sgs = Pool([n.buf(512) for _ in range(3)])
    mg = [n.buf(512) for _ in range(KT)]
    yt = [list(n.rsplit(n.y_rwkv[:, j * 512:(j + 1) * 512], yr[j], yt[j])) for j in range(4)]
    ys = [(yr, yt), (n.y_pool, pt), (n.y_att, [ct] * 4)]
    mt = []
    for m in range(KT):
        for z in range(3):
            w, wt, ws = n.weights(n.ins["w2_gate"][m, z], 1536)
            w = views(w, "p (k c) -> p k c", k=12)
            gb, g, gf = n.banks.take()
            ub, u, uf = n.banks.take()
            tg = n.group3(g[:, :], [(at(w, k), n.xn[k], xt[k]) for k in range(KT)], wt, gf)
            tu = n.group3(u[:, :], [(at(w, KT + k), ys[z][0][k], ys[z][1][k]) for k in range(4)], uf)
            n.done(ws, tu)
            i, sg, sf = sgs.take()
            t = n.rstd_free = n.dve(lambda e: e.tensor_tensor(sg, g[:, :], n.r, ALU.mult), tg, sf)
            n.banks.put(gb, t)
            t = n.act(lambda e: e.activation(sg, sg, ACT.Sigmoid), t)
            if z == 0:
                t = n.dve(lambda e, m=m, sg=sg, u=u: e.tensor_tensor(mg[m], sg, u[:, :], ALU.mult), t, tu)
                n.banks.put(ub, t)
                ta = t
            else:
                t = n.dve(lambda e, sg=sg, u=u: e.tensor_tensor(sg, sg, u[:, :], ALU.mult), t, tu)
                n.banks.put(ub, t)
                t = ta = n.dve(lambda e, m=m, sg=sg: e.tensor_tensor(mg[m], mg[m], sg, ALU.add), t, ta)
            sgs.put(i, t)
        mt.append(ta)
    mt = [list(n.rsplit(mg[m], n.xn[m], mt[m], tg)) for m in range(KT)]
    return out_proj(n, n.ins["w2_out"], n.xn, mt)


def experts(n, norm):
    ins = n.ins
    router = n.buf(128)
    iota = n.buf(64)
    slotcol = n.buf(1)
    sels = n.buf(1024)
    small = n.buf(4 * 16 * 4 + 16)
    affT, work, slotT, eq = (n.buf(512) for _ in range(4))
    mx8 = n.buf(8)
    ones5 = n.buf(512)
    big = n.buf(8192)
    hn_tok = big[:, 0:4096].rearrange("p (i f) -> p i f", i=4)
    G = big[:, 4096:8192].rearrange("p (i s) -> p i s", i=4)
    ys = [big[:, i * 1024:(i + 1) * 1024] for i in range(8)]
    xg = n.buf(8192).rearrange("p (k s) -> p k s", k=KT)
    gv = [n.buf(512) for _ in range(8)]
    hids = Pool([n.buf(1024) for _ in range(1)])
    hidTs = Pool([n.buf(1024) for _ in range(2)])
    n.add_slots(2)
    bar = n.barrier()
    tl = n.load([(router, ins["router"]), (iota, ins["iota"]), (slotcol, ins["slotcol"]), (sels, ins["sels"])], bar)
    n.pool(lambda e: e.memset(affT, 0.0))
    n.pool(lambda e: e.memset(slotT, 0.0))
    to = n.pool(lambda e: e.memset(ones5, 1.0))
    n.dve.wait(to)
    xt = norm.finish("norm_ffn_2", n.xn)
    b, bank, bf = n.banks.take()
    for i in range(4):
        t = n.group(bank[:, i * 16:(i + 1) * 16],
                    [(n.xn[k][:, i * P:(i + 1) * P], router[:, k * 16:(k + 1) * 16], xt[k]) for k in range(KT)], tl, bf)
    l3 = bank[:, 0:64].rearrange("p (i e) -> p i e", i=4)
    aff = small[:, 0:64].rearrange("p (i e) -> p i e", i=4)
    slot = small[:, 64:128].rearrange("p (i e) -> p i e", i=4)
    m4, s4 = small[:, 128:132], small[:, 132:136]
    t1 = n.dve(lambda e: e.tensor_reduce(m4, l3, AX_X, ALU.max), t)
    t = n.dve(lambda e: e.tensor_tensor(aff, l3, m4.unsqueeze(2).to_broadcast([P, 4, 16]), ALU.subtract), t1)
    n.banks.put(b, t)
    t = n.act(lambda e: e.activation(aff, aff, ACT.Exp), t)
    t = n.dve(lambda e: e.tensor_reduce(s4, aff, AX_X, ALU.add), t)
    t = n.dve(lambda e: e.reciprocal(s4, s4), t)
    t_aff = n.dve(lambda e: e.tensor_tensor(aff, aff, s4.unsqueeze(2).to_broadcast([P, 4, 16]), ALU.mult), t)
    b, bank, bf = n.banks.take()
    for i in range(4):
        tok = n.transpose(bank[0:16, i * P:(i + 1) * P], aff[:, i, :], t_aff, bf)
    tT = n.dve(lambda e: e.tensor_copy(affT[0:16], bank[0:16, :]), tok)
    n.banks.put(b, tT)
    for i in range(4):
        for half in range(2):
            b, bank, bf = n.banks.take()
            for j in range(4):
                k = 4 * half + j
                tok = n.transpose(bank[:, j * P:(j + 1) * P], n.xn[k][:, i * P:(i + 1) * P], bf, xt[k], mark=(j == 3))
            th = n.act(lambda e, i=i, half=half, bank=bank: e.activation(hn_tok[:, i, half * 512:(half + 1) * 512], bank[:, :],
                                                                      ACT.Copy), tok)
            n.banks.put(b, th)
    for z in range(2):
        n.add_slot(n.xn_all[:, z * SLOT:(z + 1) * SLOT], tok)
    n.fetch()
    tv = []
    for i in range(8):
        b, bank, bf = n.banks.take()
        tok = n.group(bank[:, :], [(sels[:, i * P:(i + 1) * P], affT)], bf, tT, tl)
        tv.append(n.act(lambda e: e.activation(gv[i], bank[:, :], ACT.Copy), tok))
        n.banks.put(b, tv[i])
    t = tT
    for r in range(8):
        src = affT if r == 0 else work
        t = n.dve(lambda e, src=src: e.max(mx8[0:16], src[0:16]), t)
        t = n.dve(lambda e, src=src: e.match_replace(work[0:16], mx8[0:16], src[0:16], -1.0), t)
    t = n.dve(lambda e: e.tensor_scalar(eq[0:16], work[0:16], 0.0, None, ALU.is_lt), t)
    t = n.dve(lambda e: e.tensor_tensor_scan(slotT[0:16], ones5[0:16], eq[0:16], 0.0, ALU.mult, ALU.add), t, to)
    t = n.dve(lambda e: e.tensor_tensor(slotT[0:16], slotT[0:16], eq[0:16], ALU.mult), t)
    t_slot = n.dve(lambda e: e.tensor_scalar(slotT[0:16], slotT[0:16], -1.0, None, ALU.add), t)
    b, bank, bf = n.banks.take()
    for i in range(4):
        tok = n.transpose(bank[:, i * 16:(i + 1) * 16], slotT[0:16, i * P:(i + 1) * P], t_slot, bf)
    t = n.dve(lambda e: e.tensor_copy(small[:, 64:128], bank[:, 0:64]), tok)
    n.banks.put(b, t)
    for i in range(4):
        tG = n.dve(lambda e, i=i: e.tensor_tensor(G[:, i, :].rearrange("p (a s) -> p a s", a=16),
                                                iota.unsqueeze(1).to_broadcast([P, 16, 64]),
                                                slot[:, i, :].unsqueeze(2).to_broadcast([P, 16, 64]), ALU.is_equal), t, tl)
    txg = {}

    def dispatch(half, k):
        b, bank, bf = n.banks.take()
        tok = n.group(bank[:, :], [(hn_tok[:, i, k * P:(k + 1) * P], G[:, i, half * 512:(half + 1) * 512]) for i in range(4)],
                      tG, th, bf)
        dst = xg[:, k, half * 512:(half + 1) * 512]
        if k % 2:
            t = n.act(lambda e: e.activation(dst, bank[:, :], ACT.Copy), tok)
        else:
            t = n.dve(lambda e: e.tensor_copy(dst, bank[:, :]), tok)
        n.banks.put(b, t)
        txg[k, half] = t
        return tok

    for k in range(KT):
        dispatch(0, k)
    tgv = {}

    def spread(i):
        b, bank, bf = n.banks.take()
        tok = n.group(bank[:, :], [(sels[:, i * P:(i + 1) * P], slotT)], bf, t_slot)
        tgv[i] = n.dve(lambda e: e.scalar_tensor_tensor(out=gv[i], in0=bank[:, :], scalar=slotcol, in1=gv[i],
                                                        op0=ALU.is_equal, op1=ALU.mult), tok, tv[i])
        n.banks.put(b, tgv[i])

    def combine(m, pairs, norm=None):
        b, bank, bf = n.banks.take()
        tok = n.group(bank[:, :], [(ys[i][:, m * P:(m + 1) * P], gv[i], [ty[i], tgv[i]]) for i in pairs], bf)
        if norm:
            norm.flush()
        t = n.dve(lambda e: e.tensor_tensor(n.h[m], bank[:, :], n.h[m], ALU.add), tok)
        n.banks.put(b, t)
        if norm:
            norm.add(n.h[m], t)
        n.ht[m] = t

    def product(src, pair, lhs, waits):
        t0, t1 = n.banks.take(), n.banks.take()
        for j in range(4):
            w = [n.weights(expert_block(src, 2 * pair + a, j), 2048) for a in range(2)]
            for kk in range(2):
                k = 2 * j + kk
                for cc, (b, bank, bf) in enumerate((t0, t1)):
                    for a in range(2):
                        tok = n.pe(lambda e, bank=bank, a=a, cc=cc, k=k, kk=kk, w=w: e.matmul(
                            bank[a * 64:a * 64 + 64, :], lhs(k, a), w[a][0][:, kk * 1024 + cc * 512:kk * 1024 + cc * 512 + 512],
                            start=(k == 0), stop=(k == 7)), w[a][1], bf, waits(k, a), mark=(kk == 1 and cc == 1 and a == 1))
            for a in range(2):
                n.done(w[a][2], tok)
        return (t0[0], t0[1]), (t1[0], t1[1]), tok

    def down(i, hT, ti, tT2):
        y0, y1, tok = product(ins["exp_down"], i, lambda k, a: hT[:, k * P + a * 64:k * P + a * 64 + 64], lambda k, a: tT2)
        hidTs.put(ti, tok)
        ta = n.act(lambda e: e.activation(ys[i][:, 0:512], y0[1][:, :], ACT.Copy), tok, t_dispatched)
        tb = n.dve(lambda e: e.tensor_copy(ys[i][:, 512:1024], y1[1][:, :]), tok, t_dispatched)
        n.banks.put(y0[0], ta)
        n.banks.put(y1[0], tb)
        return [ta, tb]

    ty = []
    pend = None
    for i in range(8):
        lhs = lambda k, a, i=i: xg[:, k, (2 * i + a) * 64:(2 * i + a) * 64 + 64]
        w = lambda k, a, i=i: txg[k, i // 4]
        g0, g1, tg = product(ins["exp_gate"], i, lhs, w)
        if i == 0:
            for k in range(4):
                dispatch(1, k)
        hi, hid, hf = hids.take()
        ts = []
        for c, (b, bank) in enumerate((g0, g1)):
            t = n.act(lambda e, c=c, bank=bank, hid=hid: e.activation(hid[:, c * 512:(c + 1) * 512], bank[:, :], ACT.Silu), tg, hf)
            n.banks.put(b, t)
            ts.append(t)
        u0, u1, tu = product(ins["exp_up"], i, lhs, w)
        for c, (b, bank) in enumerate((u0, u1)):
            t = n.dve(lambda e, c=c, bank=bank, hid=hid: e.tensor_tensor(hid[:, c * 512:(c + 1) * 512],
                                                                       hid[:, c * 512:(c + 1) * 512], bank[:, :], ALU.mult), tu, ts[c])
            n.banks.put(b, t)
            ts[c] = t
        if i == 0:
            for k in range(4, 8):
                t_dispatched = dispatch(1, k)
        elif i < 5:
            spread(2 * i - 2)
            spread(2 * i - 1)
        elif i < 7:
            for m in range(4 * i - 20, 4 * i - 16):
                combine(m, range(4))
        else:
            for m in range(KT):
                combine(m, (4, 5))
        if pend is not None:
            ty.append(down(*pend))
        ti, hT, tf = hidTs.take()
        tt = []
        for c in range(2):
            b, bank, bf = n.banks.take()
            for j in range(4):
                tok = n.transpose(bank[:, j * P:(j + 1) * P], hid[:, c * 512 + j * P:c * 512 + (j + 1) * P], ts[c], bf, mark=(j == 3))
            if c:
                t = n.act(lambda e, c=c, bank=bank, hT=hT: e.activation(hT[:, c * 512:(c + 1) * 512], bank[:, :], ACT.Copy), tok, tf)
            else:
                t = n.dve(lambda e, c=c, bank=bank, hT=hT: e.tensor_copy(hT[:, c * 512:(c + 1) * 512], bank[:, :]), tok, tf)
            n.banks.put(b, t)
            tt.append(t)
        hids.put(hi, tok)
        pend = (i, hT, ti, tt)
    ty.append(down(*pend))
    nxt = Norm(n)
    for m in range(KT):
        combine(m, (6, 7), nxt)
    return nxt


def expert_block(w, e, j):
    return w[e, j * 256:(j + 1) * 256, :].rearrange("(k p) c -> p k c", p=P)


def weight_order(ins):
    order = []

    def add(blocks, floats, split=True):
        order.extend((b, floats, split) for b in blocks)

    def add_ffn(i):
        add([ins["w_gu"][i][m] for m in range(FF)], 2048)
        add([ins["w_dn"][i][m, :, z * 1408:(z + 1) * 1408] for m in range(KT) for z in range(2)], 1408)

    def add_ple(i):
        add([ins["w_ple"][i, m] for m in range(KT)], 1280)

    add_ffn(0)
    add([ins["w_ab_qk"][j] for j in range(10)], 2048)
    add([ins["w_ab_v"][j] for j in range(4)], 2048)
    add([ins["w_ab_out"][j] for j in range(4)], 2048)
    add_ffn(1)
    add_ple(0)
    add_ffn(2)
    add([ins["w_c_qk"][j] for j in range(8)], 2048)
    add([ins["w_c_v"][j] for j in range(4)], 2048)
    add([ins["w_c_out"][j] for j in range(4)], 2048)
    add_ffn(3)
    add_ple(1)
    fence = len(order)
    add([ins["w2_rwkv"][j] for j in range(7)], 2048)
    add([ins["w2_rwkv1"]], 1024)
    add([ins["lora"][0], ins["lora"][1]], 1024, False)
    add([ins["g2"]], 512, False)
    add([ins["pool_w"]], 512, False)
    add([ins["w2_pool"][j] for j in range(2)], 2048)
    add([ins["w2_att"][0], ins["w2_att"][1]], 2048)
    add([ins["w2_att1"], ins["w2_attv"]], 1024)
    add([ins["w2_gate"][m, z] for m in range(KT) for z in range(3)], 1536)
    add([ins["w2_out"][j] for j in range(4)], 2048)
    for i in range(9):
        for name, pair in (("exp_gate", i), ("exp_up", i), ("exp_down", i - 1)):
            if 0 <= pair < 8:
                add([expert_block(ins[name], 2 * pair + a, j) for j in range(4) for a in range(2)], 2048, False)
    return order, fence


def second_block(n):
    n.close(2)
    n.parts = None
    n.fence = len(n.order)
    n.open(2 * SLOT)
    n.add_slots(2)
    inner = n.open(2048)
    n.y_rwkv = n.buf(2048)
    yt = rwkv(n)
    n.open(8192, F32R)
    n.y_pool, n.y_att = ([n.pair() for _ in range(4)] for _ in range(2))
    open_xn(n)
    n.open_parts()
    tx = []
    for k in range(KT):
        g, (hi, lo) = n.vec("norm_mix_2", k), n.xn[k]
        th = n.act(lambda e: e.activation(hi, n.h[k], ACT.Copy, scale=g))
        tl = n.dve(lambda e: e.scalar_tensor_tensor(out=lo, in0=n.h[k], scalar=g, in1=hi.bitcast(F32), op0=ALU.mult,
                                                    op1=ALU.subtract), th)
        tx.append([th, tl])
    work = len(n.stack)
    n.open(6400)
    pt = pool_branch(n, tx)
    n.close(work)
    at = axial_attention(n, tx)
    n.close(work)
    norm = merge(n, tx, yt, pt, at)
    n.close(inner)
    n.parts = None
    n.open(TOTAL - P_FLOATS - KT * 512 - 2 * SLOT)
    n.xn_all = n.buf(KT * 512)
    n.xn = [n.xn_all[:, k * 512:(k + 1) * 512] for k in range(KT)]
    return experts(n, norm)


def program(nc, ins, out):
    with ExitStack() as ctx:
        n = make_net(nc, ctx, ins)
        first_block(n)
        norm = second_block(n)
        t = norm.finish("norm_final_2", n.xn)
        s = n.sem("s_out")
        for k in range(KT):
            n.sp(lambda e, k=k: e.dma_start(out[k], n.xn[k]).then_inc(s, 16), t[k], mark=False)
        n.sp.wait((s, 16 * KT))


def _cols(w, cols=None):
    if cols is not None:
        w = w[:, cols]
    k, m = w.shape
    return w.reshape(k // P, P, m // P, P).transpose(2, 1, 0, 3)


def _two(t):
    a, p, k, c = t.shape
    return np.ascontiguousarray(t.reshape(a // 2, 2, p, k, c).transpose(0, 2, 1, 3, 4)).reshape(a // 2, p, 2 * k * c)


def _wide(w):
    k, m = w.shape
    return np.ascontiguousarray(w.reshape(k // P, P, m).transpose(1, 0, 2)).reshape(P, -1)


def _head_cols(tiles):
    return np.concatenate([np.arange(h * 64, h * 64 + 64) for pair in tiles for h in pair])


def _constants():
    c = np.zeros((5, P, P), np.float32)
    c[0] = np.eye(P)
    c[1] = 1.0
    for a in range(2):
        c[2, a * 64:a * 64 + 64, a * 64:a * 64 + 64] = 1.0
        for i in range(32):
            c[3, a * 64 + i + 32, a * 64 + i] = -1.0
            c[3, a * 64 + i, a * 64 + i + 32] = 1.0
            c[4, a * 64 + 2 * i + 1, a * 64 + 2 * i] = -1.0
            c[4, a * 64 + 2 * i, a * 64 + 2 * i + 1] = 1.0
    f32 = np.float32
    inv = (10000.0 ** (-(np.arange(32) / 32))).astype(f32)
    ang = (np.arange(S, dtype=f32)[:, None] * inv[None, :]).astype(f32).astype(np.float64)
    rope1 = np.stack([np.tile(np.cos(ang).T, (4, 1)), np.tile(np.sin(ang).T, (4, 1))]).astype(f32)
    fr = (10000.0 ** (-(np.arange(0, 32, 2) / 32))).astype(f32)
    row = np.repeat(np.arange(8, dtype=f32), 64)
    col = np.tile(np.arange(64, dtype=f32), 8)
    ang = np.concatenate([row[:, None] * fr, col[:, None] * fr], axis=-1).astype(np.float64)
    rope2 = np.stack([np.tile(np.repeat(np.cos(ang).T, 2, axis=0), (2, 1)),
                      np.tile(np.repeat(np.sin(ang).T, 2, axis=0), (2, 1))]).astype(f32)
    i = np.arange(P)[:, None]
    j = np.arange(384)[None, :] - P
    mask_a = np.where(np.abs(i - j) <= 128, 0, NEG).astype(f32)
    mb1 = np.zeros((P, 4, S), f32)
    for r in range(4):
        mb1[:, r] = np.where(np.abs(4 * np.arange(P)[:, None] + r - np.arange(S)[None, :]) <= 64, 0, NEG)
    d = np.arange(P)[:, None] - np.arange(P)[None, :]
    mb23 = np.concatenate([np.where(np.abs(d) <= 64, 0, NEG), np.where(d % 4 == 0, 0, NEG)], 1).astype(f32)
    cq = np.arange(P) % 64
    cs = np.clip(cq - 8, 0, 48)[:, None]
    kc = np.arange(64)[None, :]
    win = np.where((kc >= cs) & (kc < cs + 16), 0, NEG).astype(f32)
    mask_c = np.tile(win, (1, 16))
    reset = np.ones((P, S), f32)
    reset[:, ::64] = 0
    t = np.arange(S)
    icnt = np.zeros((P, 4, S), f32)
    for g, w in enumerate((2, 4, 8, 16)):
        lo, hi = w // 2, w - w // 2 - 1
        icnt[:, g] = 1.0 / (np.clip(t + hi + 1, 0, S) - np.clip(t - lo, 0, S))
    a, b = np.arange(P)[:, None], np.arange(P)[None, :]
    mask_r = np.zeros((2, P, 448), f32)
    for d in range(2):
        head = a // 64 == b // 64
        strict = (a % 64 < b % 64) if d == 0 else (a % 64 > b % 64)
        block = (a % 64) // 16 == (b % 64) // 16
        mask_r[d, :, 0:128] = head & strict & block
        mask_r[d, :, 128:256] = head & strict & ~block
        mask_r[d, :, 256:384] = head & strict
        tt = np.arange(64)[None, :]
        mask_r[d, :, 384:448] = (a % 64 <= tt) if d == 0 else (a % 64 >= tt)
    sels = np.zeros((P, 8, P), f32)
    for e in range(16):
        sels[e, e // 2, (e % 2) * 64:(e % 2) * 64 + 64] = 1
    more = dict(reset=reset, icnt=icnt.reshape(P, -1), mask_r=mask_r, sels=sels.reshape(P, -1),
                iota=np.tile(np.arange(64, dtype=f32), (P, 1)), slotcol=(np.arange(P) % 64).astype(f32).reshape(P, 1))
    return dict(more, consts=c, rope1=rope1, rope2=rope2, mask_a=mask_a, mask_b1=mb1.reshape(P, -1), mask_b23=mb23,
                mask_c=mask_c)


def _layout(x):
    f = {k: np.asarray(v) for k, v in x.items()}
    a = dict(_constants())
    a["x"] = np.ascontiguousarray(f["x"][0].T).reshape(KT, P, S)
    a["p"] = np.ascontiguousarray(f["p"][:, 0].transpose(0, 2, 1)).reshape(2, 2, P, S)
    v = lambda z: z.reshape(-1, P).T
    dup = lambda z: np.concatenate([z, z]).reshape(P, 1)
    parts = [v(f["norm_ffn1"][0]), v(f["norm_ffn1"][1]), v(f["norm_mix"][0]), v(f["norm_mix"][1]),
             v(f["norm_ffn2"][0]), v(f["norm_ffn2"][1]), v(f["norm_ple"][0]), v(f["norm_ple"][1]),
             v(f["norm_final"]), v(f["norm_mix_2"][0]), v(f["norm_ffn_2"][0]), v(f["norm_final_2"]),
             v(f["shift_prev_2"][0]), v(f["shift_next_2"][0]), v(f["rwkv_w0_2"][0, 0]), v(f["rwkv_w0_2"][0, 1]),
             v(f["rwkv_a0_2"][0, 0]), v(f["rwkv_a0_2"][0, 1]), v(f["rwkv_k_k_2"][0]), v(f["rwkv_k_a_2"][0]),
             v(f["rwkv_r_k_2"][0]), v(f["rwkv_ln_w_2"][0]), v(f["rwkv_ln_b_2"][0]), v(f["pool_scale_2"][0]),
             dup(f["q_norm_2"][0]), dup(f["k_norm_2"][0])]
    a["vecs"] = np.ascontiguousarray(np.concatenate(parts, axis=1))
    a["sink_a"] = f["sink_a"].reshape(1, 12)
    gu, dn = [], []
    for layer in range(2):
        for s in ("ffn1", "ffn2"):
            g = _cols(f[f"{s}_w_gate"][layer])
            u = _cols(f[f"{s}_w_up"][layer])
            gu.append(np.stack([g, u], axis=2).reshape(FF, P, 2048))
            dn.append(_cols(f[f"{s}_w_down"][layer]).reshape(KT, P, FF * P))
    a["w_gu"] = np.stack(gu)
    a["w_dn"] = np.stack(dn)
    w = f["w_in_ab"][0]
    ha = _head_cols(A_TILES)
    qk = np.concatenate([ha, np.arange(768, 1024), np.arange(1280, 1280 + 1536)])
    a["w_ab_qk"] = _two(_cols(w, qk))
    a["w_ab_v"] = np.stack([_wide(w[:, 1024:1280])] + [_wide(w[:, 2816 + 256 * g:2816 + 256 * (g + 1)]) for g in range(3)])
    rows = np.concatenate([ha, np.arange(768, 1024)])
    a["w_ab_out"] = _two(_cols(f["w_out_ab"][0][rows]))
    w = f["w_in_c"][0]
    a["w_c_qk"] = _two(_cols(w[:, 0:2048]))
    a["w_c_v"] = np.stack([_wide(w[:, 2048 + 256 * g:2048 + 256 * (g + 1)]) for g in range(4)])
    a["w_c_out"] = _two(_cols(f["w_out_c"][0]))
    rpb = f["rpb_c"][0]
    t = np.zeros((16, P, 16, 64), rpb.dtype)
    for p in range(P):
        half, c = p // 64, p % 64
        lo, hi = max(0, c - 15), min(64, c + 16)
        t[:, p, half:half + 15, lo:hi] = rpb[:, :, lo - c + 15:hi - c + 15]
    a["rpb"] = t.reshape(16, P, 1024)
    a["w_ple"] = np.stack([np.concatenate([_cols(f["w_ple_gate"][i]), _cols(f["w_ple_proj"][i])], axis=2)
                           .reshape(KT, P, 1280) for i in range(2)])
    w = f["w_in_2"][0]
    a["w2_rwkv"] = _two(_cols(w[:, 0:1792]))
    a["w2_rwkv1"] = _cols(w[:, 1792:1920]).reshape(P, 1024)
    a["w2_pool"] = _two(_cols(w[:, 1920:2432]))
    hq = _head_cols(ATT_TILES)
    a["w2_att"] = _two(_cols(w[:, 2432:2944], hq))
    a["w2_att1"] = _cols(w[:, 2944:3072]).reshape(P, 1024)
    a["w2_attv"] = _wide(w[:, 3072:3200])
    gates = _cols(w[:, 3200:6272]).reshape(3, KT, P, KT, P)
    br = np.stack([_cols(f["w_branch_rwkv_2"][0]), _cols(f["w_branch_pool_2"][0]),
                   _cols(f["w_branch_attn_2"][0][hq])])
    a["w2_gate"] = np.concatenate([gates, br], axis=3).transpose(1, 0, 2, 3, 4).reshape(KT, 3, P, 1536)
    a["w2_out"] = _two(_cols(f["w_out_2"][0]))
    lora = np.zeros((2, P, 2, 512), f["rwkv_w2_2"].dtype)
    for z, name in enumerate(("rwkv_w2_2", "rwkv_a2_2")):
        for d in range(2):
            lora[d, d * 64:d * 64 + 64, z] = f[name][0, d]
    a["lora"] = lora.reshape(2, P, 1024)
    a["g2"] = f["rwkv_g2_2"][0]
    a["pool_w"] = np.ascontiguousarray(f["pool_w_2"][0].transpose(1, 0, 2)).reshape(P, 512)
    a["router"] = _wide(f["router_2"][0])
    for name in ("exp_gate", "exp_up", "exp_down"):
        a[name] = f[f"{name}_2"][0]
    return a


def kernel(**inputs):
    import concourse.bacc as _bacc
    from concourse import mybir as _mybir
    from concourse.bass_utils import run_bass_kernel_spmd as _run

    nc = _bacc.Bacc("TRN2", target_bir_lowering=False, num_devices=1)
    feed, ins = {}, {}
    for name, x in _layout(inputs).items():
        x = np.ascontiguousarray(x)
        feed[f"in_{name}"] = x
        ins[name] = nc.dram_tensor(f"in_{name}", x.shape, _mybir.dt.from_np(x.dtype), kind="ExternalInput").ap()
    out = nc.dram_tensor("out_0", (KT, P, S), _mybir.dt.float32, kind="ExternalOutput").ap()
    program(nc, ins, out)
    r = _run(nc, [feed], core_ids=[0])
    return np.ascontiguousarray(r.results[0]["out_0"].reshape(D, S).T).reshape(1, S, D)
```
